# Optimizing a Trainium2 kernel written in Bass

```python
import jax, jax.numpy as jnp
from jax import lax
import numpy as np
import math
import jax
import jax.numpy as jnp

D_MODEL = 1024
BATCH = 1
SEQ = 256
DEPTH = 2

GRID_W = 64
CTX_LEN = 256
HEAD_DIM = 64
ATTN_HEADS = 8
KV_HEADS = 2
Q_PER_KV = ATTN_HEADS // KV_HEADS
ATTN_WIDTH = ATTN_HEADS * HEAD_DIM
KV_WIDTH = KV_HEADS * HEAD_DIM
WINDOW = 128
BLOCK = 128
FOURIER_GROUPS = 4
FOURIER_GROUP_DIM = 64
FOURIER_WIDTH = FOURIER_GROUPS * FOURIER_GROUP_DIM
CONV_GROUPS = 4
CONV_WIDTH = 256
CONV_TAPS = 3
MIX_WIDTH = ATTN_WIDTH + FOURIER_WIDTH + CONV_WIDTH
PROJ_SIZES = (ATTN_WIDTH, KV_WIDTH, KV_WIDTH, ATTN_WIDTH,
              FOURIER_WIDTH, FOURIER_WIDTH,
              CONV_WIDTH, CONV_WIDTH, CONV_WIDTH, CONV_WIDTH)
PROJ_WIDTH = 2 * ATTN_WIDTH + 2 * KV_WIDTH + 2 * FOURIER_WIDTH + 4 * CONV_WIDTH
ROPE_FREQS = HEAD_DIM // 4
ROPE_BASE = 10000.0
NORM_EPS = 1e-6


def rmsnorm(x, g):
    xf = x.astype(jnp.float32)
    y = xf * lax.rsqrt(jnp.mean(xf * xf, axis=-1, keepdims=True) + NORM_EPS)
    return (y * g.astype(jnp.float32)).astype(x.dtype)

def split_cols(p, sizes):
    out = []
    start = 0
    for s in sizes:
        out.append(p[..., start:start + s])
        start += s
    return out

def axial_rope_tables(n):
    rows = n // GRID_W
    row = jnp.repeat(jnp.arange(rows, dtype=jnp.float32), GRID_W)
    col = jnp.tile(jnp.arange(GRID_W, dtype=jnp.float32), rows)
    inv_freq = jnp.power(ROPE_BASE, -jnp.arange(ROPE_FREQS, dtype=jnp.float32) / ROPE_FREQS)
    ang = jnp.concatenate([row[:, None] * inv_freq, col[:, None] * inv_freq], axis=-1)
    return jnp.cos(ang), jnp.sin(ang)

def apply_axial_rope(x, cos, sin):
    b, n, h, d = x.shape
    xr = x.astype(jnp.float32).reshape(b, n, h, 2, 2, ROPE_FREQS)
    x1 = xr[..., 0, :]
    x2 = xr[..., 1, :]
    cs = cos.reshape(n, 1, 2, ROPE_FREQS)
    sn = sin.reshape(n, 1, 2, ROPE_FREQS)
    out = jnp.stack([x1 * cs - x2 * sn, x1 * sn + x2 * cs], axis=-2)
    return out.reshape(b, n, h, d).astype(x.dtype)

def sink_softmax(s, sink_b):
    m = jnp.maximum(jnp.max(s, axis=-1, keepdims=True), sink_b)
    e = jnp.exp(s - m)
    return e / (jnp.sum(e, axis=-1, keepdims=True) + jnp.exp(sink_b - m))

def window_attention(q, k, v, kc, vc, sink_b):
    b, n = q.shape[:2]
    nb = n // BLOCK
    span = BLOCK + 2 * WINDOW
    nc = kc.shape[1]
    qb = (q * (HEAD_DIM ** -0.5)).reshape(b, nb, BLOCK, KV_HEADS, Q_PER_KV, HEAD_DIM).transpose(1, 0, 2, 3, 4, 5)
    pad = ((0, 0), (WINDOW, WINDOW), (0, 0), (0, 0))
    kp = jnp.pad(k, pad)
    vp = jnp.pad(v, pad)
    offs_q = jnp.arange(BLOCK)
    offs_k = jnp.arange(span) - WINDOW

    def one_block(args):
        qi, i = args
        start = i * BLOCK
        ks = lax.dynamic_slice_in_dim(kp, start, span, axis=1)
        vs = lax.dynamic_slice_in_dim(vp, start, span, axis=1)
        qpos = start + offs_q
        kpos = start + offs_k
        valid = (jnp.abs(qpos[:, None] - kpos[None, :]) <= WINDOW) & (kpos >= 0)[None, :] & (kpos < n)[None, :]
        s_loc = jnp.einsum('bqkgd,bnkd->bkgqn', qi, ks).astype(jnp.float32)
        s_loc = jnp.where(valid, s_loc, -jnp.inf)
        s_ctx = jnp.einsum('bqkgd,bnkd->bkgqn', qi, kc).astype(jnp.float32)
        p = sink_softmax(jnp.concatenate([s_ctx, s_loc], axis=-1), sink_b).astype(v.dtype)
        return (jnp.einsum('bkgqn,bnkd->bqkgd', p[..., :nc], vc)
                + jnp.einsum('bkgqn,bnkd->bqkgd', p[..., nc:], vs))

    o = lax.map(one_block, (qb, jnp.arange(nb)))
    return o.transpose(1, 0, 2, 3, 4, 5).reshape(b, n, ATTN_WIDTH)

def context_attention(q, k, v, sink_b):
    b, n = q.shape[:2]
    qg = (q * (HEAD_DIM ** -0.5)).reshape(b, n, KV_HEADS, Q_PER_KV, HEAD_DIM)
    s = jnp.einsum('bqkgd,bnkd->bkgqn', qg, k).astype(jnp.float32)
    p = sink_softmax(s, sink_b).astype(v.dtype)
    return jnp.einsum('bkgqn,bnkd->bqkgd', p, v).reshape(b, n, ATTN_WIDTH)

def fourier_mix(u, w_f):
    b, n, _ = u.shape
    ug = u.reshape(b, n, FOURIER_GROUPS, FOURIER_GROUP_DIM).astype(jnp.float32)
    f = jnp.fft.fft2(ug, axes=(1, 3), norm='ortho').real.astype(u.dtype)
    return jnp.einsum('bngc,gcd->bngd', f, w_f).reshape(b, n, FOURIER_WIDTH)

def short_conv_mix(z, b_gate, c_gate, w, bias):
    t = c_gate * z
    tp = jnp.pad(t, ((0, 0), (1, 1), (0, 0)))
    y = tp[:, :-2] * w[0] + tp[:, 1:-1] * w[1] + tp[:, 2:] * w[2] + bias
    return b_gate * y

def gated_merge(a, ga, f, gf, s, gc, w_out):
    h = jnp.concatenate([a * jax.nn.silu(ga), f * jax.nn.silu(gf), s * jax.nn.silu(gc)], axis=-1)
    return h @ w_out

def layer(x, ctx, c, c_ctx, w_mod, b_mod, g_pre, g_post, w_in, w_out, sink, w_fourier, conv_w, conv_b,
          cos, sin, update_ctx):
    b, n = x.shape[:2]
    nc = ctx.shape[1]
    shift, scale, gate = jnp.split(jax.nn.silu(c) @ w_mod + b_mod, 3, axis=-1)
    shift_c, scale_c, gate_c = jnp.split(jax.nn.silu(c_ctx) @ w_mod + b_mod, 3, axis=-1)
    sink_b = sink.astype(jnp.float32).reshape(1, KV_HEADS, Q_PER_KV, 1, 1)

    hx = rmsnorm(x, g_pre) * (1 + scale[:, None]) + shift[:, None]
    hc = rmsnorm(ctx, g_pre) * (1 + scale_c) + shift_c

    if update_ctx:
        qc, kc, vc, gac, ufc, gfc, zcc, bcc, ccc, gcc = split_cols(hc @ w_in, PROJ_SIZES)
    else:
        kc, vc = split_cols(hc @ w_in[:, ATTN_WIDTH:ATTN_WIDTH + 2 * KV_WIDTH], (KV_WIDTH, KV_WIDTH))
    kc = kc.reshape(b, nc, KV_HEADS, HEAD_DIM)
    vc = vc.reshape(b, nc, KV_HEADS, HEAD_DIM)

    q, k, v, ga, uf, gf, zc, bc, cc, gc = split_cols(hx @ w_in, PROJ_SIZES)
    q = apply_axial_rope(q.reshape(b, n, ATTN_HEADS, HEAD_DIM), cos, sin)
    k = apply_axial_rope(k.reshape(b, n, KV_HEADS, HEAD_DIM), cos, sin)
    v = v.reshape(b, n, KV_HEADS, HEAD_DIM)
    a = window_attention(q, k, v, kc, vc, sink_b)
    f = fourier_mix(uf, w_fourier)
    s = short_conv_mix(zc, bc, cc, conv_w, conv_b)
    y = gated_merge(a, ga, f, gf, s, gc, w_out)
    x_new = x + gate[:, None] * rmsnorm(y, g_post)

    if update_ctx:
        ac = context_attention(qc.reshape(b, nc, ATTN_HEADS, HEAD_DIM), kc, vc, sink_b)
        fc = fourier_mix(ufc, w_fourier)
        sc = short_conv_mix(zcc, bcc, ccc, conv_w, conv_b)
        yc = gated_merge(ac, gac, fc, gfc, sc, gcc, w_out)
        ctx = ctx + gate_c * rmsnorm(yc, g_post)
    return x_new, ctx

def first_inputs(seed: int = 0) -> dict:
    key = jax.random.key(seed)
    ks = jax.random.split(key, 14)
    nrm = jax.random.normal
    x = nrm(ks[0], (BATCH, SEQ, D_MODEL), jnp.float32)
    c = nrm(ks[1], (BATCH, D_MODEL), jnp.float32)
    ctx = nrm(ks[2], (BATCH, CTX_LEN, D_MODEL), jnp.float32)
    c_ctx = nrm(ks[3], (D_MODEL,), jnp.float32)
    w_mod = nrm(ks[4], (DEPTH, D_MODEL, 3 * D_MODEL), jnp.float32) * (0.5 * D_MODEL ** -0.5)
    b_mod = 0.01 * nrm(ks[5], (DEPTH, 3 * D_MODEL), jnp.float32)
    g_pre = 1.0 + 0.05 * nrm(ks[6], (DEPTH, D_MODEL), jnp.float32)
    g_post = 1.0 + 0.05 * nrm(ks[7], (DEPTH, D_MODEL), jnp.float32)
    w_in = nrm(ks[8], (DEPTH, D_MODEL, PROJ_WIDTH), jnp.float32) * (D_MODEL ** -0.5)
    w_out = nrm(ks[9], (DEPTH, MIX_WIDTH, D_MODEL), jnp.float32) * (MIX_WIDTH ** -0.5)
    sink = 0.5 * nrm(ks[10], (DEPTH, ATTN_HEADS), jnp.float32)
    w_fourier = nrm(ks[11], (DEPTH, FOURIER_GROUPS, FOURIER_GROUP_DIM, FOURIER_GROUP_DIM), jnp.float32) * (FOURIER_GROUP_DIM ** -0.5)
    conv_w = nrm(ks[12], (DEPTH, CONV_TAPS, CONV_WIDTH), jnp.float32) * (CONV_TAPS ** -0.5)
    conv_b = 0.01 * nrm(ks[13], (DEPTH, CONV_WIDTH), jnp.float32)
    return {'x': x, 'c': c, 'ctx': ctx, 'c_ctx': c_ctx, 'w_mod': w_mod, 'b_mod': b_mod,
            'g_pre': g_pre, 'g_post': g_post, 'w_in': w_in, 'w_out': w_out, 'sink': sink,
            'w_fourier': w_fourier, 'conv_w': conv_w, 'conv_b': conv_b}

def first_block(x, c, ctx, c_ctx, w_mod, b_mod, g_pre, g_post, w_in, w_out, sink, w_fourier, conv_w, conv_b):
    cos, sin = axial_rope_tables(x.shape[1])
    for l in range(DEPTH):
        x, ctx = layer(x, ctx, c, c_ctx, w_mod[l], b_mod[l], g_pre[l], g_post[l], w_in[l], w_out[l],
                       sink[l], w_fourier[l], conv_w[l], conv_b[l], cos, sin, l < DEPTH - 1)
    return x


N_EVEN = (DEPTH + 1) // 2
N_ODD = DEPTH // 2
N_MOD = 9
D_FF = 2816
EPS = 1e-6

DA_HEADS = 4
DA_HD = 64
DA_VD = 2 * DA_HD
ML_HEADS = 4
ML_QK = 64
ML_V = 128
ML_CONV = 3
GLA_HEADS = 4
GLA_K = 128
GLA_V = 256
GLA_RANK = 16
GLA_TAU = 16.0

CHUNK = 64
Q_BLOCK = 128
ROPE_AXIS = DA_HD // 2

EVEN_SPLITS = (DA_HEADS * 2 * DA_HD, DA_HEADS * 2 * DA_HD, DA_HEADS * DA_VD,
               2 * ML_HEADS * ML_QK, ML_HEADS * ML_V, ML_HEADS * ML_V, 4 * ML_HEADS)
EVEN_IN = sum(EVEN_SPLITS)
ODD_SPLITS = (GLA_HEADS * GLA_K, GLA_HEADS * GLA_K, GLA_HEADS * GLA_V, GLA_HEADS * GLA_V, 2 * GLA_RANK)
ODD_IN = sum(ODD_SPLITS)


def _split(p, sizes):
    idx = np.cumsum(sizes)[:-1].tolist()
    return jnp.split(p, idx, axis=-1)

def rms_norm(x, g):
    xf = x.astype(jnp.float32)
    y = xf * lax.rsqrt(jnp.mean(xf * xf, axis=-1, keepdims=True) + EPS)
    return y.astype(x.dtype) * g

def ada_norm(x, g, shift, scale):
    return rms_norm(x, g) * (1.0 + scale) + shift

def swiglu(h, w_in, w_out):
    a, b = jnp.split(h @ w_in, 2, axis=-1)
    return (jax.nn.silu(a) * b) @ w_out

def axial_rope_tables_2(rows, dtype):
    row = jnp.repeat(jnp.arange(rows), GRID_W).astype(jnp.float32)
    col = (jnp.arange(rows * GRID_W) % GRID_W).astype(jnp.float32)
    inv = ROPE_BASE ** (-jnp.arange(ROPE_AXIS // 2, dtype=jnp.float32) * 2.0 / ROPE_AXIS)
    ar = row[:, None] * inv
    ac = col[:, None] * inv
    return (jnp.cos(ar).astype(dtype), jnp.sin(ar).astype(dtype),
            jnp.cos(ac).astype(dtype), jnp.sin(ac).astype(dtype))

def _rope_1d(x, cos, sin):
    cos = cos[None, :, None, None, :]
    sin = sin[None, :, None, None, :]
    x1, x2 = jnp.split(x, 2, axis=-1)
    return jnp.concatenate([x1 * cos - x2 * sin, x2 * cos + x1 * sin], axis=-1)

def rope_2d(x, rope):
    cr, sr, cc, sc = rope
    xr, xc = jnp.split(x, 2, axis=-1)
    return jnp.concatenate([_rope_1d(xr, cr, sr), _rope_1d(xc, cc, sc)], axis=-1)

def diff_softmax_core(q, k, v, lam):
    s = jnp.einsum('bqhcd,bkhcd->bhcqk', q.astype(jnp.float32), k.astype(jnp.float32)) * (DA_HD ** -0.5)
    p = jax.nn.softmax(s, axis=-1)
    w = p[:, :, 0] - lam * p[:, :, 1]
    return jnp.einsum('bhqk,bkhe->bqhe', w, v.astype(jnp.float32))

def diff_attn_latent(q, k, v, lam):
    b, t, h, _, d = q.shape
    nb = t // Q_BLOCK
    qb = jnp.moveaxis(q.reshape(b, nb, Q_BLOCK, h, 2, d), 1, 0)
    out = lax.map(lambda qq: diff_softmax_core(qq, k, v, lam), qb)
    return jnp.moveaxis(out, 0, 1).reshape(b, t, h, -1)

def dw_conv(x, w, bias):
    ch = x.shape[-1]
    pad = ML_CONV // 2
    y = lax.conv_general_dilated(x, w[:, None, :].astype(x.dtype), window_strides=(1,),
                                 padding=((pad, pad),), dimension_numbers=('NWC', 'WIO', 'NWC'),
                                 feature_group_count=ch)
    return y + bias

def to_chunks(a):
    b, s, h = a.shape[:3]
    rest = a.shape[3:]
    a = a.reshape((b, s // CHUNK, CHUNK, h) + rest)
    return a.transpose((1, 0, 3, 2) + tuple(range(4, a.ndim)))

def from_chunks(y):
    nc, b, h, l = y.shape[:4]
    rest = y.shape[4:]
    y = y.transpose((1, 0, 3, 2) + tuple(range(4, y.ndim)))
    return y.reshape((b, nc * l, h) + rest)

def mlstm_scan(q, k, v, ig, lf, state):
    xs = tuple(to_chunks(a.astype(jnp.float32)) for a in (q, k, v, ig, lf))
    tril = jnp.tril(jnp.ones((CHUNK, CHUNK), dtype=bool))

    def step(carry, inp):
        cmat, nvec, m = carry
        qc, kc, vc, ic, fc = inp
        bcum = jnp.cumsum(fc, axis=-1)
        dmat = jnp.where(tril, bcum[..., :, None] - bcum[..., None, :] + ic[..., None, :], -jnp.inf)
        m_inter = bcum + m[..., None]
        m_t = jnp.maximum(m_inter, jnp.max(dmat, axis=-1))
        w_inter = jnp.exp(m_inter - m_t)
        s = jnp.einsum('bhtd,bhsd->bhts', qc, kc) * jnp.exp(dmat - m_t[..., None])
        num = jnp.einsum('bhts,bhse->bhte', s, vc) + w_inter[..., None] * jnp.einsum('bhtd,bhed->bhte', qc, cmat)
        den = jnp.sum(s, axis=-1) + w_inter * jnp.einsum('bhtd,bhd->bht', qc, nvec)
        h = num / jnp.maximum(jnp.abs(den), jnp.exp(-m_t))[..., None]
        bl = bcum[..., -1]
        g = bl[..., None] - bcum + ic
        m_new = jnp.maximum(bl + m, jnp.max(g, axis=-1))
        decay = jnp.exp(bl + m - m_new)
        wk = jnp.exp(g - m_new[..., None])
        cmat = decay[..., None, None] * cmat + jnp.einsum('bhs,bhse,bhsd->bhed', wk, vc, kc)
        nvec = decay[..., None] * nvec + jnp.einsum('bhs,bhsd->bhd', wk, kc)
        return (cmat, nvec, m_new), h

    state, hs = lax.scan(step, state, xs)
    return from_chunks(hs), state

def gla_scan(q, k, v, la, state):
    xs = tuple(to_chunks(a.astype(jnp.float32)) for a in (q, k, v, la))
    tril = jnp.tril(jnp.ones((CHUNK, CHUNK), dtype=bool))

    def step(smat, inp):
        qc, kc, vc, ac = inp
        bcum = jnp.cumsum(ac, axis=2)
        qe = qc * jnp.exp(bcum)
        ke = kc * jnp.exp(-bcum)
        a = jnp.where(tril, jnp.einsum('bhtd,bhsd->bhts', qe, ke), 0.0)
        o = jnp.einsum('bhts,bhse->bhte', a, vc) + jnp.einsum('bhtd,bhde->bhte', qe, smat)
        bl = bcum[:, :, -1]
        kd = kc * jnp.exp(bl[:, :, None] - bcum)
        smat = jnp.exp(bl)[..., None] * smat + jnp.einsum('bhsd,bhse->bhde', kd, vc)
        return smat, o

    state, os_ = lax.scan(step, state, xs)
    return from_chunks(os_), state

def bidir_scan(scan, qkv_c, qkv_x, gc_f, gc_b, gx_f, gx_b, st0, need_ctx):
    def rev(arrs):
        return tuple(jnp.flip(a, axis=1) for a in arrs)
    yc_f, s_f = scan(*qkv_c, *gc_f, st0)
    yc_b, s_b = scan(*rev(qkv_c), *rev(gc_b), st0)
    yx_f, _ = scan(*qkv_x, *gx_f, s_f)
    yx_b, _ = scan(*rev(qkv_x), *rev(gx_b), s_b)
    yx = yx_f + jnp.flip(yx_b, axis=1)
    yc = yc_f + jnp.flip(yc_b, axis=1) if need_ctx else None
    return yx, yc

def even_mixer(hx, hc, w_in, w_out, diff_lambda, diff_norm_g, conv_w, conv_b, gate_b, ml_norm_g,
               lam_init, rope, need_ctx):
    dt = hx.dtype
    px = _split(hx @ w_in, EVEN_SPLITS)
    pc = _split(hc @ w_in, EVEN_SPLITS)
    lp = diff_lambda.astype(jnp.float32)
    lam = jnp.exp(jnp.sum(lp[0] * lp[1])) - jnp.exp(jnp.sum(lp[2] * lp[3])) + lam_init

    def da_heads(p):
        b, t = p[0].shape[:2]
        return (p[0].reshape(b, t, DA_HEADS, 2, DA_HD), p[1].reshape(b, t, DA_HEADS, 2, DA_HD),
                p[2].reshape(b, t, DA_HEADS, DA_VD))

    def ml_heads(p):
        b, t = p[0].shape[:2]
        qk = jax.nn.silu(dw_conv(p[3], conv_w, conv_b))
        q, k = jnp.split(qk, 2, axis=-1)
        q = q.reshape(b, t, ML_HEADS, ML_QK) * (ML_QK ** -0.5)
        k = k.reshape(b, t, ML_HEADS, ML_QK)
        v = p[4].reshape(b, t, ML_HEADS, ML_V)
        g = (p[6] + gate_b.reshape(-1)).astype(jnp.float32).reshape(b, t, 4, ML_HEADS)
        fwd = (g[:, :, 0], jax.nn.log_sigmoid(g[:, :, 2]))
        bwd = (g[:, :, 1], jax.nn.log_sigmoid(g[:, :, 3]))
        return (q, k, v), fwd, bwd

    def merge(attn, mem, o_pre):
        b, t = attn.shape[:2]
        a = (rms_norm(attn, diff_norm_g) * (1.0 - lam_init)).reshape(b, t, -1)
        m = rms_norm(mem, ml_norm_g).reshape(b, t, -1) * jax.nn.sigmoid(o_pre)
        return jnp.concatenate([a, m], axis=-1).astype(dt) @ w_out

    qx, kx, vx = da_heads(px)
    qc, kc, vc = da_heads(pc)
    qx = rope_2d(qx, rope)
    kx = rope_2d(kx, rope)
    ax = diff_attn_latent(qx, jnp.concatenate([kc, kx], axis=1), jnp.concatenate([vc, vx], axis=1), lam)

    qkv_x, gx_f, gx_b = ml_heads(px)
    qkv_c, gc_f, gc_b = ml_heads(pc)
    bsz = hx.shape[0]
    st0 = (jnp.zeros((bsz, ML_HEADS, ML_V, ML_QK), jnp.float32),
           jnp.zeros((bsz, ML_HEADS, ML_QK), jnp.float32),
           jnp.zeros((bsz, ML_HEADS), jnp.float32))
    mx, mc = bidir_scan(mlstm_scan, qkv_c, qkv_x, gc_f, gc_b, gx_f, gx_b, st0, need_ctx)

    out_x = merge(ax, mx, px[5])
    out_c = merge(diff_softmax_core(qc, kc, vc, lam), mc, pc[5]) if need_ctx else None
    return out_x, out_c

def odd_mixer(hx, hc, w_in, w_out, w_gate, b_gate, norm_g, need_ctx):
    dt = hx.dtype
    px = _split(hx @ w_in, ODD_SPLITS)
    pc = _split(hc @ w_in, ODD_SPLITS)

    def heads(p):
        b, t = p[0].shape[:2]
        q = p[0].reshape(b, t, GLA_HEADS, GLA_K) * (GLA_K ** -0.5)
        k = p[1].reshape(b, t, GLA_HEADS, GLA_K)
        v = p[2].reshape(b, t, GLA_HEADS, GLA_V)
        lr_f, lr_b = jnp.split(p[4], 2, axis=-1)

        def decay(lr, d):
            z = (lr @ w_gate[d] + b_gate[d]).astype(jnp.float32)
            return (jax.nn.log_sigmoid(z) / GLA_TAU).reshape(b, t, GLA_HEADS, GLA_K)
        return (q, k, v), (decay(lr_f, 0),), (decay(lr_b, 1),)

    def merge(o, r):
        b, t = o.shape[:2]
        y = rms_norm(o, norm_g).reshape(b, t, -1) * jax.nn.silu(r)
        return y.astype(dt) @ w_out

    qkv_x, gx_f, gx_b = heads(px)
    qkv_c, gc_f, gc_b = heads(pc)
    st0 = jnp.zeros((hx.shape[0], GLA_HEADS, GLA_K, GLA_V), jnp.float32)
    ox, oc = bidir_scan(gla_scan, qkv_c, qkv_x, gc_f, gc_b, gx_f, gx_b, st0, need_ctx)
    out_x = merge(ox, px[3])
    out_c = merge(oc, pc[3]) if need_ctx else None
    return out_x, out_c

def second_inputs(seed: int = 0) -> dict:
    key = jax.random.key(seed)
    ks = iter(jax.random.split(key, 32))

    def nrm(shape, scale):
        return jax.random.normal(next(ks), shape, jnp.float32) * scale

    d = D_MODEL
    inv = d ** -0.5
    x = nrm((BATCH, SEQ, d), 1.0)
    c = nrm((BATCH, d), 1.0)
    ctx = nrm((BATCH, CTX_LEN, d), 1.0)
    c_ctx = nrm((d,), 1.0)
    ada_w = nrm((DEPTH, d, N_MOD * d), 0.3 * inv)
    ada_b = nrm((DEPTH, N_MOD * d), 0.02)
    norm_g = 1.0 + nrm((DEPTH, 3, d), 0.02)
    ffn_w_in = nrm((DEPTH, 2, d, 2 * D_FF), inv)
    ffn_w_out = nrm((DEPTH, 2, D_FF, d), D_FF ** -0.5)
    even_w_in = nrm((N_EVEN, d, EVEN_IN), inv)
    even_w_out = nrm((N_EVEN, d, d), inv)
    diff_lambda = nrm((N_EVEN, 4, DA_HD), 0.1)
    diff_norm_g = 1.0 + nrm((N_EVEN, DA_VD), 0.02)
    mlstm_conv_w = nrm((N_EVEN, ML_CONV, 2 * ML_HEADS * ML_QK), ML_CONV ** -0.5)
    mlstm_conv_b = nrm((N_EVEN, 2 * ML_HEADS * ML_QK), 0.02)
    fbias = jnp.concatenate([jnp.zeros((2, ML_HEADS), jnp.float32),
                             jnp.tile(jnp.linspace(3.0, 6.0, ML_HEADS, dtype=jnp.float32)[None], (2, 1))], axis=0)
    mlstm_gate_b = fbias[None] + nrm((N_EVEN, 4, ML_HEADS), 0.1)
    mlstm_norm_g = 1.0 + nrm((N_EVEN, ML_HEADS, ML_V), 0.02)
    odd_w_in = nrm((N_ODD, d, ODD_IN), inv)
    odd_w_out = nrm((N_ODD, d, d), inv)
    gla_w_gate = nrm((N_ODD, 2, GLA_RANK, GLA_HEADS * GLA_K), GLA_RANK ** -0.5)
    gla_b_gate = nrm((N_ODD, 2, GLA_HEADS * GLA_K), 0.1)
    gla_norm_g = 1.0 + nrm((N_ODD, GLA_V), 0.02)
    final_g = 1.0 + nrm((d,), 0.02)
    return {"x": x, "c": c, "ctx": ctx, "c_ctx": c_ctx, "ada_w": ada_w, "ada_b": ada_b,
            "norm_g": norm_g, "ffn_w_in": ffn_w_in, "ffn_w_out": ffn_w_out,
            "even_w_in": even_w_in, "even_w_out": even_w_out, "diff_lambda": diff_lambda,
            "diff_norm_g": diff_norm_g, "mlstm_conv_w": mlstm_conv_w, "mlstm_conv_b": mlstm_conv_b,
            "mlstm_gate_b": mlstm_gate_b, "mlstm_norm_g": mlstm_norm_g, "odd_w_in": odd_w_in,
            "odd_w_out": odd_w_out, "gla_w_gate": gla_w_gate, "gla_b_gate": gla_b_gate,
            "gla_norm_g": gla_norm_g, "final_g": final_g}

def second_block(x, c, ctx, c_ctx, ada_w, ada_b, norm_g, ffn_w_in, ffn_w_out, even_w_in, even_w_out,
              diff_lambda, diff_norm_g, mlstm_conv_w, mlstm_conv_b, mlstm_gate_b, mlstm_norm_g,
              odd_w_in, odd_w_out, gla_w_gate, gla_b_gate, gla_norm_g, final_g):
    bsz, n_tok, d = x.shape
    rows = n_tok // GRID_W
    rope = axial_rope_tables_2(rows, x.dtype)
    s_lat = jax.nn.silu(c)
    s_ctx = jax.nn.silu(c_ctx)
    hctx = ctx
    for l in range(DEPTH):
        last = l == DEPTH - 1
        mx = (s_lat @ ada_w[l] + ada_b[l]).reshape(bsz, N_MOD, 1, d)
        mc = (s_ctx @ ada_w[l] + ada_b[l]).reshape(N_MOD, d)
        x = x + 0.5 * mx[:, 2] * swiglu(ada_norm(x, norm_g[l, 0], mx[:, 0], mx[:, 1]), ffn_w_in[l, 0], ffn_w_out[l, 0])
        hctx = hctx + 0.5 * mc[2] * swiglu(ada_norm(hctx, norm_g[l, 0], mc[0], mc[1]), ffn_w_in[l, 0], ffn_w_out[l, 0])
        hx = ada_norm(x, norm_g[l, 1], mx[:, 3], mx[:, 4])
        hc = ada_norm(hctx, norm_g[l, 1], mc[3], mc[4])
        if l % 2 == 0:
            e = l // 2
            lam_init = 0.8 - 0.6 * math.exp(-0.3 * l)
            yx, yc = even_mixer(hx, hc, even_w_in[e], even_w_out[e], diff_lambda[e], diff_norm_g[e],
                                mlstm_conv_w[e], mlstm_conv_b[e], mlstm_gate_b[e], mlstm_norm_g[e],
                                lam_init, rope, not last)
        else:
            o = l // 2
            yx, yc = odd_mixer(hx, hc, odd_w_in[o], odd_w_out[o], gla_w_gate[o], gla_b_gate[o],
                               gla_norm_g[o], not last)
        x = x + mx[:, 5] * yx
        x = x + 0.5 * mx[:, 8] * swiglu(ada_norm(x, norm_g[l, 2], mx[:, 6], mx[:, 7]), ffn_w_in[l, 1], ffn_w_out[l, 1])
        if not last:
            hctx = hctx + mc[5] * yc
            hctx = hctx + 0.5 * mc[8] * swiglu(ada_norm(hctx, norm_g[l, 2], mc[6], mc[7]), ffn_w_in[l, 1], ffn_w_out[l, 1])
    return rms_norm(x, final_g)


_first_inputs = second_inputs


def second_inputs(seed=0):
    import zlib

    import numpy as np

    out = dict(_first_inputs(seed))
    spreads = {}
    factors = {}
    for name, (base, spread) in spreads.items():
        noise = np.random.default_rng([zlib.crc32(name.encode()), seed]).standard_normal(out[name].shape)
        drawn = base * np.exp(spread * noise) if base else spread * noise
        out[name] = jnp.asarray(drawn.astype(out[name].dtype))
    for name, factor in factors.items():
        out[name] = (out[name] * factor).astype(out[name].dtype)
    return out


_narrow_inputs = second_inputs


def second_inputs(seed=0):
    out = dict(_narrow_inputs(seed))
    wider = {'norm_g': 9.14,
     'diff_lambda': 6.13,
     'diff_norm_g': 12.0,
     'mlstm_conv_b': 12.0,
     'mlstm_norm_g': 12.0,
     'gla_w_gate': 4.28,
     'gla_b_gate': 12.0,
     'gla_norm_g': 12.0,
     'final_g': 3.18}
    for name, times in wider.items():
        mean = out[name].mean()
        out[name] = (mean + times * (out[name] - mean)).astype(out[name].dtype)
    return out


def setup_inputs(seed=0):
    out = dict(first_inputs(seed))
    for name, value in second_inputs(seed + 1).items():
        if name != "x":
            out[name + "_2"] = value
    return out


def reference(
    x, c, ctx, c_ctx, w_mod, b_mod, g_pre, g_post, w_in, w_out, sink, w_fourier, conv_w, conv_b,
    c_2, ctx_2, c_ctx_2, ada_w_2, ada_b_2, norm_g_2, ffn_w_in_2, ffn_w_out_2, even_w_in_2,
    even_w_out_2, diff_lambda_2, diff_norm_g_2, mlstm_conv_w_2, mlstm_conv_b_2, mlstm_gate_b_2,
    mlstm_norm_g_2, odd_w_in_2, odd_w_out_2, gla_w_gate_2, gla_b_gate_2, gla_norm_g_2,
    final_g_2,
):
    x = first_block(
        x, c, ctx, c_ctx, w_mod, b_mod, g_pre, g_post, w_in, w_out, sink, w_fourier, conv_w,
        conv_b,
    )
    return second_block(
        x, c_2, ctx_2, c_ctx_2, ada_w_2, ada_b_2, norm_g_2, ffn_w_in_2, ffn_w_out_2,
        even_w_in_2, even_w_out_2, diff_lambda_2, diff_norm_g_2, mlstm_conv_w_2, mlstm_conv_b_2,
        mlstm_gate_b_2, mlstm_norm_g_2, odd_w_in_2, odd_w_out_2, gla_w_gate_2, gla_b_gate_2,
        gla_norm_g_2, final_g_2,
    )


_drawn_inputs = setup_inputs


def setup_inputs(seed=0):
    import zlib

    import numpy as np

    out = dict(_drawn_inputs(seed))
    spreads = {}
    factors = {'b_mod': 3.092,
     'sink': 21.561,
     'conv_b': 8.0,
     'mlstm_conv_b_2': 3.831,
     'mlstm_norm_g_2': 3.322}
    for name, (base, spread) in spreads.items():
        noise = np.random.default_rng([zlib.crc32(name.encode()), seed]).standard_normal(out[name].shape)
        drawn = base * np.exp(spread * noise) if base else spread * noise
        out[name] = jnp.asarray(drawn.astype(out[name].dtype))
    for name, factor in factors.items():
        out[name] = (out[name] * factor).astype(out[name].dtype)
    return out
```

```python
import math
from contextlib import ExitStack

import numpy as np

import concourse.bass as bass
from concourse import mybir

F32 = mybir.dt.float32
U32 = mybir.dt.uint32
ALU = mybir.AluOpType
ACT = mybir.ActivationFunctionType
AX = mybir.AxisListType

P = 128
D = 1024
KC = D // P
SEQ = 256
CTX = 256
NT = SEQ + CTX
TT = NT // P
DEPTH = 2
EPS = 1e-6
BANK = 512

HD = 64
HEADS = 8
Q_PER_KV = 4
PROJ1 = 2816
D_FF = 2816
FC = D_FF // P
EVEN_IN = 3088
ODD_IN = 3104
DA_HEADS = 4
ML_HEADS = 4
GLA_HEADS = 4
CHUNK = 64
LAM_INIT = 0.8 - 0.6 * math.exp(-0.3 * 0)
GLA_TAU = 16.0

RING = 4
SEG = 256
NEG = -1.0e30


def shape_constants():
    c = {}
    c["ident"] = np.eye(P, dtype=np.float32)
    freqs = HD // 4
    inv = np.power(np.float32(10000.0), -np.arange(freqs, dtype=np.float32) / np.float32(freqs)).astype(np.float32)
    t = np.arange(SEQ)
    pos = np.stack([t // 64, t % 64]).astype(np.float32)
    rope = np.zeros((P, 2, SEQ), np.float32)
    for p in range(P):
        axis, half, f = (p % 64) // 32, (p % 32) // 16, p % 16
        ang = (pos[axis] * inv[f]).astype(np.float32)
        rope[p, 0] = np.cos(ang)
        rope[p, 1] = np.sin(ang) * (-1.0 if half == 0 else 1.0)
    c["rope"] = rope.reshape(P, 2 * SEQ)
    a64 = 2 * np.pi * (np.outer(np.arange(64), np.arange(64)) % 64) / 64
    dftc = np.zeros((P, 2, P))
    for g in range(2):
        s = slice(64 * g, 64 * g + 64)
        dftc[s, 0, s] = np.cos(a64) / 8
        dftc[s, 1, s] = np.sin(a64) / 8
    c["dftc"] = dftc.reshape(P, 2 * P).astype(np.float32)
    an = 2 * np.pi * (np.outer(np.arange(SEQ), np.arange(SEQ)) % SEQ) / SEQ
    dftn = np.stack([np.cos(an), -np.sin(an)]) / 16
    c["dftn"] = dftn.reshape(2, 2, P, SEQ).transpose(2, 1, 0, 3).reshape(P, 4 * SEQ).astype(np.float32)
    q, k = np.arange(P)[:, None], np.arange(P)[None, :]
    c["wmask"] = np.stack([np.where(k <= q, 0, NEG), np.where(k >= q, 0, NEG)], 1).reshape(P, 2 * P).astype(np.float32)
    m = np.zeros((P, 2, 2, SEQ), np.float32)
    for tile in range(2):
        s = tile * P + np.arange(P)[:, None]
        tq = np.arange(SEQ)[None, :]
        m[:, 0, tile] = np.where(tq >= s, 0, NEG)
        m[:, 1, tile] = np.where(tq <= s, 0, NEG)
    c["mmask"] = m.reshape(P, 4 * SEQ)
    s, tq = np.arange(P)[:, None], np.arange(P)[None, :]
    same = s // CHUNK == tq // CHUNK
    g = np.stack([(tq >= s) & same, (tq <= s) & same], 1).astype(np.float32)
    c["gmask"] = np.repeat(g[:, :, None, :], 2, 2).reshape(P, 2 * SEQ)
    r = np.ones((P, 2, SEQ), np.float32)
    r[:, 0, 0::CHUNK] = 0
    r[:, 1, CHUNK - 1::CHUNK] = 0
    c["restart"] = r.reshape(P, 2 * SEQ)
    sel = np.zeros((P, 8, P), np.float32)
    for d in range(2):
        for h in range(4):
            sel[32 * d + h, 4 * d + h] = 1
    c["sel"] = sel.reshape(P, 8 * P)
    ms = np.zeros((P, 2), np.float32)
    for j in range(4):
        for v in range(2):
            ms[32 * j + v, v] = 1
    c["modsel"] = ms
    return c


CONST = shape_constants()
CONST_COLS = {}
_at = 0
for _n, _a in CONST.items():
    CONST_COLS[_n] = (_at, _a.shape[1])
    _at += _a.shape[1]
CONST_W = _at


class Phase:

    def __init__(self, kind, rises, **kw):
        self.kind, self.rises, self.kw, self.start = kind, rises, kw, {}

    def at(self, name, k=0):
        return self.start.get(name, 0) + k


def gemm_rises(n, per, banks=4):
    r = {"unit_done": n * per}
    for j in range(banks):
        r[f"bank_free{j}"] = len(range(j, n, banks))
    return r


def plan():
    ph = []

    def add(kind, rises, **kw):
        ph.append(Phase(kind, rises, **kw))

    def gemm(w, col0, n, evac, tok=(0, NT), src="hT", ks=(KC,), **kw):
        add("gemm", gemm_rises(n, len(ks)), w=w, col0=col0, n=n, evac=evac, tok=tok, src=src, ks=ks, **kw)

    def norm(mode, nt, n=0, **kw):
        add("norm", {"sq_ready": 8, "sq_used": 8, "ms_ready": 1, "rms_ready": 1, "normed": 8 * nt // SEQ,
                     "h_ready": 8 if mode == "pre" else 0}, mode=mode, nt=nt, n=n, **kw)

    def mod(block, l):
        segs = (3 if block == 0 else 9) * D // SEG
        add("mod", {"mod_rows": segs, "mod_cols": segs, "bank_free4": segs // 2, "bank_free5": segs // 2,
                    "bank_free6": segs}, block=block, l=l, segs=segs)
        add("modvec", {"mod_ready": 1}, block=block, l=l)

    add("setup", {"rows_T": 2, "rows_sb": 2, "s_ready": 2})
    add("load", {"tokens_T": 8, **{f"bank_free{b}": 1 for b in range(8)}}, which=0)
    for l in range(DEPTH):
        both = l < DEPTH - 1
        nt = NT if both else SEQ
        mod(0, l)
        norm("pre", NT, block=0, l=l, n=0)
        gemm(("w_in", l), 0, 4, "copy", tok=(0, nt), dst=0)
        gemm(("w_in", l), 512, 1, "copy", dst=4)
        gemm(("w_in", l), 640, 1, "tok", dst=0)
        gemm(("w_in", l), 768, 16, "copy", tok=(0, nt), dst=6)
        na = 16 if both else 8
        add("mix1", {"k_swapped": 1, "roped": 1, "gates_done": 1, "scores_ready": 2 * na, "negmax_ready": 2 * na,
                     "probs_raw": 2 * na, "probs_ready": 2 * na, "probsT_done": 2 * na, "probsT_sb": 2 * na,
                     "pv_done": na, "att_gated": na // 2, "dft1": na // 4, "dft1_sb": na // 4, "dft2": 2, "dft2_sb": 2,
                     "dft3": 2, "dft3_gated": 2, "conv_done": 1}, l=l, both=both)
        gemm(("w_out", l), 0, 8, "copy", tok=(0, nt), src="mixT", dst="hT")
        norm("post", nt, block=0, l=l)
    add("load", {"tokens_T": 8, **{f"bank_free{b}": 1 for b in range(8)}}, which=1)
    for l in range(DEPTH):
        last = l == DEPTH - 1
        mod(1, l)

        def ffn(i, nt):
            norm("pre", nt, block=1, l=l, n=2 * i)
            gemm(("ffn_w_in_2", l, i), 0, 2 * FC, "swiglu", tok=(0, nt))
            gemm(("ffn_w_out_2", l, i), 0, KC, "resid", tok=(0, nt), src="big", ks=(8, 8, 6), l=l, g=2 * i)

        ffn(0, NT)
        norm("pre", NT, block=1, l=l, n=1)
        w = ("even_w_in_2", 0) if l == 0 else ("odd_w_in_2", 0)
        if l == 0:
            gemm(w, 0, 8, "copy", dst=0)
            gemm(w, 1024, 4, "tok", dst=0)
            gemm(w, 1536, 4, "copy", dst=8)
            gemm(w, 2048, 4, "tok", dst=512)
            gemm(w, 2560, 4, "copy", dst=12)
            add("even", {"roped2": 1, "lam_e": 1, "lam_ready": 1, "gate_rows": 2, "gate_bias": 1, "gate_ln": 1, "rows_ready": 1,
                         "scores_ready": 32, "negmax_ready": 16,
                         "probs_raw": 32, "probs_ready": 16, "probsT_done": 16, "probsT_sb": 16, "pv_done": 16, "att_evac": 8,
                         "conv_lin": 1, "conv_silu": 1, "acol_T": 1,
                         "qk_done": 4, "bcast": 16, "ebm": 8, "args": 8, "decay": 8, "weighted": 8,
                         "numden": 8, "den_abs": 8, "mem_done": 8,
                         "hsq": 2, "hsum": 2, "hms": 2, "hrms": 2, "osig": 1, "mix_done": 2}, l=l)
            gemm(("even_w_out_2", 0), 0, 8, "resid", src="mixT", l=l, g=1)
        else:
            gemm(w, 0, 4, "copy", tok=(0, SEQ), dst=0)
            gemm(w, 512, 4, "copy", dst=4)
            gemm(w, 1024, 8, "tok", dst=0)
            gemm(w, 2048, 8, "copy", tok=(0, SEQ), dst=8)
            add("odd", {"lr_done": 1, "lr_sb": 1, "z_done": 8, "z_sb": 8, "la_ln": 2, "cums": 8,
                        "c_exp": 8, "ckd": 8, "ckd_T": 8, "ckd_sb": 8, "st_done": 8, "st_sb": 8,
                        "x_exp": 8, "x_in": 8, "xkd_T": 8, "xkd_sb": 8, "a_done": 8, "a_sb": 8,
                        "u_done": 24, "u_sb": 24, "o_done": 1, "o_sb": 4, "r_silu": 1, "hsq": 4, "hsum": 4, "hms": 4, "hrms": 4,
                        "mix_done": 4}, l=l)
            gemm(("odd_w_out_2", 0), 0, 8, "resid", tok=(0, SEQ), src="mixT", l=l, g=1)
        ffn(1, SEQ if last else NT)
    norm("final", SEQ)
    add("store", {"out_T": 4, "out_sb": 4})
    total = {}
    for p in ph:
        p.start = dict(total)
        for k, v in p.rises.items():
            total[k] = total.get(k, 0) + v
    return ph, total


def build_program(nc, t, const, out):
    phases, total = plan()
    seen = {}
    with ExitStack() as stack:
        def sb(name, shape, dt=F32):
            return stack.enter_context(nc.sbuf_tensor(name, shape, dt))

        resid = sb("resid", [P, KC, NT])
        hT = sb("hT", [P, KC, NT])
        big = sb("big", [P, 24 * NT])
        big3 = big[:, :].rearrange("p (c n) -> p c n", n=NT)
        vtok = sb("vtok", [P, TT, D])
        mixT = sb("mixT", [P, KC, NT])
        ring = sb("ring", [P, RING, KC, P])
        modw = mixT[:, :, :].rearrange("p c n -> p (c n)").rearrange("p (s k n) -> p s k n", s=2, k=KC)
        modb = sb("modb", [P, 2, SEG])
        modr = sb("modr", [P, 2, SEG])
        scr = sb("scr", [P, 8192])
        cst = sb("cst", [P, CONST_W])
        rows1 = sb("rows1", [120, P])
        rows2 = sb("rows2", [47, P])
        cols1 = sb("cols1", [P, 120])
        cols2 = sb("cols2", [P, 47])
        svec = sb("svec", [P, 2, KC, 32])
        modT = [sb(f"modT{i}", [P, 24 if i < 2 else 72, 2]) for i in range(4)]
        modA = [sb(f"modA{i}", [P, 2 if i < 2 else 6, KC, 2]) for i in range(4)]
        sq = scr[:, 0:1024].rearrange("p (s n) -> p s n", n=NT)
        rms, rstd = scr[:, 1024:1536], scr[:, 1536:2048]
        sg = scr[:, 2048:3072].rearrange("p (s n) -> p s n", n=NT)
        ones = sb("ones", [P, SEQ])
        wfbd = sb("wfbd", [P, 4, P])
        sinkb = sb("sinkb", [P, DEPTH * HEADS])
        nsink = sb("nsink", [P, DEPTH * HEADS])
        dlam = sb("dlam", [P, 4 * HD])
        small = sb("small", [P, 192])
        wgate = sb("wgate", [P, KC, P])
        gateb = sb("gateb", [64, 2])
        wlr = sb("wlr", [P, KC, 64])
        wgla = sb("wgla", [64, GLA_HEADS * P])
        ps = stack.enter_context(nc.psum_tensor("ps", [P, 8, BANK], F32))

        sems = {}

        def S(name):
            if name not in sems:
                sems[name] = stack.enter_context(nc.semaphore(name))
            return sems[name]

        def up(ins, name, times=1):
            seen[name] = seen.get(name, 0) + times
            return ins.then_inc(S(name), 1)

        def C(name):
            a, n = CONST_COLS[name]
            return cst[:, a:a + n]

        for n in list(total) + ["consts_in", "tokens_in", "zeroed", "dve_chain", "act_chain", "out_written"]:
            S(n)
        w_full = [S(f"w_full{s}") for s in range(RING)]
        mod_full = [S(f"mod_full{s}") for s in range(2)]
        ident = C("ident")
        ropeC, ropeS = C("rope")[:, 0:SEQ], C("rope")[:, SEQ:2 * SEQ]
        dftn = C("dftn").rearrange("p (t c n) -> p t c n", t=2, c=2)
        wmask = C("wmask").rearrange("p (t k) -> p t k", t=2)
        mmask = C("mmask").rearrange("p (d t k) -> p d t k", d=2, t=2)
        gmask = C("gmask").rearrange("p (d k) -> p d k", d=2)
        restart = C("restart").rearrange("p (d k) -> p d k", d=2)
        sel = C("sel").rearrange("p (r n) -> p r n", n=P)
        onesPP = ones[:, 0:P]
        xstage = vtok[:, :, :]

        G_PRE, G_POST, NORM_G, FINAL_G = 32, 48, 64, 112
        CONV_W, CONV_B, MCONV_W, MCONV_B, DIFF_G, ML_G, GLA_G, GLA_B = 0, 12, 16, 28, 32, 33, 37, 39
        SWAP16 = [i ^ 16 for i in range(32)]

        block = stack.enter_context(nc.Block())

        def weight(key):
            w = t[key[0]]
            for i in key[1:]:
                w = w[i]
            return w

        def evacuated(eng, p):
            for b in range(8):
                if p.at(f"bank_free{b}"):
                    eng.wait_ge(S(f"bank_free{b}"), p.at(f"bank_free{b}"))

        def turns(eng, n, step):
            full = n // step
            if full > 1:
                with eng.Fori(0, full) as i:
                    yield i, range(step), full
            elif full == 1:
                yield 0, range(step), 1
            if n % step:
                yield full, range(n % step), 1

        def gemm_step(p):
            return 4

        def sp_setup(eng, p):
            loads = 0
            k = 0
            for name, n in (("c", 8), ("c_ctx", 8), ("c_2", 8), ("c_ctx_2", 8), ("g_pre", 16), ("g_post", 16),
                            ("norm_g_2", 48), ("final_g_2", 8)):
                eng.dma_start(rows1[k:k + n, :], t[name]).then_inc(S("consts_in"), 16)
                k += n
                loads += 1
            k = 0
            for name, n in (("conv_w", 12), ("conv_b", 4), ("mlstm_conv_w_2", 12), ("mlstm_conv_b_2", 4),
                            ("diff_norm_g_2", 1), ("mlstm_norm_g_2", 4), ("gla_norm_g_2", 2), ("gla_b_gate_2", 8)):
                eng.dma_start(rows2[k:k + n, :], t[name]).then_inc(S("consts_in"), 16)
                k += n
                loads += 1
            eng.dma_start(cst[:, :], const).then_inc(S("consts_in"), 16)
            eng.dma_start(sinkb[:, :], t["sink"].partition_broadcast(P)).then_inc(S("consts_in"), 16)
            eng.dma_start(dlam[:, :], t["diff_lambda_2"].partition_broadcast(P)).then_inc(S("consts_in"), 16)
            loads += 3
            eng.wait_ge(S("zeroed"), 6)
            for g in range(2):
                eng.dma_start(wfbd[64 * g:64 * g + 64, :, 64 * g:64 * g + 64], t["w_fourier"][g]).then_inc(S("consts_in"), 16)
            evw = t["even_w_in_2"][0].rearrange("(k p) n -> p k n", p=P)
            for g in range(2):
                for d in range(2):
                    at = 3072 + 8 * g + 4 * d
                    eng.dma_start(wgate[:, :, 64 * g + 32 * d:64 * g + 32 * d + 4], evw[:, :, at:at + 4],
                                  allow_slow_non_contiguous=True).then_inc(S("consts_in"), 16)
                    eng.dma_start(gateb[32 * d:32 * d + 4, g:g + 1], t["mlstm_gate_b_2"][8 * g + 4 * d:8 * g + 4 * d + 4, :],
                                  allow_slow_non_contiguous=True).then_inc(S("consts_in"), 16)
            odw = t["odd_w_in_2"][0].rearrange("(k p) n -> p k n", p=P)
            for d in range(2):
                eng.dma_start(wlr[:, :, 32 * d:32 * d + 16], odw[:, :, 3072 + 16 * d:3088 + 16 * d]).then_inc(S("consts_in"), 16)
                eng.dma_start(wgla[32 * d:32 * d + 16, :], t["gla_w_gate_2"][d]).then_inc(S("consts_in"), 16)
            loads += 2 + 8 + 4
            assert loads == CONST_LOADS

        CONST_LOADS = 33

        def sp_load(eng, p):
            if p.kw["which"] == 0:
                for i, n in enumerate(("x", "ctx")):
                    eng.dma_start(xstage[:, 2 * i:2 * i + 2, :], t[n].rearrange("(a p) d -> p a d", p=P)).then_inc(S("tokens_in"), 16)
            else:
                eng.wait_ge(S("unit_done"), p.at("unit_done"))
                eng.dma_start(xstage[:, 2:4, :], t["ctx_2"].rearrange("(a p) d -> p a d", p=P)).then_inc(S("tokens_in"), 16)

        def sp_mod(eng, p):
            blk, l, segs = p.kw["block"], p.kw["l"], p.kw["segs"]
            w = (t["w_mod"], t["ada_w_2"])[blk][l].rearrange("(k p) n -> p k n", p=P)
            b = (t["b_mod"], t["ada_b_2"])[blk]
            eng.wait_ge(S("unit_done"), p.at("unit_done"))
            with eng.Fori(0, segs // 2) as i:
                for par in range(2):
                    eng.wait_ge(S(f"bank_free{4 + par}"), p.at(f"bank_free{4 + par}") + i)
                    eng.dma_start(modw[:, par], w[:, :, bass.ds(i * (2 * SEG) + par * SEG, SEG)]).then_inc(mod_full[par], 16)
                    eng.dma_start(modb[0:2, par, :], b[l:l + 1, bass.ds(i * (2 * SEG) + par * SEG, SEG)].broadcast_to([2, SEG])).then_inc(mod_full[par], 16)

        def sp_gemm(eng, p):
            k = p.kw
            w, ks, u0 = weight(k["w"]), k["ks"], p.at("unit_done")
            per = len(ks)
            w3 = w.rearrange("(k p) n -> p k n", p=P)
            for i, js, _ in turns(eng, k["n"], gemm_step(p)):
                for j in js:
                    for s, kc in enumerate(ks):
                        u = u0 + j * per + s
                        if u >= RING:
                            eng.wait_ge(S("unit_done"), i * (4 * per) + (u - RING + 1))
                        if k["evac"] == "swiglu":
                            col = i * (2 * P) + ((j // 2) * P + (j % 2) * D_FF)
                        else:
                            col = i * (4 * P) + (k["col0"] + j * P)
                        eng.dma_start(ring[:, u % RING, 0:kc, :], w3[:, s * 8:s * 8 + kc, bass.ds(col, P)]).then_inc(w_full[u % RING], 16)

        def sp_store(eng, p):
            for tile in range(2):
                for half in range(2):
                    eng.wait_ge(S("out_sb"), 2 * tile + half + 1)
                    eng.dma_start(out[tile * P:(tile + 1) * P, half * 512:half * 512 + 512],
                                  vtok[:, tile, half * 512:half * 512 + 512]).then_inc(S("out_written"), 16)
            eng.wait_ge(S("out_written"), 64)

        mm, tr = nc.tensor.matmul, nc.tensor.transpose

        def pe_setup(eng, p):
            eng.wait_ge(S("consts_in"), 16 * CONST_LOADS)
            up(tr(ps[:, 0, 0:120], rows1[:, :], ident[0:120, 0:120]), "rows_T")
            up(tr(ps[:, 1, 0:47], rows2[:, :], ident[0:47, 0:47]), "rows_T")

        def pe_load(eng, p):
            which = p.kw["which"]
            eng.wait_ge(S("tokens_in"), 32 + 16 * which)
            if which == 0:
                eng.wait_ge(S("rows_sb"), 2)
            else:
                eng.wait_ge(S("normed"), p.at("normed"))
            evacuated(eng, p)
            for c in range(KC):
                tiles = range(4) if which == 0 else (2, 3)
                for a in tiles:
                    last = tr(ps[:, c, a * P:(a + 1) * P], xstage[:, a, c * P:(c + 1) * P], ident)
                up(last, "tokens_T")

        def pe_mod(eng, p):
            blk, segs = p.kw["block"], p.kw["segs"]
            if p.at("mod_rows") == 0:
                eng.wait_ge(S("s_ready"), 2)
            evacuated(eng, p)
            with eng.Fori(0, segs // 2) as i:
                for par in range(2):
                    eng.wait_ge(mod_full[par], i * 32 + (p.at("mod_rows") * 16 + 32))
                    eng.wait_ge(S(f"bank_free{4 + par}"), p.at(f"bank_free{4 + par}") + i)
                    for k in range(KC):
                        j = k % 4
                        last = mm(ps[32 * j:32 * j + 32, 4 + par, 0:SEG], svec[:, blk, k, :], modw[:, par, k, :],
                                  start=k < 4, stop=k >= 4)
                    up(last, "mod_rows", segs // 2)
                for par in range(2):
                    eng.wait_ge(S(f"bank_free{4 + par}"), p.at(f"bank_free{4 + par}") + i + 1)
                    eng.wait_ge(S("bank_free6"), p.at("bank_free6") + 2 * i + par)
                    for c in range(2):
                        last = mm(ps[:, 6, 2 * c:2 * c + 2], modr[:, par, c * P:(c + 1) * P], C("modsel"), start=True, stop=True)
                    up(last, "mod_cols", segs // 2)

        def pe_norm(eng, p):
            nt = p.kw["nt"]
            evacuated(eng, p)
            for c in range(KC):
                eng.wait_ge(S("sq_ready"), p.at("sq_ready", c + 1))
                up(mm(ps[:, 7, 0:nt], onesPP, sq[:, c % 2, 0:nt], start=c == 0, stop=c == KC - 1), "sq_used")

        def pe_gemm(eng, p):
            k = p.kw
            a, b = k["tok"]
            ks, u0 = k["ks"], p.at("unit_done")
            per = len(ks)
            src = {"hT": hT[:, :, :], "mixT": mixT[:, :, :], "big": big3}[k["src"]]
            if k["src"] == "hT":
                eng.wait_ge(S("h_ready"), p.at("h_ready"))
            evacuated(eng, p)
            for i, js, rounds in turns(eng, k["n"], gemm_step(p)):
                for j in js:
                    eng.wait_ge(S(f"bank_free{j}"), p.at(f"bank_free{j}") + i)
                    for s, kc in enumerate(ks):
                        u = u0 + j * per + s
                        eng.wait_ge(w_full[u % RING], i * (16 * per) + (16 * (u // RING) + 16))
                        w = ring[:, u % RING]
                        if k["evac"] == "tok":
                            for tile in range(TT):
                                for c in range(kc):
                                    last = mm(ps[:, j, tile * P:(tile + 1) * P], src[:, c, tile * P:(tile + 1) * P], w[:, c, :],
                                              start=c == 0, stop=c == kc - 1)
                        else:
                            for c in range(kc):
                                last = mm(ps[:, j, 0:b - a], w[:, c, :], src[:, s * 8 + c, a:b],
                                          start=s == 0 and c == 0, stop=s == per - 1 and c == kc - 1)
                        up(last, "unit_done", rounds)

        def pe_store(eng, p):
            eng.wait_ge(S("normed"), p.at("normed"))
            for tile in range(2):
                for half in range(2):
                    for c in range(4):
                        last = tr(ps[:, 2 * tile + half, c * P:(c + 1) * P], hT[:, half * 4 + c, tile * P:(tile + 1) * P], ident)
                    up(last, "out_T")

        chain = {"dve": 0, "act": 0}
        act = nc.scalar.activation

        def alink(ins):
            chain["act"] += 1
            ins.then_inc(S("act_chain"), 1)
            nc.scalar.wait_ge(S("act_chain"), chain["act"])

        def act_setup(eng, p):
            eng.wait_ge(S("zeroed"), 6)
            eng.wait_ge(S("rows_sb"), 2)
            for blk in range(2):
                up(act(svec[:, blk, :, 0:2], cols1[:, 16 * blk:16 * blk + 16].rearrange("p (v k) -> p k v", v=2), ACT.Silu), "s_ready")

        def act_load(eng, p):
            a = 0 if p.kw["which"] == 0 else SEQ
            for c in range(1, KC, 2):
                eng.wait_ge(S("tokens_T"), p.at("tokens_T", c + 1))
                up(act(resid[:, c, a:NT], ps[:, c, a:NT], ACT.Copy), f"bank_free{c}")

        def act_norm(eng, p):
            nt, mode = p.kw["nt"], p.kw["mode"]
            src = hT if mode == "post" else resid
            evacuated(eng, p)
            eng.wait_ge(S("normed"), p.at("normed")) if p.at("normed") else None
            for c in range(KC):
                if c >= 2:
                    eng.wait_ge(S("sq_used"), p.at("sq_used", c - 1))
                up(act(sq[:, c % 2, 0:nt], src[:, c, 0:nt], ACT.Square), "sq_ready")
            eng.wait_ge(S("ms_ready"), p.at("ms_ready", 1))
            up(act(rms[:, 0:nt], rms[:, 0:nt], ACT.Sqrt), "rms_ready")
            if mode == "pre":
                m = 2 * p.kw["block"] + p.kw["l"]
                for c in range(KC):
                    eng.wait_ge(S("normed"), p.at("normed", (c + 1) * (nt // SEQ)))
                    for v in range(nt // SEQ):
                        sh = modT[m][:, p.kw["n"] * 24 + c, v:v + 1]
                        cols = slice(v * SEQ, (v + 1) * SEQ)
                        last = act(hT[:, c, cols], hT[:, c, cols], ACT.Identity, bias=sh, scale=1.0)
                    up(last, "h_ready")

        def act_gemm(eng, p):
            k = p.kw
            a, b = k["tok"]
            n = b - a
            per, u0 = len(k["ks"]), p.at("unit_done")
            if k["evac"] == "resid":
                return
            for i, js, rounds in turns(eng, k["n"], gemm_step(p)):
                for j in js:
                    if k["evac"] == "swiglu":
                        if j % 2:
                            continue
                        eng.wait_ge(S("unit_done"), i * 4 + (u0 + j + 1))
                        eng.wait_ge(S(f"bank_free{j + 1}"), p.at(f"bank_free{j + 1}") + i)
                        up(act(sg[:, j // 2, 0:n], ps[:, j, 0:n], ACT.Silu), f"bank_free{j}", rounds)
                    elif j % 2:
                        eng.wait_ge(S("unit_done"), i * 4 + (u0 + j + 1))
                        up(act(gemm_dst(k, i, j, n), gemm_out(k, j, n), ACT.Copy), f"bank_free{j}", rounds)

        def gemm_out(k, j, n):
            if k["evac"] == "tok":
                return ps[:, j, :].rearrange("p (a n) -> p a n", n=P)
            return ps[:, j, 0:n]

        def gemm_dst(k, i, j, n):
            if k["evac"] == "tok":
                return vtok[:, :, bass.ds(i * (4 * P) + (k["dst"] + j * P), P)]
            if k["dst"] == "hT":
                return hT[:, :, :].rearrange("p c n -> p (c n)")[:, bass.ds(i * (4 * NT) + j * NT, n)]
            return big[:, bass.ds(i * (4 * NT) + (k["dst"] + j) * NT, n)]

        def act_store(eng, p):
            for g in (1, 3):
                eng.wait_ge(S("out_T"), g + 1)
                eng.wait_ge(S("out_sb"), g)
                up(act(vtok[:, g // 2, (g % 2) * 512:(g % 2) * 512 + 512], ps[:, g, :], ACT.Copy), "out_sb")

        V = nc.vector

        def link(ins):
            chain["dve"] += 1
            ins.then_inc(S("dve_chain"), 1)
            nc.vector.wait_ge(S("dve_chain"), chain["dve"])

        def dve_setup(eng, p):
            for z in (svec[:, :, :, :], wfbd[:, :, :], modb[:, :, :], wgate[:, :, :], gateb[:, :], wlr[:, :, :]):
                V.memset(z, 0.0).then_inc(S("zeroed"), 1)
            link(V.memset(ones[:, :], 1.0))
            for i, (dst, n) in enumerate(((cols1, 120), (cols2, 47))):
                eng.wait_ge(S("rows_T"), i + 1)
                up(V.tensor_copy(dst[:, :], ps[:, i, 0:n]), "rows_sb")
            eng.wait_ge(S("consts_in"), 16 * CONST_LOADS)
            eng.wait_ge(S("rows_sb"), 2)
            link(V.tensor_scalar(nsink[:, :], sinkb[:, :], -1.0, None, ALU.mult))

        def dve_load(eng, p):
            a = 0 if p.kw["which"] == 0 else SEQ
            for c in range(0, KC, 2):
                eng.wait_ge(S("tokens_T"), p.at("tokens_T", c + 1))
                up(V.tensor_copy(resid[:, c, a:NT], ps[:, c, a:NT]), f"bank_free{c}")

        def dve_mod(eng, p):
            segs, m = p.kw["segs"], 2 * p.kw["block"] + p.kw["l"]
            flat = modT[m][:, :, :].rearrange("p c v -> p (c v)")
            with eng.Fori(0, segs // 2) as i:
                for par in range(2):
                    eng.wait_ge(S("mod_rows"), p.at("mod_rows") + 2 * i + par + 1)
                    up(V.tensor_tensor(modr[:, par, :], ps[:, 4 + par, 0:SEG], modb[:, par, :], ALU.add), f"bank_free{4 + par}", segs // 2)
                for par in range(2):
                    eng.wait_ge(S("mod_cols"), p.at("mod_cols") + 2 * i + par + 1)
                    up(V.tensor_copy(flat[:, bass.ds(i * 8 + par * 4, 4)], ps[:, 6, 0:4]), "bank_free6", segs // 2)

        def dve_modvec(eng, p):
            blk, l = p.kw["block"], p.kw["l"]
            m = 2 * blk + l
            evacuated(eng, p)

            def gcol(at):
                return cols1[:, at:at + KC].unsqueeze(2).broadcast_to([P, KC, 2])

            T, A = modT[m], modA[m]
            if blk == 0:
                V.scalar_tensor_tensor(A[:, 0], T[:, 8:16, :], 1.0, gcol(G_PRE + 8 * l), ALU.add, ALU.mult)
                last = V.tensor_tensor(A[:, 1], T[:, 16:24, :], gcol(G_POST + 8 * l), ALU.mult)
            else:
                for i in range(3):
                    V.scalar_tensor_tensor(A[:, 2 * i], T[:, 24 * i + 8:24 * i + 16, :], 1.0, gcol(NORM_G + 24 * l + 8 * i), ALU.add, ALU.mult)
                    last = V.tensor_scalar(A[:, 2 * i + 1], T[:, 24 * i + 16:24 * i + 24, :], 1.0 if i == 1 else 0.5, None, ALU.mult)
            up(last, "mod_ready")
            eng.wait_ge(S("mod_ready"), p.at("mod_ready", 1))

        def dve_norm(eng, p):
            nt, mode = p.kw["nt"], p.kw["mode"]
            eng.wait_ge(S("sq_used"), p.at("sq_used", 8))
            up(V.tensor_scalar(rms[:, 0:nt], ps[:, 7, 0:nt], 1.0 / D, EPS, ALU.mult, ALU.add), "ms_ready")
            eng.wait_ge(S("rms_ready"), p.at("rms_ready", 1))
            link(V.reciprocal(rstd[:, 0:nt], rms[:, 0:nt]))
            if mode != "final":
                m = 2 * p.kw["block"] + p.kw["l"]
            for c in range(KC):
                for v in range(nt // SEQ):
                    cols = slice(v * SEQ, (v + 1) * SEQ)
                    if mode == "pre":
                        up(V.scalar_tensor_tensor(hT[:, c, cols], resid[:, c, cols], modA[m][:, 2 * p.kw["n"] if p.kw["block"] else 0, c, v:v + 1],
                                                  rstd[:, cols], ALU.mult, ALU.mult), "normed")
                    elif mode == "post":
                        link(V.scalar_tensor_tensor(hT[:, c, cols], hT[:, c, cols], modA[m][:, 1, c, v:v + 1], rstd[:, cols], ALU.mult, ALU.mult))
                        up(V.tensor_tensor(resid[:, c, cols], resid[:, c, cols], hT[:, c, cols], ALU.add), "normed")
                    else:
                        up(V.scalar_tensor_tensor(hT[:, c, cols], resid[:, c, cols], cols1[:, FINAL_G + c:FINAL_G + c + 1],
                                                  rstd[:, cols], ALU.mult, ALU.mult), "normed")
            eng.wait_ge(S("normed"), p.at("normed", 8 * (nt // SEQ)))

        def dve_gemm(eng, p):
            k = p.kw
            a, b = k["tok"]
            n = b - a
            per, u0 = len(k["ks"]), p.at("unit_done")
            for i, js, rounds in turns(eng, k["n"], gemm_step(p)):
                for j in js:
                    if k["evac"] != "resid" and (j % 2) != (k["evac"] == "swiglu"):
                        continue
                    eng.wait_ge(S("unit_done"), i * (4 * per) + (u0 + j * per + per))
                    if k["evac"] == "swiglu":
                        eng.wait_ge(S(f"bank_free{j - 1}"), p.at(f"bank_free{j - 1}") + i + 1)
                        up(V.tensor_tensor(big[:, bass.ds(i * (2 * NT) + (j // 2) * NT, n)], sg[:, j // 2, 0:n], ps[:, j, 0:n], ALU.mult),
                           f"bank_free{j}", rounds)
                    elif k["evac"] == "resid":
                        gate = modA[2 + k["l"]][:, :, :, :].rearrange("p s c v -> p (s c v)")
                        for v in range(n // SEQ):
                            cols = bass.ds(i * (4 * NT) + j * NT + v * SEQ, SEQ)
                            rs = resid[:, :, :].rearrange("p c n -> p (c n)")[:, cols]
                            at = (2 * k["g"] + 1) * KC * 2 + j * 2 + v
                            last = V.scalar_tensor_tensor(rs, ps[:, j, v * SEQ:(v + 1) * SEQ], gate[:, bass.ds(i * 8 + at, 1)], rs,
                                                          ALU.mult, ALU.add)
                        up(last, f"bank_free{j}", rounds)
                    else:
                        up(V.tensor_copy(gemm_dst(k, i, j, n), gemm_out(k, j, n)), f"bank_free{j}", rounds)

        def dve_store(eng, p):
            for g in (0, 2):
                eng.wait_ge(S("out_T"), g + 1)
                if g:
                    eng.wait_ge(S("out_sb"), g)
                up(V.tensor_copy(vtok[:, g // 2, (g % 2) * 512:(g % 2) * 512 + 512], ps[:, g, :]), "out_sb")

        probs = scr[:, 0:2048].rearrange("p (s k) -> p s k", k=512)
        probsT = scr[:, 2048:4096].rearrange("p (s b q) -> p s b q", s=2, b=4)
        dftU = scr[:, 4096:6144].rearrange("p (g k) -> p g k", k=512)
        dftF = scr[:, 6144:7168].rearrange("p (c n) -> p c n", n=NT)
        kswap = scr[:, 7168:7680]
        nmx, nm, rsum, esink = (small[:, 32 * i:32 * i + 32] for i in range(4))

        def items1(p):
            x = [(h, 0, 0, 4) for h in range(HEADS)]
            return x + ([(h, SEQ, SEQ, 2) for h in range(HEADS)] if p.kw["both"] else [])

        def pe_mix1(eng, p):
            l, sets = p.kw["l"], 2 if p.kw["both"] else 1
            items = items1(p)
            evacuated(eng, p)
            for c in range(2):
                for s in range(sets):
                    for a in range(2):
                        last = mm(ps[:, 2 * c + s, a * 256:a * 256 + 256], big3[:, 10 + c, s * SEQ + a * P:s * SEQ + a * P + P],
                                  C("dftc"), start=True, stop=True)
                    up(last, "dft1")
            eng.wait_ge(S("dft1_sb"), p.at("dft1_sb", 2 * sets))
            for c in range(2):
                for s in range(sets):
                    for a in range(2):
                        for part in range(2):
                            last = mm(ps[:, 4 + c, s * SEQ:s * SEQ + SEQ], dftU[:, 2 * c + s, a * 256 + part * P:a * 256 + part * P + P],
                                      dftn[:, a, part, :], start=a + part == 0, stop=a + part == 2)
                up(last, "dft2")
            for c in range(2):
                eng.wait_ge(S("dft2_sb"), p.at("dft2_sb", c + 1))
                up(mm(ps[:, 6 + c, 0:sets * SEQ], wfbd[:, 2 * l + c, :], dftF[:, c, 0:sets * SEQ], start=True, stop=True), "dft3")

            eng.wait_ge(S("k_swapped"), p.at("k_swapped", 1))

            def scores(i):
                h, q0, k0, kt = items[i]
                if i >= 2:
                    eng.wait_ge(S("probs_raw"), p.at("probs_raw", 2 * i - 2))
                r = slice(64 * (h % 2), 64 * (h % 2) + 64)
                keys = big3[r, 4, k0:k0 + kt * P] if h // Q_PER_KV == h % 2 else kswap[r, k0:k0 + kt * P]
                for qt in range(2):
                    b = 2 * (i % 2) + qt
                    last = mm(ps[:, b, 0:kt * P], big3[r, h // 2, q0 + qt * P:q0 + qt * P + P], keys, start=True, stop=q0 > 0)
                    if q0 == 0:
                        cut = (1 - qt) * P
                        last = mm(ps[:, b, cut:cut + P], ident, wmask[:, qt, :], start=False, stop=True)
                    up(last, "scores_ready")

            def transposes(i):
                h, q0, k0, kt = items[i]
                for qt in range(2):
                    eng.wait_ge(S("probs_ready"), p.at("probs_ready", 2 * i + qt + 1))
                    if i >= 1:
                        eng.wait_ge(S("probsT_sb"), p.at("probsT_sb", 2 * i - 1 + qt))
                    for kb in range(kt):
                        last = tr(ps[:, 4 + qt, kb * P:kb * P + P], probs[:, 2 * (i % 2) + qt, kb * P:kb * P + P], ident)
                    up(last, "probsT_done")

            def values(i):
                h, q0, k0, kt = items[i]
                pair = i // 2
                eng.wait_ge(S("probsT_sb"), p.at("probsT_sb", 2 * i + 2))
                if pair < 2:
                    eng.wait_ge(S("dft3_gated"), p.at("dft3_gated", 2))
                else:
                    eng.wait_ge(S("att_gated"), p.at("att_gated", pair - 1))
                g, r = h // Q_PER_KV, slice(64 * (h % 2), 64 * (h % 2) + 64)
                for kb in range(kt):
                    last = mm(ps[r, 6 + pair % 2, 0:SEQ], vtok[:, k0 // P + kb, g * HD:(g + 1) * HD], probsT[:, i % 2, kb, :],
                              start=kb == 0, stop=kb == kt - 1)
                up(last, "pv_done")

            scores(0)
            for i in range(len(items)):
                if i + 1 < len(items):
                    scores(i + 1)
                transposes(i)
                if i:
                    values(i - 1)
            values(len(items) - 1)
            eng.wait_ge(S("att_gated"), p.at("att_gated", len(items) // 2))
            eng.wait_ge(S("conv_done"), p.at("conv_done", 1))

        def act_mix1(eng, p):
            l, sets = p.kw["l"], 2 if p.kw["both"] else 1
            items, nt = items1(p), sets * SEQ
            evacuated(eng, p)
            for c in range(2):
                for s in range(sets):
                    eng.wait_ge(S("dft1"), p.at("dft1", sets * c + s + 1))
                    up(act(dftU[:, 2 * c + s, :], ps[:, 2 * c + s, :], ACT.Copy), "dft1_sb")
            for c in range(2):
                eng.wait_ge(S("dft2"), p.at("dft2", c + 1))
                up(act(dftF[:, c, 0:nt], ps[:, 4 + c, 0:nt], ACT.Copy), "dft2_sb")
            for a, b in ((12, 14), (6, 10), (20, 22)):
                last = act(big3[:, a:b, 0:nt], big3[:, a:b, 0:nt], ACT.Silu)
            up(last, "gates_done")

            def exps(i):
                h, q0, k0, kt = items[i]
                for qt in range(2):
                    n = 2 * i + qt
                    eng.wait_ge(S("negmax_ready"), p.at("negmax_ready", n + 1))
                    act(esink[:, n:n + 1], sinkb[:, l * HEADS + h:l * HEADS + h + 1], ACT.Exp, bias=nm[:, n:n + 1])
                    b = 2 * (i % 2) + qt
                    up(act(probs[:, b, 0:kt * P], ps[:, b, 0:kt * P], ACT.Exp, bias=nm[:, n:n + 1], scale=HD ** -0.5,
                           accum_out=rsum[:, n:n + 1]), "probs_raw")

            def keep_T(i):
                h, q0, k0, kt = items[i]
                if i >= 2:
                    eng.wait_ge(S("pv_done"), p.at("pv_done", i - 1))
                for qt in range(2):
                    eng.wait_ge(S("probsT_done"), p.at("probsT_done", 2 * i + qt + 1))
                    up(act(probsT[:, i % 2, 0:kt, qt * P:qt * P + P], ps[:, 4 + qt, 0:kt * P].rearrange("p (b q) -> p b q", q=P), ACT.Copy),
                       "probsT_sb")

            for i in range(len(items)):
                exps(i)
                if i:
                    keep_T(i - 1)
            keep_T(len(items) - 1)

        def conv3(y, x, w, bias, nt, done=None):
            link(V.tensor_scalar(y[:, 0:nt], x[:, 0:nt], w(1), bias, ALU.mult, ALU.add))
            for s in range(nt // SEQ):
                a, b = s * SEQ, (s + 1) * SEQ
                link(V.scalar_tensor_tensor(y[:, a + 1:b], x[:, a:b - 1], w(0), y[:, a + 1:b], ALU.mult, ALU.add))
                ins = V.scalar_tensor_tensor(y[:, a:b - 1], x[:, a + 1:b], w(2), y[:, a:b - 1], ALU.mult, ALU.add)
                up(ins, done) if done and b == nt else link(ins)

        def rotary(chunks, n, tmp, name):
            shape = [P, n, SEQ]
            x, tmp = chunks[:, :, 0:SEQ], tmp.rearrange("p (c n) -> p c n", n=SEQ)
            link(V.stream_shuffle(tmp, x, SWAP16))
            link(V.tensor_tensor(tmp, tmp, ropeS.unsqueeze(1).broadcast_to(shape), ALU.mult))
            link(V.tensor_tensor(x, x, ropeC.unsqueeze(1).broadcast_to(shape), ALU.mult))
            up(V.tensor_tensor(x, x, tmp, ALU.add), name)

        def dve_mix1(eng, p):
            l, sets = p.kw["l"], 2 if p.kw["both"] else 1
            items, nt = items1(p), sets * SEQ
            hflat = hT[:, :, :].rearrange("p c n -> p (c n)")
            evacuated(eng, p)
            rotary(big3[:, 0:5], 5, hflat[:, 0:5 * SEQ], "roped")
            eng.wait_ge(S("roped"), p.at("roped", 1))
            V.tensor_copy(kswap[0:64, :], big3[64:128, 4, :])
            up(V.tensor_copy(kswap[64:128, :], big3[0:64, 4, :]), "k_swapped")
            for c in range(2):
                t_, y = hT[:, 4 + c, 0:nt], hT[:, 6 + c, 0:nt]
                link(V.tensor_tensor(t_, big3[:, 14 + c, 0:nt], big3[:, 18 + c, 0:nt], ALU.mult))
                conv3(y, t_, lambda tap: cols2[:, CONV_W + (l * 3 + tap) * 2 + c:CONV_W + (l * 3 + tap) * 2 + c + 1],
                      cols2[:, CONV_B + 2 * l + c:CONV_B + 2 * l + c + 1], nt)
                link(V.tensor_tensor(y, y, big3[:, 16 + c, 0:nt], ALU.mult))
            eng.wait_ge(S("gates_done"), p.at("gates_done", 1))
            up(V.tensor_tensor(mixT[:, 6:8, 0:nt], hT[:, 6:8, 0:nt], big3[:, 20:22, 0:nt], ALU.mult), "conv_done")
            for c in range(2):
                eng.wait_ge(S("dft3"), p.at("dft3", c + 1))
                up(V.tensor_tensor(mixT[:, 4 + c, 0:nt], ps[:, 6 + c, 0:nt], big3[:, 12 + c, 0:nt], ALU.mult), "dft3_gated")

            def maxima(i):
                h, q0, k0, kt = items[i]
                for qt in range(2):
                    n = 2 * i + qt
                    eng.wait_ge(S("scores_ready"), p.at("scores_ready", n + 1))
                    link(V.reduce_max(nmx[:, n:n + 1], ps[:, 2 * (i % 2) + qt, 0:kt * P], AX.X, negate=True))
                    up(V.tensor_scalar(nm[:, n:n + 1], nmx[:, n:n + 1], HD ** -0.5, nsink[:, l * HEADS + h:l * HEADS + h + 1],
                                       ALU.mult, ALU.min), "negmax_ready")

            def normalise(i):
                h, q0, k0, kt = items[i]
                for qt in range(2):
                    n = 2 * i + qt
                    eng.wait_ge(S("probs_raw"), p.at("probs_raw", n + 1))
                    link(V.tensor_tensor(rsum[:, n:n + 1], rsum[:, n:n + 1], esink[:, n:n + 1], ALU.add))
                    link(V.reciprocal(nmx[:, n:n + 1], rsum[:, n:n + 1]))
                    pr = probs[:, 2 * (i % 2) + qt, 0:kt * P]
                    up(V.tensor_scalar(pr, pr, nmx[:, n:n + 1], None, ALU.mult), "probs_ready")

            def gate(pair):
                h, q0, k0, kt = items[2 * pair]
                eng.wait_ge(S("pv_done"), p.at("pv_done", 2 * pair + 2))
                up(V.tensor_tensor(mixT[:, h // 2, q0:q0 + SEQ], ps[:, 6 + pair % 2, 0:SEQ], big3[:, 6 + h // 2, q0:q0 + SEQ], ALU.mult),
                   "att_gated")

            maxima(0)
            for i in range(len(items)):
                if i + 1 < len(items):
                    maxima(i + 1)
                normalise(i)
                if i >= 3 and i % 2:
                    gate((i - 3) // 2)
            gate(len(items) // 2 - 1)

        wT = scr[:, 2048:3072].rearrange("p (s k) -> p s k", k=512)
        decay = scr[:, 3072:6144].rearrange("p (s t r q) -> p s t r q", s=2, t=2, r=3)
        dargs = scr[:, 6144:7168].rearrange("p (t r q) -> p t r q", t=2, r=2)
        dnm, ebm = scr[:, 7168:7680], scr[:, 7680:8192]
        hsq = scr[:, 0:2048].rearrange("p (h n) -> p h n", n=NT)
        grow = [hT[0:64, i, :] for i in range(4)]
        acol = hT[:, 5, 0:4 * 64]
        items2 = [(h, qt) for h in range(DA_HEADS) for qt in range(TT)]

        def keys2(qt):
            return (0, 4) if qt < 2 else (SEQ, 2)

        def pe_even(eng, p):
            evacuated(eng, p)
            for g in range(2):
                for k in range(KC):
                    last = mm(ps[0:64, 6 + g, :], wgate[:, k, 64 * g:64 * g + 64], hT[:, k, :], start=k == 0, stop=k == KC - 1)
                up(last, "gate_rows")
            eng.wait_ge(S("roped2"), p.at("roped2", 1))

            def scores(i):
                h, qt = items2[i]
                k0, kt = keys2(qt)
                if i >= 2:
                    eng.wait_ge(S("probs_raw"), p.at("probs_raw", 2 * i - 2))
                for c in range(2):
                    r = slice(64 * c, 64 * c + 64)
                    up(mm(ps[:, 2 * (i % 2) + c, 0:kt * P], big3[r, h, qt * P:qt * P + P], big3[r, 4 + h, k0:k0 + kt * P],
                          start=True, stop=True), "scores_ready")

            def transposes(i):
                kt = keys2(items2[i][1])[1]
                eng.wait_ge(S("probs_ready"), p.at("probs_ready", i + 1))
                if i >= 2:
                    eng.wait_ge(S("probsT_sb"), p.at("probsT_sb", i - 1))
                for kb in range(kt):
                    last = tr(ps[:, 4 + i % 2, kb * P:kb * P + P], probs[:, 2 * (i % 2), kb * P:kb * P + P], ident)
                up(last, "probsT_done")

            def values(i):
                h, qt = items2[i]
                k0, kt = keys2(qt)
                g = i // 2
                eng.wait_ge(S("probsT_sb"), p.at("probsT_sb", i + 1))
                if g < 2:
                    eng.wait_ge(S("gate_bias"), p.at("gate_bias", 1))
                else:
                    eng.wait_ge(S("att_evac"), p.at("att_evac", g - 1))
                for kb in range(kt):
                    last = mm(ps[:, 6 + g % 2, (qt % 2) * P:(qt % 2) * P + P], vtok[:, k0 // P + kb, h * P:h * P + P],
                              wT[:, i % 2, kb * P:kb * P + P], start=kb == 0, stop=kb == kt - 1)
                up(last, "pv_done")

            scores(0)
            for i in range(len(items2)):
                if i + 1 < len(items2):
                    scores(i + 1)
                transposes(i)
                if i:
                    values(i - 1)
            values(len(items2) - 1)

            def head_sums(n):
                eng.wait_ge(S("hsq"), p.at("hsq", n + 1))
                for h in range(4):
                    last = mm(ps[:, h, :], onesPP, hsq[:, h, :], start=True, stop=True)
                up(last, "hsum")

            head_sums(0)
            eng.wait_ge(S("rows_ready"), p.at("rows_ready", 1))
            eng.wait_ge(S("att_evac"), p.at("att_evac", 8))
            for a in range(TT):
                last = tr(ps[:, 7, a * 64:a * 64 + 64], grow[0][:, a * P:a * P + P], ident[0:64, 0:64])
            up(last, "acol_T")
            eng.wait_ge(S("conv_silu"), p.at("conv_silu", 1))
            eng.wait_ge(S("hms"), p.at("hms", 1))
            for h in range(ML_HEADS):
                r = slice(64 * (h % 2), 64 * (h % 2) + 64)
                if h:
                    eng.wait_ge(S("weighted"), p.at("weighted", 2 * h))
                q = big3[r, 16 + h // 2, :]
                k = big3[r, 18 + h // 2, :]
                for a in range(2):
                    mm(ps[:, a, :], k[:, SEQ + a * P:SEQ + a * P + P], q, start=True, stop=True)
                    last = mm(ps[:, 2, a * SEQ:a * SEQ + SEQ], k[:, a * P:a * P + P], q[:, 0:SEQ], start=True, stop=True)
                up(last, "qk_done")
                for d in range(2):
                    j = 2 * h + d
                    if j:
                        eng.wait_ge(S("decay"), p.at("decay", j))
                        eng.wait_ge(S("ebm"), p.at("ebm", j))
                    up(mm(ps[:, 3, :], sel[0:64, 4 * d + h, :], grow[2], start=True, stop=True), "bcast")
                    up(mm(ps[:, 4, :], sel[0:64, 4 * d + h, :], grow[3], start=True, stop=True), "bcast")
                    eng.wait_ge(S("weighted"), p.at("weighted", j + 1))
                    if j:
                        eng.wait_ge(S("mem_done"), p.at("mem_done", j))
                    for a in range(2):
                        both = decay[:, j % 2, a, 1:3, :]
                        mm(ps[:, 5, :], vtok[:, 2 + a, 512 + h * P:512 + h * P + P], both, start=a == 0, stop=False)
                    for a in range(2):
                        mm(ps[:, 5, 0:SEQ], vtok[:, a, 512 + h * P:512 + h * P + P], decay[:, j % 2, a, 0, :], start=False, stop=a == 1)
                    for a in range(2):
                        mm(ps[:, 6, :], onesPP, decay[:, j % 2, a, 1:3, :], start=a == 0, stop=False)
                    for a in range(2):
                        last = mm(ps[:, 6, 0:SEQ], onesPP, decay[:, j % 2, a, 0, :], start=False, stop=a == 1)
                    up(last, "numden")
            head_sums(1)
            eng.wait_ge(S("mix_done"), p.at("mix_done", 2))

        def act_even(eng, p):
            evacuated(eng, p)
            eng.wait_ge(S("lam_e"), p.at("lam_e", 1))
            up(act(small[:, 162:164], small[:, 160:162], ACT.Exp), "lam_ready")
            eng.wait_ge(S("gate_bias"), p.at("gate_bias", 1))
            alink(act(grow[2], grow[1], ACT.Abs))
            alink(act(grow[2], grow[2], ACT.Exp, scale=-1.0))
            up(act(grow[2], grow[2], ACT.Ln, bias=1.0), "gate_ln")

            def exps(i):
                kt = keys2(items2[i][1])[1]
                eng.wait_ge(S("negmax_ready"), p.at("negmax_ready", i + 1))
                for c in range(2):
                    n = 2 * i + c
                    b = 2 * (i % 2) + c
                    up(act(probs[:, b, 0:kt * P], ps[:, b, 0:kt * P], ACT.Exp, bias=nm[:, n:n + 1], scale=HD ** -0.5,
                           accum_out=rsum[:, n:n + 1]), "probs_raw")

            def keep_T(i):
                n = keys2(items2[i][1])[1] * P
                if i >= 2:
                    eng.wait_ge(S("pv_done"), p.at("pv_done", i - 1))
                eng.wait_ge(S("probsT_done"), p.at("probsT_done", i + 1))
                up(act(wT[:, i % 2, 0:n], ps[:, 4 + i % 2, 0:n], ACT.Copy), "probsT_sb")

            for i in range(len(items2)):
                exps(i)
                if i:
                    keep_T(i - 1)
            keep_T(len(items2) - 1)

            def head_roots(n, src, dst):
                up(act(hsq[:, :, :], src, ACT.Square), "hsq")
                eng.wait_ge(S("hms"), p.at("hms", n + 1))
                up(act(dst, dst, ACT.Sqrt), "hrms")

            eng.wait_ge(S("att_evac"), p.at("att_evac", 8))
            head_roots(0, big3[:, 20:24, :], mixT[:, 0:4, :])
            eng.wait_ge(S("conv_lin"), p.at("conv_lin", 1))
            up(act(big3[:, 16:20, :], big3[:, 16:20, :], ACT.Silu), "conv_silu")
            up(act(big3[:, 12:16, :], big3[:, 12:16, :], ACT.Sigmoid), "osig")
            eng.wait_ge(S("acol_T"), p.at("acol_T", 1))
            alink(act(acol, ps[:, 7, 0:4 * 64], ACT.Copy))
            for h in range(ML_HEADS):
                for d in range(2):
                    j = 2 * h + d

                    def a_of(tile):
                        at = tile * 64 + 32 * d + h
                        return acol[:, at:at + 1]

                    eng.wait_ge(S("bcast"), p.at("bcast", 2 * j + 2))
                    if j:
                        eng.wait_ge(S("mem_done"), p.at("mem_done", j))
                    up(act(ebm, ps[:, 4, :], ACT.Exp, scale=-1.0), "ebm")
                    eng.wait_ge(S("args"), p.at("args", j + 1))
                    if j >= 2:
                        eng.wait_ge(S("numden"), p.at("numden", j - 1))
                    for a in range(2):
                        act(decay[:, j % 2, a, 0, :], dargs[:, a, 0, :], ACT.Exp, bias=a_of(a))
                        act(decay[:, j % 2, a, 1, :], ps[:, 3, 0:SEQ], ACT.Exp, bias=a_of(2 + a), scale=-1.0)
                        last = act(decay[:, j % 2, a, 2, :], dargs[:, a, 1, :], ACT.Exp, bias=a_of(2 + a))
                    up(last, "decay")
                    eng.wait_ge(S("numden"), p.at("numden", j + 1))
                    up(act(dnm, ps[:, 6, :], ACT.Abs), "den_abs")
            eng.wait_ge(S("mem_done"), p.at("mem_done", 8))
            head_roots(1, big3[:, 0:4, :], mixT[:, 4:8, :])

        def dve_even(eng, p):
            evacuated(eng, p)
            eng.wait_ge(S("gate_rows"), p.at("gate_rows", 2))
            V.tensor_scalar(grow[0], ps[0:64, 6, :], gateb[:, 0:1], None, ALU.add)
            up(V.tensor_scalar(grow[1], ps[0:64, 7, :], gateb[:, 1:2], None, ALU.add), "gate_bias")
            rotary(big3[:, 0:8], 8, mixT[:, 0:4, :].rearrange("p c n -> p (c n)"), "roped2")
            for i in range(2):
                link(V.tensor_tensor(dlam[:, 128 * i:128 * i + 64], dlam[:, 128 * i:128 * i + 64], dlam[:, 128 * i + 64:128 * i + 128], ALU.mult))
                ins = V.reduce_sum(small[:, 160 + i:161 + i], dlam[:, 128 * i:128 * i + 64], AX.X)
                link(ins) if i == 0 else up(ins, "lam_e")
            eng.wait_ge(S("lam_ready"), p.at("lam_ready", 1))
            link(V.scalar_tensor_tensor(small[:, 164:165], small[:, 163:164], -LAM_INIT, small[:, 162:163], ALU.add, ALU.subtract))
            link(V.tensor_scalar(small[:, 165:166], cols2[:, DIFF_G:DIFF_G + 1], 1.0 - LAM_INIT, None, ALU.mult))

            def maxima(i):
                kt = keys2(items2[i][1])[1]
                for c in range(2):
                    n = 2 * i + c
                    eng.wait_ge(S("scores_ready"), p.at("scores_ready", n + 1))
                    link(V.reduce_max(nmx[:, n:n + 1], ps[:, 2 * (i % 2) + c, 0:kt * P], AX.X, negate=True))
                up(V.tensor_scalar(nm[:, 2 * i:2 * i + 2], nmx[:, 2 * i:2 * i + 2], HD ** -0.5, None, ALU.mult), "negmax_ready")

            def combine(i):
                kt = keys2(items2[i][1])[1]
                n, b = 2 * i, 2 * (i % 2)
                eng.wait_ge(S("probs_raw"), p.at("probs_raw", n + 2))
                link(V.reciprocal(esink[:, n:n + 2], rsum[:, n:n + 2]))
                link(V.tensor_tensor(esink[:, n + 1:n + 2], esink[:, n + 1:n + 2], small[:, 164:165], ALU.mult))
                p0, p1 = probs[:, b, 0:kt * P], probs[:, b + 1, 0:kt * P]
                link(V.tensor_scalar(p0, p0, esink[:, n:n + 1], None, ALU.mult))
                up(V.scalar_tensor_tensor(p0, p1, esink[:, n + 1:n + 2], p0, ALU.mult, ALU.add), "probs_ready")

            def keep(g):
                eng.wait_ge(S("pv_done"), p.at("pv_done", 2 * g + 2))
                up(V.tensor_copy(big3[:, 20 + g // 2, (g % 2) * SEQ:(g % 2) * SEQ + SEQ], ps[:, 6 + g % 2, 0:SEQ]), "att_evac")

            maxima(0)
            for i in range(len(items2)):
                if i + 1 < len(items2):
                    maxima(i + 1)
                combine(i)
                if i >= 3 and i % 2:
                    keep((i - 3) // 2)
            keep(len(items2) // 2 - 1)

            for c in range(4):
                conv3(big3[:, 16 + c, :], big3[:, 8 + c, :], lambda tap: cols2[:, MCONV_W + tap * 4 + c:MCONV_W + tap * 4 + c + 1],
                      cols2[:, MCONV_B + c:MCONV_B + c + 1], NT, "conv_lin" if c == 3 else None)

            def head_norm(n, src, g, dst):
                eng.wait_ge(S("hsum"), p.at("hsum", n + 1))
                up(V.tensor_scalar(dst, ps[:, 0:4, :], 1.0 / P, EPS, ALU.mult, ALU.add), "hms")
                eng.wait_ge(S("hrms"), p.at("hrms", n + 1))
                link(V.reciprocal(dst, dst))
                for h in range(4):
                    ins = V.scalar_tensor_tensor(dst[:, h, :], src[:, h, :], g(h), dst[:, h, :], ALU.mult, ALU.mult)
                return ins

            up(head_norm(0, big3[:, 20:24, :], lambda h: small[:, 165:166], mixT[:, 0:4, :]), "mix_done")

            f, b, a, m = grow[1], grow[3], grow[0], grow[2]
            eng.wait_ge(S("gate_ln"), p.at("gate_ln", 1))
            link(V.scalar_tensor_tensor(f, f, 0.0, grow[2], ALU.min, ALU.subtract))

            def scan(dst, data, op0, op1, first):
                fw, bw = slice(0, 32), slice(32, 64)
                link(V.tensor_tensor_scan(dst[fw, SEQ:NT], first(fw, SEQ, NT), data[fw, SEQ:NT], 0.0, op0, op1))
                link(V.tensor_tensor_scan(dst[fw, 0:SEQ], first(fw, 0, SEQ), data[fw, 0:SEQ], dst[fw, NT - 1:NT], op0, op1))
                link(V.tensor_tensor_scan(dst[bw, SEQ:NT][:, ::-1], first(bw, SEQ, NT)[:, ::-1], data[bw, SEQ:NT][:, ::-1], 0.0, op0, op1))
                link(V.tensor_tensor_scan(dst[bw, 0:SEQ][:, ::-1], first(bw, 0, SEQ)[:, ::-1], data[bw, 0:SEQ][:, ::-1], dst[bw, SEQ:SEQ + 1], op0, op1))

            scan(b, f, ALU.mult, ALU.add, lambda r, s, e: ones[r, 0:SEQ])
            link(V.tensor_tensor(a, a, b, ALU.subtract))
            scan(m, a, ALU.max, ALU.max, lambda r, s, e: a[r, s:e])
            up(V.tensor_tensor(b, b, m, ALU.add), "rows_ready")

            for h in range(ML_HEADS):
                for d in range(2):
                    j = 2 * h + d
                    eng.wait_ge(S("bcast"), p.at("bcast", 2 * j + 1))
                    if j:
                        eng.wait_ge(S("decay"), p.at("decay", j))
                    mrow = ps[:, 3, :].rearrange("p (r q) -> p r q", r=2)
                    for t_ in range(2):
                        last = V.scalar_tensor_tensor(dargs[:, t_], mrow, -1.0, mmask[:, d, t_].unsqueeze(1).broadcast_to([P, 2, SEQ]),
                                                      ALU.mult, ALU.add)
                    up(last, "args")
                    eng.wait_ge(S("decay"), p.at("decay", j + 1))
                    eng.wait_ge(S("qk_done"), p.at("qk_done", h + 1))
                    for t_ in range(2):
                        w = decay[:, j % 2, t_]
                        V.scalar_tensor_tensor(w[:, 1:3, :], ps[:, t_, :].rearrange("p (r q) -> p r q", r=2), HD ** -0.5, w[:, 1:3, :],
                                               ALU.mult, ALU.mult)
                        last = V.scalar_tensor_tensor(w[:, 0, :], ps[:, 2, t_ * SEQ:t_ * SEQ + SEQ], HD ** -0.5, w[:, 0, :], ALU.mult, ALU.mult)
                    up(last, "weighted")
                    eng.wait_ge(S("den_abs"), p.at("den_abs", j + 1))
                    link(V.tensor_tensor(dnm, dnm, ebm, ALU.max))
                    link(V.reciprocal(dnm, dnm))
                    if d == 0:
                        up(V.tensor_tensor(big3[:, h, :], ps[:, 5, :], dnm, ALU.mult), "mem_done")
                    else:
                        link(V.tensor_tensor(dnm, ps[:, 5, :], dnm, ALU.mult))
                        up(V.tensor_tensor(big3[:, h, :], big3[:, h, :], dnm, ALU.add), "mem_done")
            link(head_norm(1, big3[:, 0:4, :], lambda h: cols2[:, ML_G + h:ML_G + h + 1], mixT[:, 4:8, :]))
            eng.wait_ge(S("osig"), p.at("osig", 1))
            up(V.tensor_tensor(mixT[:, 4:8, :], mixT[:, 4:8, :], big3[:, 12:16, :], ALU.mult), "mix_done")

        lrT = scr[0:64, 0:512]
        ckd = scr[:, 512:2560].rearrange("p (i n) -> p i n", n=SEQ)
        ckdT = scr[:, 2560:4608].rearrange("p (i n) -> p i n", n=SEQ)
        state = scr[:, 4608:6656].rearrange("p (i n) -> p i n", n=SEQ)
        amask = scr[:, 0:2048].rearrange("p (i n) -> p i n", n=SEQ)
        bend, blast, eblast = small[:, 0:8], small[:, 32:64], small[:, 64:96]
        STREAMS = [(d, h) for d in range(2) for h in range(GLA_HEADS)]

        def pe_odd(eng, p):
            evacuated(eng, p)
            for k in range(KC):
                last = mm(ps[0:64, 0, :], wlr[:, k, :], hT[:, k, :], start=k == 0, stop=k == KC - 1)
            up(last, "lr_done")
            eng.wait_ge(S("lr_sb"), p.at("lr_sb", 1))
            for i, (d, h) in enumerate(STREAMS):
                if i >= 4:
                    eng.wait_ge(S("z_sb"), p.at("z_sb", i - 3))
                r = slice(32 * d, 32 * d + 16)
                up(mm(ps[:, 1 + i % 4, :], wgla[r, h * P:h * P + P], lrT[r, :], start=True, stop=True), "z_done")
            eng.wait_ge(S("z_sb"), p.at("z_sb", 8))
            for i, (d, h) in enumerate(STREAMS):
                eng.wait_ge(S("ckd"), p.at("ckd", i + 1))
                if i >= 4:
                    eng.wait_ge(S("ckd_sb"), p.at("ckd_sb", i - 3))
                for a in range(2):
                    last = tr(ps[:, i % 4, a * P:a * P + P], ckd[:, i, a * P:a * P + P], ident)
                up(last, "ckd_T")
            for i, (d, h) in enumerate(STREAMS):
                eng.wait_ge(S("ckd_sb"), p.at("ckd_sb", i + 1))
                if i >= 4:
                    eng.wait_ge(S("st_sb"), p.at("st_sb", i - 3))
                for a in range(2):
                    last = mm(ps[:, 4 + i % 4, 0:SEQ], ckdT[:, i, a * P:a * P + P], vtok[:, 2 + a, h * SEQ:h * SEQ + SEQ], start=a == 0, stop=a == 1)
                up(last, "st_done")
            for i, (d, h) in enumerate(STREAMS):
                eng.wait_ge(S("x_in"), p.at("x_in", i + 1))
                eng.wait_ge(S("xkd_sb"), p.at("xkd_sb", i - 3)) if i >= 4 else eng.wait_ge(S("ckd_sb"), p.at("ckd_sb", 8))
                for a in range(2):
                    last = tr(ps[:, i % 4, a * P:a * P + P], hT[:, i, a * P:a * P + P], ident)
                up(last, "xkd_T")
                eng.wait_ge(S("a_sb"), p.at("a_sb", i - 3)) if i >= 4 else eng.wait_ge(S("st_sb"), p.at("st_sb", 8))
                for a in range(2):
                    last = mm(ps[:, 4 + i % 4, a * P:a * P + P], mixT[:, i, SEQ + a * P:SEQ + a * P + P], mixT[:, i, a * P:a * P + P],
                              start=True, stop=True)
                up(last, "a_done")
            eng.wait_ge(S("xkd_sb"), p.at("xkd_sb", 8))
            eng.wait_ge(S("a_sb"), p.at("a_sb", 8))
            for i, (d, h) in enumerate(STREAMS):
                for half in range(2):
                    for a in range(2):
                        mm(ps[:, h, half * SEQ + a * P:half * SEQ + a * P + P], vtok[:, a, h * SEQ + half * P:h * SEQ + half * P + P],
                           amask[:, i, a * P:a * P + P], start=d + half + a == 0, stop=False, skip_group_check=True)
            for st in range(4):
                for i, (d, h) in enumerate(STREAMS):
                    c = 3 - st if d else st
                    r, a, n = slice(64 * (c % 2), 64 * (c % 2) + 64), c // 2, 8 * st + i
                    if st:
                        eng.wait_ge(S("u_sb"), p.at("u_sb", n - 7))
                    for half in range(2):
                        last = mm(ps[:, h, half * SEQ + c * CHUNK:half * SEQ + c * CHUNK + CHUNK], state[:, i, half * P:half * P + P],
                                  mixT[:, i, c * CHUNK:c * CHUNK + CHUNK], start=False, stop=True, skip_group_check=True)
                    if st < 3:
                        if n >= 4:
                            eng.wait_ge(S("u_sb"), p.at("u_sb", n - 3))
                        up(mm(ps[:, 4 + n % 4, 0:SEQ], hT[r, i, SEQ + a * P:SEQ + a * P + P], vtok[r, a, h * SEQ:h * SEQ + SEQ],
                              start=True, stop=True), "u_done")
            up(last, "o_done")
            for h in range(GLA_HEADS):
                eng.wait_ge(S("hsq"), p.at("hsq", h + 1))
                for half in range(2):
                    last = mm(ps[:, 4 + h, 0:SEQ], onesPP, hT[:, h, half * SEQ:half * SEQ + SEQ], start=half == 0, stop=half == 1)
                up(last, "hsum")
            eng.wait_ge(S("mix_done"), p.at("mix_done", 4))

        def act_odd(eng, p):
            evacuated(eng, p)
            eng.wait_ge(S("lr_done"), p.at("lr_done", 1))
            up(act(lrT, ps[0:64, 0, :], ACT.Copy), "lr_sb")
            up(act(big3[:, 8:16, 0:SEQ], big3[:, 8:16, 0:SEQ], ACT.Silu), "r_silu")
            for d in range(2):
                eng.wait_ge(S("z_sb"), p.at("z_sb", 4 * d + 4))
                z, e = big3[:, 16 + 4 * d:20 + 4 * d, :], hT[:, 4 * d:4 * d + 4, :]
                alink(act(e, z, ACT.Abs))
                alink(act(e, e, ACT.Exp, scale=-1.0))
                up(act(e, e, ACT.Ln, bias=1.0), "la_ln")
            for i in range(8):
                eng.wait_ge(S("cums"), p.at("cums", i + 1))
                up(act(ckd[:, i, :], big3[:, 16 + i, SEQ:NT], ACT.Exp, bias=bend[:, i:i + 1], scale=-1.0 / GLA_TAU), "c_exp")
            for i in range(8):
                eng.wait_ge(S("ckd_T"), p.at("ckd_T", i + 1))
                up(act(ckdT[:, i, :], ps[:, i % 4, 0:SEQ], ACT.Copy), "ckd_sb")
            for i in range(8):
                b = big3[:, 16 + i, 0:SEQ]
                act(mixT[:, i, 0:SEQ], b, ACT.Exp, scale=1.0 / GLA_TAU)
                act(mixT[:, i, SEQ:NT], b, ACT.Exp, scale=-1.0 / GLA_TAU)
                for c in range(4):
                    cols = slice(c * CHUNK, (c + 1) * CHUNK)
                    act(hT[:, i, cols], b[:, cols], ACT.Exp, bias=blast[:, 4 * i + c:4 * i + c + 1], scale=-1.0 / GLA_TAU)
                up(act(eblast[:, 4 * i:4 * i + 4], blast[:, 4 * i:4 * i + 4], ACT.Exp), "x_exp")
            for i in range(8):
                eng.wait_ge(S("xkd_T"), p.at("xkd_T", i + 1))
                up(act(hT[:, i, SEQ:NT], ps[:, i % 4, 0:SEQ], ACT.Copy), "xkd_sb")
            for h in range(GLA_HEADS):
                eng.wait_ge(S("o_sb"), p.at("o_sb", h + 1))
                up(act(hT[:, h, :], big3[:, 4 + h, :], ACT.Square), "hsq")
            for h in range(GLA_HEADS):
                eng.wait_ge(S("hms"), p.at("hms", h + 1))
                up(act(hT[:, 4 + h, 0:SEQ], hT[:, 4 + h, 0:SEQ], ACT.Sqrt), "hrms")

        def dve_odd(eng, p):
            evacuated(eng, p)
            for i in range(8):
                eng.wait_ge(S("z_done"), p.at("z_done", i + 1))
                up(V.tensor_scalar(big3[:, 16 + i, :], ps[:, 1 + i % 4, :], cols2[:, GLA_B + i:GLA_B + i + 1], None, ALU.add), "z_sb")
            for d in range(2):
                eng.wait_ge(S("la_ln"), p.at("la_ln", d + 1))
                z, e = big3[:, 16 + 4 * d:20 + 4 * d, :], hT[:, 4 * d:4 * d + 4, :]
                link(V.scalar_tensor_tensor(z, z, 0.0, e, ALU.min, ALU.subtract))
                for h in range(GLA_HEADS):
                    i = 4 * d + h
                    back = slice(None, None, -1) if d else slice(None)
                    bc, bx = big3[:, 16 + i, SEQ:NT], big3[:, 16 + i, 0:SEQ]
                    V.tensor_tensor_scan(bc[:, back], ones[:, 0:SEQ], bc[:, back], 0.0, ALU.mult, ALU.add)
                    link(V.tensor_tensor_scan(bx[:, back], restart[:, d, :][:, back], bx[:, back], 0.0, ALU.mult, ALU.add))
                    end = bc[:, 0:1] if d else bc[:, SEQ - 1:SEQ]
                    ends = bx.rearrange("p (c k) -> p c k", k=CHUNK)[:, :, 0 if d else CHUNK - 1]
                    V.tensor_scalar(blast[:, 4 * i:4 * i + 4], ends, 1.0 / GLA_TAU, None, ALU.mult)
                    up(V.tensor_scalar(bend[:, i:i + 1], end, 1.0 / GLA_TAU, None, ALU.mult), "cums")
            for i, (d, h) in enumerate(STREAMS):
                eng.wait_ge(S("c_exp"), p.at("c_exp", i + 1))
                up(V.tensor_tensor(ckd[:, i, :], ckd[:, i, :], big3[:, 4 + h, SEQ:NT], ALU.mult), "ckd")
            for i in range(8):
                eng.wait_ge(S("st_done"), p.at("st_done", i + 1))
                up(V.tensor_copy(state[:, i, :], ps[:, 4 + i % 4, 0:SEQ]), "st_sb")
            link(V.memset(amask[:, :, :], 0.0))
            for i, (d, h) in enumerate(STREAMS):
                eng.wait_ge(S("x_exp"), p.at("x_exp", i + 1))
                V.scalar_tensor_tensor(mixT[:, i, 0:SEQ], big3[:, h, 0:SEQ], P ** -0.5, mixT[:, i, 0:SEQ], ALU.mult, ALU.mult)
                V.tensor_tensor(mixT[:, i, SEQ:NT], big3[:, 4 + h, 0:SEQ], mixT[:, i, SEQ:NT], ALU.mult)
                up(V.tensor_tensor(hT[:, i, 0:SEQ], big3[:, 4 + h, 0:SEQ], hT[:, i, 0:SEQ], ALU.mult), "x_in")
            for i, (d, h) in enumerate(STREAMS):
                eng.wait_ge(S("a_done"), p.at("a_done", i + 1))
                up(V.copy_predicated(amask[:, i, :], gmask[:, d, :].bitcast(U32), ps[:, 4 + i % 4, 0:SEQ]), "a_sb")
            for st in range(3):
                for i, (d, h) in enumerate(STREAMS):
                    c, n = 3 - st if d else st, 8 * st + i
                    eng.wait_ge(S("u_done"), p.at("u_done", n + 1))
                    up(V.scalar_tensor_tensor(state[:, i, :], state[:, i, :], eblast[:, 4 * i + c:4 * i + c + 1], ps[:, 4 + n % 4, 0:SEQ],
                                              ALU.mult, ALU.add), "u_sb")
            eng.wait_ge(S("o_done"), p.at("o_done", 1))
            for h in range(GLA_HEADS):
                up(V.tensor_copy(big3[:, 4 + h, :], ps[:, h, :]), "o_sb")
            for h in range(GLA_HEADS):
                eng.wait_ge(S("hsum"), p.at("hsum", h + 1))
                up(V.tensor_scalar(hT[:, 4 + h, 0:SEQ], ps[:, 4 + h, 0:SEQ], 1.0 / (2 * P), EPS, ALU.mult, ALU.add), "hms")
            eng.wait_ge(S("r_silu"), p.at("r_silu", 1))
            for h in range(GLA_HEADS):
                eng.wait_ge(S("hrms"), p.at("hrms", h + 1))
                rs = hT[:, 4 + h, 0:SEQ]
                link(V.reciprocal(rs, rs))
                for half in range(2):
                    o = mixT[:, 2 * h + half, 0:SEQ]
                    link(V.scalar_tensor_tensor(o, big3[:, 4 + h, half * SEQ:half * SEQ + SEQ], cols2[:, GLA_G + half:GLA_G + half + 1], rs,
                                                ALU.mult, ALU.mult))
                    last = V.tensor_tensor(o, o, big3[:, 8 + 2 * h + half, 0:SEQ], ALU.mult)
                up(last, "mix_done")

        def run(eng, stages):
            for p in phases:
                if p.kind in stages:
                    stages[p.kind](eng, p)

        @block.sync
        def _(eng):
            run(eng, {"setup": sp_setup, "load": sp_load, "mod": sp_mod, "gemm": sp_gemm, "store": sp_store})

        @block.tensor
        def _(eng):
            run(eng, {"setup": pe_setup, "load": pe_load, "mod": pe_mod, "norm": pe_norm, "gemm": pe_gemm,
                      "mix1": pe_mix1, "even": pe_even, "odd": pe_odd, "store": pe_store})

        @block.scalar
        def _(eng):
            run(eng, {"setup": act_setup, "load": act_load, "norm": act_norm, "gemm": act_gemm,
                      "mix1": act_mix1, "even": act_even, "odd": act_odd, "store": act_store})

        @block.vector
        def _(eng):
            run(eng, {"setup": dve_setup, "load": dve_load, "mod": dve_mod, "modvec": dve_modvec, "norm": dve_norm,
                      "gemm": dve_gemm, "mix1": dve_mix1, "even": dve_even, "odd": dve_odd, "store": dve_store})

    for name, n in total.items():
        assert seen.get(name, 0) == n, (name, seen.get(name, 0), n)


INPUTS = ["x", "c", "ctx", "c_ctx", "w_mod", "b_mod", "g_pre", "g_post", "w_in", "w_out", "sink", "w_fourier", "conv_w",
          "conv_b", "c_2", "ctx_2", "c_ctx_2", "ada_w_2", "ada_b_2", "norm_g_2", "ffn_w_in_2", "ffn_w_out_2",
          "even_w_in_2", "even_w_out_2", "diff_lambda_2", "diff_norm_g_2", "mlstm_conv_w_2", "mlstm_conv_b_2",
          "mlstm_gate_b_2", "mlstm_norm_g_2", "odd_w_in_2", "odd_w_out_2", "gla_w_gate_2", "gla_b_gate_2",
          "gla_norm_g_2", "final_g_2"]


def dram_views(ap):
    v = dict(ap)
    for n in ("x", "ctx", "ctx_2"):
        v[n] = ap[n][0]
    for n in ("c", "c_2"):
        v[n] = ap[n][0].rearrange("(r p) -> r p", p=P)
    for n in ("c_ctx", "c_ctx_2", "final_g_2"):
        v[n] = ap[n].rearrange("(r p) -> r p", p=P)
    for n in ("g_pre", "g_post", "conv_b", "mlstm_conv_b_2", "diff_norm_g_2", "gla_norm_g_2"):
        v[n] = ap[n].rearrange("l (r p) -> (l r) p", p=P)
    for n in ("norm_g_2", "conv_w", "mlstm_conv_w_2"):
        v[n] = ap[n].rearrange("l s (r p) -> (l s r) p", p=P)
    v["mlstm_norm_g_2"] = ap["mlstm_norm_g_2"][0]
    v["gla_b_gate_2"] = ap["gla_b_gate_2"][0].rearrange("d (r p) -> (d r) p", p=P)
    v["gla_w_gate_2"] = ap["gla_w_gate_2"][0]
    v["sink"] = ap["sink"].rearrange("l h -> (l h)")
    v["diff_lambda_2"] = ap["diff_lambda_2"][0].rearrange("a b -> (a b)")
    v["mlstm_gate_b_2"] = ap["mlstm_gate_b_2"][0].rearrange("a (b o) -> (a b) o", o=1)
    wf = ap["w_fourier"].rearrange("l (c g) p n -> g p (l c) n", g=2)
    v["w_fourier"] = [wf[0], wf[1]]
    return v


def kernel(**inputs):
    import concourse.bacc as bacc
    from concourse.bass_utils import run_bass_kernel_spmd

    nc = bacc.Bacc("TRN2", target_bir_lowering=False, num_devices=1)
    arrays, aps = {}, {}
    for name in INPUTS:
        a = np.ascontiguousarray(inputs[name])
        arrays[f"in_{name}"] = a
        aps[name] = nc.dram_tensor(f"in_{name}", a.shape, mybir.dt.from_np(a.dtype), kind="ExternalInput").ap()
    arrays["in_const"] = np.ascontiguousarray(np.concatenate(list(CONST.values()), axis=1))
    const = nc.dram_tensor("in_const", (P, CONST_W), F32, kind="ExternalInput").ap()
    out = nc.dram_tensor("out_0", (1, SEQ, D), F32, kind="ExternalOutput").ap()
    build_program(nc, dram_views(aps), const, out[0])
    result = run_bass_kernel_spmd(nc, [arrays], core_ids=[0])
    return result.results[0]["out_0"]
```

```python
import math
from contextlib import ExitStack

import numpy as np

import concourse.bass as bass
from concourse import mybir

F32 = mybir.dt.float32
U32 = mybir.dt.uint32
F32R = mybir.dt.float32r
ALU = mybir.AluOpType
ACT = mybir.ActivationFunctionType
AX = mybir.AxisListType

P = 128
D = 1024
KC = D // P
SEQ = 256
CTX = 256
NT = SEQ + CTX
TT = NT // P
DEPTH = 2
EPS = 1e-6
BANK = 512

HD = 64
HEADS = 8
Q_PER_KV = 4
PROJ1 = 2816
D_FF = 2816
FC = D_FF // P
EVEN_IN = 3088
ODD_IN = 3104
DA_HEADS = 4
ML_HEADS = 4
GLA_HEADS = 4
CHUNK = 64
LAM_INIT = 0.8 - 0.6 * math.exp(-0.3 * 0)
GLA_TAU = 16.0

STAGE = 2
RING = 4
LEAD = 2
FH = FC // 2
SEG = 256
NEG = -1.0e30


def shape_constants():
    c = {}
    c["ident"] = np.eye(P, dtype=np.float32)
    freqs = HD // 4
    inv = np.power(np.float32(10000.0), -np.arange(freqs, dtype=np.float32) / np.float32(freqs)).astype(np.float32)
    t = np.arange(SEQ)
    pos = np.stack([t // 64, t % 64]).astype(np.float32)
    rope = np.zeros((P, 2, SEQ), np.float32)
    for p in range(P):
        axis, half, f = (p % 64) // 32, (p % 32) // 16, p % 16
        ang = (pos[axis] * inv[f]).astype(np.float32)
        rope[p, 0] = np.cos(ang)
        rope[p, 1] = np.sin(ang) * (-1.0 if half == 0 else 1.0)
    c["rope"] = rope.reshape(P, 2 * SEQ)
    a64 = 2 * np.pi * (np.outer(np.arange(64), np.arange(64)) % 64) / 64
    dftc = np.zeros((P, 2, P))
    for g in range(2):
        s = slice(64 * g, 64 * g + 64)
        dftc[s, 0, s] = np.cos(a64) / 8
        dftc[s, 1, s] = np.sin(a64) / 8
    c["dftc"] = dftc.reshape(P, 2 * P).astype(np.float32)
    an = 2 * np.pi * (np.outer(np.arange(SEQ), np.arange(SEQ)) % SEQ) / SEQ
    dftn = np.stack([np.cos(an), -np.sin(an)]) / 16
    c["dftn"] = dftn.reshape(2, 2, P, SEQ).transpose(2, 1, 0, 3).reshape(P, 4 * SEQ).astype(np.float32)
    q, k = np.arange(P)[:, None], np.arange(P)[None, :]
    c["wmask"] = np.stack([np.where(k <= q, 0, NEG), np.where(k >= q, 0, NEG)], 1).reshape(P, 2 * P).astype(np.float32)
    m = np.zeros((P, 2, 2, SEQ), np.float32)
    for tile in range(2):
        s = tile * P + np.arange(P)[:, None]
        tq = np.arange(SEQ)[None, :]
        m[:, 0, tile] = np.where(tq >= s, 0, NEG)
        m[:, 1, tile] = np.where(tq <= s, 0, NEG)
    c["mmask"] = m.reshape(P, 4 * SEQ)
    s, tq = np.arange(P)[:, None], np.arange(P)[None, :]
    same = s // CHUNK == tq // CHUNK
    c["gmask"] = np.stack([(tq >= s) & same, (tq <= s) & same], 1).astype(np.float32).reshape(P, 2 * P)
    r = np.ones((P, 2, SEQ), np.float32)
    r[:, 0, 0::CHUNK] = 0
    r[:, 1, CHUNK - 1::CHUNK] = 0
    c["restart"] = r.reshape(P, 2 * SEQ)
    ms = np.zeros((P, 2), np.float32)
    for j in range(4):
        for v in range(2):
            ms[32 * j + v, v] = 1
    c["modsel"] = ms
    return c


CONST = shape_constants()
CONST_COLS = {}
_at = 0
for _n, _a in CONST.items():
    CONST_COLS[_n] = (_at, _a.shape[1])
    _at += _a.shape[1]
CONST_W = _at


class Phase:

    def __init__(self, kind, rises, **kw):
        self.kind, self.rises, self.kw, self.start = kind, rises, kw, {}

    def at(self, name, k=0):
        return self.start.get(name, 0) + k


def gemm_rises(n, per, evac, fed, sumsq):
    r = {"unit_done": n * per, "w_hi": n * per - (0 if fed else LEAD)}
    r["w_ready"] = r["w_hi"]
    for j in range(4):
        r[f"bank_free{j}"] = len(range(j // 2, n, 2)) if evac == "tok" else len(range(j, n, 4))
    if evac == "swiglu":
        r["g_hi_ready"] = r["g_ready"] = n // 2
    if sumsq:
        r["sq_ready"] = r["sq_used"] = n
        r["sums_clear"] = 1
    return r


def plan():
    ph = []

    def add(kind, rises, **kw):
        ph.append(Phase(kind, rises, **kw))

    def gemm(w, col0, n, evac, tok=(0, NT), src="h", ks=(KC,), row0=0, fed=True, sumsq=None, hper=0, **kw):
        per = 2 if evac == "tok" else len(ks)
        r = gemm_rises(n, per, evac, fed, sumsq)
        host = None
        if hper:
            host = dict(queue[0])
            segs = hper * (n // 4)
            queue[0]["seg0"] += segs
            if queue[0]["seg0"] == queue[0]["segs"]:
                queue.pop(0)
            assert not queue or queue[0]["seg0"] < queue[0]["segs"]
            r.update({"mod_rows": segs, "mod_cols": segs, "mod_sum0": segs // 2, "mod_sum1": segs // 2, "mod_kept": segs})
        add("gemm", r, hper=hper, host=host, w=w, col0=col0, n=n, evac=evac, tok=tok, src=src, ks=ks,
            per=per, step=2 if evac == "tok" else 4, row0=row0, fed=fed, sumsq=sumsq, **kw)

    def squares(nt, after):
        add("squares", {"sq_ready": KC, "sq_used": KC, "sums_clear": 1}, nt=nt, after=after)

    def norm(mode, nt, n=0, **kw):
        r = {"ms_sum": 1, "rms_ready": 1, "rstd_ready": 1}
        if mode == "pre":
            r.update({"t_ready": KC, "hi_ready": KC, "h_ready": KC})
        else:
            r["normed"] = KC * (nt // SEQ)
        add("norm", r, mode=mode, nt=nt, n=n, **kw)

    def feed(after=None):
        add("feed", {"w_hi": LEAD, "w_ready": LEAD}, after=after)

    def mixsplit(nt, after):
        feed(after)
        add("mixsplit", {"hi_ready": KC, "h_ready": KC}, nt=nt)

    queue = [dict(block=b, l=l, seg0=0, segs=(3, 9)[b] * D // SEG) for b in range(2) for l in range(DEPTH)]

    def mod():
        m = queue.pop(0)
        segs = m["segs"]
        add("mod", {"mod_rows": segs, "mod_cols": segs, "mod_sum0": segs // 2, "mod_sum1": segs // 2,
                    "mod_kept": segs}, host=None, **m)

    def modvec(block, l, parts=(0,)):
        add("modvec", {"mod_ready": 1}, block=block, l=l, parts=parts)

    add("setup", {"rows_T": 2, "rows_sb": 2, "s_ready": 2})
    add("load", {"tokens_T": 8, **{f"bank_free{b}": 1 for b in range(8)}}, which=0)
    squares(NT, "load")
    for l in range(DEPTH):
        both = l < DEPTH - 1
        nt = NT if both else SEQ
        if l == 0:
            mod()
            feed()
        modvec(0, l)
        norm("pre", NT, block=0, l=l, n=0)
        if both:
            gemm(("w_in", l), 0, 4, "copy", dst=0)
            gemm(("w_in", l), 512, 18, "copy", dst=4, fed=False, hper=2)
        else:
            gemm(("w_in", l), 0, 4, "copy", tok=(0, nt), dst=0)
            add("fetch", {})
            gemm(("w_in", l), 512, 2, "copy", dst=4)
            gemm(("w_in", l), 768, 16, "copy", tok=(0, nt), dst=6, fed=False, hper=2)
        na = 16 if both else 8
        add("mix1", {"v_T": 1, "v_sb": 1, "k_swapped": 1, "roped": 1, "gates_done": 1, "scores_ready": 2 * na, "negmax_ready": 2 * na,
                     "probs_raw": 2 * na, "probs_ready": 2 * na, "probsT_done": 2 * na, "probsT_sb": 2 * na,
                     "pv_done": na, "att_gated": na // 2, "dft1": na // 4, "dft1_sb": na // 4, "dft2": 2, "dft2_sb": 2,
                     "dft3": 2, "dft3_gated": 2, "conv_done": 1}, l=l, both=both)
        mixsplit(nt, "att_gated")
        gemm(("w_out", l), 0, 8, "copy", tok=(0, nt), dst=0, sumsq="big", hper=2)
        norm("post", nt, block=0, l=l)
        if both:
            squares(nt, "post")
    add("load", {"tokens_T": 8, **{f"bank_free{b}": 1 for b in range(8)}}, which=1)
    squares(NT, "load")
    for l in range(DEPTH):
        last = l == DEPTH - 1
        modvec(1, l, (0,) if l == 0 else (0, 1, 2))

        def ffn(i, nt, hpers):
            norm("pre", nt, block=1, l=l, n=2 * i)
            for half in range(2):
                gemm(("ffn_w_in_2", l, i), half * FH * P, 2 * FH, "swiglu", tok=(0, nt), hper=hpers[2 * half])
                gemm(("ffn_w_out_2", l, i), 0, KC, "resid", tok=(0, nt), src="g", ks=(6, 5), row0=half * FH, l=l, g=2 * i,
                     sumsq="resid" if half else None, fed=not (last and i and half), hper=hpers[2 * half + 1])

        if l == 0:
            ffn(0, NT, (2, 2, 2, 0))
            modvec(1, 0, (1, 2))
        else:
            ffn(0, NT, (0, 0, 0, 0))
        norm("pre", NT, block=1, l=l, n=1)
        w = ("even_w_in_2", 0) if l == 0 else ("odd_w_in_2", 0)
        if l == 0:
            gemm(w, 0, 8, "copy", dst=0)
            gemm(w, 1024, 2, "tok", dst=0)
            gemm(w, 1536, 4, "copy", dst=8)
            gemm(w, 2048, 2, "tok", dst=512)
            gemm(w, 2560, 4, "copy", dst=12, fed=False)
            add("even", {"roped2": 1, "lam_e": 1, "lam_ready": 1, "gate_rows": 1, "gate_bias": 1, "gate_ln": 1, "rows_ready": 1,
                         "scores_ready": 32, "negmax_ready": 16,
                         "probs_raw": 32, "probs_ready": 16, "probsT_done": 16, "probsT_sb": 16, "pv_done": 16, "att_evac": 8,
                         "conv_lin": 1, "conv_silu": 1, "acol_T": 1,
                         "qk_done": 4, "bcast": 16, "ebm": 8, "args": 8, "decay": 8, "weighted": 8,
                         "numden": 8, "den_abs": 8, "mem_done": 8,
                         "hsq": 2, "hsum": 2, "hms": 2, "hrms": 2, "osig": 1, "mix_done": 2}, l=l)
            mixsplit(NT, "mix_done")
            gemm(("even_w_out_2", 0), 0, 8, "resid", l=l, g=1, sumsq="resid")
        else:
            gemm(w, 0, 4, "copy", tok=(0, SEQ), dst=0)
            gemm(w, 512, 4, "copy", dst=4)
            gemm(w, 1024, 4, "tok", dst=0)
            gemm(w, 2048, 8, "copy", tok=(0, SEQ), dst=8, fed=False)
            add("odd", {"lr_done": 1, "lr_sb": 1, "z_done": 8, "z_sb": 8, "la_ln": 2, "cums": 8,
                        "c_exp": 8, "ckd": 8, "ckd_T": 8, "ckd_sb": 8, "st_done": 8, "st_sb": 8,
                        "x_exp": 8, "x_in": 8, "xkd_T": 8, "xkd_sb": 8, "a_done": 8, "a_sb": 8,
                        "u_done": 24, "u_sb": 24, "o_done": 1, "o_sb": 4, "r_silu": 1, "hsq": 4, "hsum": 4, "hms": 4, "hrms": 4,
                        "mix_done": 4}, l=l)
            mixsplit(SEQ, "mix_done")
            gemm(("odd_w_out_2", 0), 0, 8, "resid", tok=(0, SEQ), l=l, g=1, sumsq="resid")
        ffn(1, SEQ if last else NT, (0, 0, 0, 0) if last else (2, 4, 2, 4))
    norm("final", SEQ)
    add("store", {"out_T": 4, "out_sb": 4})
    total = {}
    for p in ph:
        p.start = dict(total)
        for k, v in p.rises.items():
            total[k] = total.get(k, 0) + v
    return ph, total


def build_program(nc, t, const, out):
    phases, total = plan()
    seen = {}
    with ExitStack() as stack:
        def sb(name, shape, dt=F32):
            return stack.enter_context(nc.sbuf_tensor(name, shape, dt))

        sizes = {"resid": KC * NT, "big": 24 * NT, "hT": KC * NT, "mixT": KC * NT, "vtok": TT * D, "stage": STAGE * KC * P,
                 "scr": 2 * RING * KC * P, "modw": 2 * KC * SEG}
        base_of = {}
        end = -(-nc.sbuf_base // 32) * 32
        for name, n in sizes.items():
            base_of[name] = end
            end += 4 * n
        sb("stretch", [P, sum(sizes.values())])

        def over(name, base, at, shape, dt=F32):
            return nc.alloc_sbuf_tensor_at(name, shape, dt, offset=base_of[base] + 4 * at)

        resid = over("resid", "resid", 0, [P, KC, NT])
        big = over("big", "big", 0, [P, 24 * NT])
        big3 = big[:, :].rearrange("p (c n) -> p c n", n=NT)
        vtok = over("vtok", "vtok", 0, [P, TT, D])
        hT = over("hT", "hT", 0, [P, KC, NT])
        mixT = over("mixT", "mixT", 0, [P, KC, NT])
        stage = over("stage", "stage", 0, [P, STAGE, KC, P])
        scr = over("scr", "scr", 0, [P, 2 * RING * KC * P])
        modw = over("modw", "modw", 0, [P, 2, KC, SEG])

        h_hi = over("h_hi", "hT", 0, [P, KC, NT], F32R)
        h_lo = over("h_lo", "mixT", 0, [P, KC, NT], F32R)
        g_hi = over("g_hi", "big", 0, [P, 12, NT], F32R)
        g_lo = over("g_lo", "big", 12 * NT, [P, 12, NT], F32R)
        w_hi = over("w_hi", "scr", 0, [P, RING, KC, P], F32R)
        w_lo = over("w_lo", "scr", 4096, [P, RING, KC, P], F32R)
        modb = sb("modb", [P, 2, SEG])
        modr = sb("modr", [P, 2, SEG])
        cst = sb("cst", [P, CONST_W])
        rows1 = sb("rows1", [120, P])
        rows2 = sb("rows2", [47, P])
        cols1 = sb("cols1", [P, 120])
        cols2 = sb("cols2", [P, 47])
        svec = sb("svec", [P, 2, KC, 32])
        modT = [sb(f"modT{i}", [P, 24 if i < 2 else 72, 2]) for i in range(4)]
        modA = [sb(f"modA{i}", [P, 2 if i < 2 else 6, KC, 2]) for i in range(4)]
        work = vtok[:, :, :].rearrange("p a d -> p (a d)")
        sq = work[:, 0:1024].rearrange("p (s n) -> p s n", n=NT)
        sqsum, rms, rstd = work[:, 1024:1536], work[:, 1536:2048], work[:, 2048:2560]
        sg = work[:, 2560:3584].rearrange("p (s n) -> p s n", n=NT)
        gt = work[:, 3584:4096]
        tnorm = work[:, 2560:4096].rearrange("p (s n) -> p s n", n=NT)
        epsc = sb("epsc", [P, 1])
        ones = sb("ones", [P, SEQ])
        wfbd = sb("wfbd", [P, 4, P])
        sinkb = sb("sinkb", [P, DEPTH * HEADS])
        nsink = sb("nsink", [P, DEPTH * HEADS])
        dlam = sb("dlam", [P, 4 * HD])
        small = sb("small", [P, 192])
        wgate = sb("wgate", [P, KC, P])
        gateb = sb("gateb", [64, 2])
        wlr = sb("wlr", [P, KC, 64])
        wgla = sb("wgla", [64, GLA_HEADS * P])
        ps = stack.enter_context(nc.psum_tensor("ps", [P, 8, BANK], F32))

        sems = {}

        def S(name):
            if name not in sems:
                sems[name] = stack.enter_context(nc.semaphore(name))
            return sems[name]

        def up(ins, name, times=1, by=1):
            seen[name] = seen.get(name, 0) + times * by
            return ins.then_inc(S(name), by)

        def C(name):
            a, n = CONST_COLS[name]
            return cst[:, a:a + n]

        for n in list(total) + ["consts_in", "tokens_in", "zeroed", "eps_set", "dve_chain", "act_chain", "out_written"]:
            S(n)
        w_full = [S(f"w_full{s}") for s in range(STAGE)]
        mod_full = [S(f"mod_full{s}") for s in range(2)]
        ident = C("ident")
        ropeC, ropeS = C("rope")[:, 0:SEQ], C("rope")[:, SEQ:2 * SEQ]
        dftn = C("dftn").rearrange("p (t c n) -> p t c n", t=2, c=2)
        wmask = C("wmask").rearrange("p (t k) -> p t k", t=2)
        mmask = C("mmask").rearrange("p (d t k) -> p d t k", d=2, t=2)
        gmask = C("gmask").rearrange("p (d k) -> p d k", d=2)
        restart = C("restart").rearrange("p (d k) -> p d k", d=2)
        onesPP = ones[:, 0:P]
        xstage = vtok[:, :, :]

        G_PRE, G_POST, NORM_G, FINAL_G = 32, 48, 64, 112
        CONV_W, CONV_B, MCONV_W, MCONV_B, DIFF_G, ML_G, GLA_G, GLA_B = 0, 12, 16, 28, 32, 33, 37, 39
        SWAP16 = [i ^ 16 for i in range(32)]

        block = stack.enter_context(nc.Block())

        def weight(key):
            w = t[key[0]]
            for i in key[1:]:
                w = w[i]
            return w

        def evacuated(eng, p):
            for b in range(8):
                if p.at(f"bank_free{b}"):
                    eng.wait_ge(S(f"bank_free{b}"), p.at(f"bank_free{b}"))
            for name in ("mod_sum0", "mod_sum1", "mod_kept"):
                if p.at(name):
                    eng.wait_ge(S(name), p.at(name))

        def turns(eng, n, step, peel=False):
            full = n // step
            if peel and n % step == 0:
                full -= 1
            if full > 1:
                with eng.Fori(0, full) as i:
                    yield i, range(step), full
            elif full == 1:
                yield 0, range(step), 1
            if n - full * step:
                yield full, range(n - full * step), 1

        def pairs(eng, segs):
            yield 0, 1
            with eng.Fori(1, segs // 2) as i:
                yield i, segs // 2 - 1

        def hosted(p, j, js):
            k = p.kw
            every = k["step"] // k["hper"] if k["hper"] else 0
            return j // every if every and len(js) == k["step"] and j % every == 0 else None

        def splits(p, i, j, rounds):
            k = p.kw
            for s in range(k["per"]):
                x = j * k["per"] + s + LEAD
                if rounds > 1 or k["fed"] or i * k["step"] * k["per"] + x < k["n"] * k["per"]:
                    yield x

        def sp_setup(eng, p):
            loads = 0
            k = 0
            for name, n in (("c", 8), ("c_ctx", 8), ("c_2", 8), ("c_ctx_2", 8), ("g_pre", 16), ("g_post", 16),
                            ("norm_g_2", 48), ("final_g_2", 8)):
                eng.dma_start(rows1[k:k + n, :], t[name]).then_inc(S("consts_in"), 16)
                k += n
                loads += 1
            k = 0
            for name, n in (("conv_w", 12), ("conv_b", 4), ("mlstm_conv_w_2", 12), ("mlstm_conv_b_2", 4),
                            ("diff_norm_g_2", 1), ("mlstm_norm_g_2", 4), ("gla_norm_g_2", 2), ("gla_b_gate_2", 8)):
                eng.dma_start(rows2[k:k + n, :], t[name]).then_inc(S("consts_in"), 16)
                k += n
                loads += 1
            eng.dma_start(cst[:, :], const).then_inc(S("consts_in"), 16)
            eng.dma_start(sinkb[:, :], t["sink"].partition_broadcast(P)).then_inc(S("consts_in"), 16)
            eng.dma_start(dlam[:, :], t["diff_lambda_2"].partition_broadcast(P)).then_inc(S("consts_in"), 16)
            loads += 3
            eng.wait_ge(S("zeroed"), 6)
            for g in range(2):
                eng.dma_start(wfbd[64 * g:64 * g + 64, :, 64 * g:64 * g + 64], t["w_fourier"][g]).then_inc(S("consts_in"), 16)
            evw = t["even_w_in_2"][0].rearrange("(k p) n -> p k n", p=P)
            for g in range(2):
                for d in range(2):
                    at = 3072 + 8 * g + 4 * d
                    eng.dma_start(wgate[:, :, 64 * g + 32 * d:64 * g + 32 * d + 4], evw[:, :, at:at + 4],
                                  allow_slow_non_contiguous=True).then_inc(S("consts_in"), 16)
                    eng.dma_start(gateb[32 * d:32 * d + 4, g:g + 1], t["mlstm_gate_b_2"][8 * g + 4 * d:8 * g + 4 * d + 4, :],
                                  allow_slow_non_contiguous=True).then_inc(S("consts_in"), 16)
            odw = t["odd_w_in_2"][0].rearrange("(k p) n -> p k n", p=P)
            for d in range(2):
                eng.dma_start(wlr[:, :, 32 * d:32 * d + 16], odw[:, :, 3072 + 16 * d:3088 + 16 * d]).then_inc(S("consts_in"), 16)
                eng.dma_start(wgla[32 * d:32 * d + 16, :], t["gla_w_gate_2"][d]).then_inc(S("consts_in"), 16)
            loads += 2 + 8 + 4
            assert loads == CONST_LOADS

        CONST_LOADS = 33

        def sp_load(eng, p):
            if p.kw["which"] == 0:
                for i, n in enumerate(("x", "ctx")):
                    eng.dma_start(xstage[:, 2 * i:2 * i + 2, :], t[n].rearrange("(a p) d -> p a d", p=P)).then_inc(S("tokens_in"), 16)

        def sp_segment(eng, p, i, per_turn, x):
            m = p.kw["host"] or p.kw
            blk, l = m["block"], m["l"]
            w = (t["w_mod"], t["ada_w_2"])[blk][l].rearrange("(k p) n -> p k n", p=P)
            b = (t["b_mod"], t["ada_b_2"])[blk]
            par = x % 2
            cols = bass.ds((i * per_turn + (m["seg0"] + x)) * SEG, SEG)
            before = p.at(f"mod_sum{par}") + x // 2
            if before or not isinstance(i, int):
                eng.wait_ge(S(f"mod_sum{par}"), i * (per_turn // 2) + before)
            eng.dma_start(modw[:, par], w[:, :, cols]).then_inc(mod_full[par], 16)
            eng.dma_start(modb[0:2, par, :], b[l:l + 1, cols].broadcast_to([2, SEG])).then_inc(mod_full[par], 16)

        def sp_mod(eng, p):
            for i, _ in pairs(eng, p.kw["segs"]):
                for x in range(2):
                    sp_segment(eng, p, i, 2, x)

        def sp_fetch(eng, p):
            eng.wait_ge(S("normed"), p.at("normed"))
            for a in range(2):
                eng.dma_start(big3[:, 6 + 4 * a:10 + 4 * a, SEQ:NT], t["ctx_2"][a * P:(a + 1) * P, :]
                              .rearrange("p (c n) -> p c n", n=SEQ)).then_inc(S("tokens_in"), 16)

        def sp_gemm(eng, p):
            k = p.kw
            w, ks, u0, per, step = weight(k["w"]), k["ks"], p.at("unit_done"), k["per"], k["step"]
            w3 = w.rearrange("(k p) n -> p k n", p=P)
            for i, js, _ in turns(eng, k["n"], step):
                for j in js:
                    x = hosted(p, j, js)
                    if x is not None:
                        sp_segment(eng, p, i, k["hper"], x)
                    for s in range(per):
                        u = u0 + j * per + s
                        if u >= STAGE:
                            eng.wait_ge(S("w_ready"), i * (step * per) + (u - STAGE + 1))
                        rows = slice(k["row0"], k["row0"] + KC)
                        if k["evac"] == "swiglu":
                            col = i * (2 * P) + (k["col0"] + (j // 2) * P + (j % 2) * D_FF)
                        elif k["evac"] == "tok":
                            col = i * (4 * P) + (k["col0"] + (2 * j + s) * P)
                        else:
                            col = i * (4 * P) + (k["col0"] + j * P)
                            first = k["row0"] + sum(ks[:s])
                            rows = slice(first, first + ks[s])
                        eng.dma_start(stage[:, u % STAGE, 0:rows.stop - rows.start, :], w3[:, rows, bass.ds(col, P)]).then_inc(w_full[u % STAGE], 16)

        def sp_store(eng, p):
            for tile in range(2):
                for half in range(2):
                    eng.wait_ge(S("out_sb"), 2 * tile + half + 1)
                    eng.dma_start(out[tile * P:(tile + 1) * P, half * 512:half * 512 + 512],
                                  vtok[:, tile, half * 512:half * 512 + 512]).then_inc(S("out_written"), 16)
            eng.wait_ge(S("out_written"), 64)

        mm, tr = nc.tensor.matmul, nc.tensor.transpose

        def pe_setup(eng, p):
            eng.wait_ge(S("consts_in"), 16 * CONST_LOADS)
            up(tr(ps[:, 0, 0:120], rows1[:, :], ident[0:120, 0:120]), "rows_T")
            up(tr(ps[:, 1, 0:47], rows2[:, :], ident[0:47, 0:47]), "rows_T")

        def pe_load(eng, p):
            which = p.kw["which"]
            eng.wait_ge(S("tokens_in"), 32 + 32 * which)
            if which == 0:
                eng.wait_ge(S("rows_sb"), 2)
            else:
                eng.wait_ge(S("normed"), p.at("normed"))
            evacuated(eng, p)
            for c in range(KC):
                tiles = range(4) if which == 0 else (2, 3)
                for a in tiles:
                    if which == 0:
                        tokens = xstage[:, a, c * P:(c + 1) * P]
                    else:
                        tokens = big3[:, 6 + 4 * (a - 2) + c // 2, SEQ + (c % 2) * P:SEQ + (c % 2) * P + P]
                    last = tr(ps[:, c, a * P:(a + 1) * P], tokens, ident)
                up(last, "tokens_T")

        def pe_rows(eng, p, i, per_turn, x, rounds):
            m = p.kw["host"] or p.kw
            par = x % 2
            eng.wait_ge(mod_full[par], i * (16 * per_turn) + (16 * p.at("mod_rows") + 32 * (x // 2) + 32))
            if p.at(f"mod_sum{par}") + x // 2 or not isinstance(i, int):
                eng.wait_ge(S(f"mod_sum{par}"), i * (per_turn // 2) + (p.at(f"mod_sum{par}") + x // 2))
            for k in range(KC):
                j = k % 4
                last = mm(ps[32 * j:32 * j + 32, 4 + par, 0:SEG], svec[:, m["block"], k, :], modw[:, par, k, :], start=k < 4, stop=k >= 4)
            up(last, "mod_rows", rounds)

        def pe_cols(eng, p, i, per_turn, x, rounds):
            par = x % 2
            eng.wait_ge(S(f"mod_sum{par}"), i * (per_turn // 2) + (p.at(f"mod_sum{par}") + x // 2 + 1))
            if p.at("mod_kept") + x or not isinstance(i, int):
                eng.wait_ge(S("mod_kept"), i * per_turn + (p.at("mod_kept") + x))
            for c in range(2):
                last = mm(ps[:, 6, 2 * c:2 * c + 2], modr[:, par, c * P:(c + 1) * P], C("modsel"), start=True, stop=True)
            up(last, "mod_cols", rounds)

        def pe_mod(eng, p):
            segs = p.kw["segs"]
            eng.wait_ge(S("s_ready"), 2)
            evacuated(eng, p)
            for i, rounds in pairs(eng, segs):
                for x in range(2):
                    pe_rows(eng, p, i, 2, x, rounds)
                for x in range(2):
                    pe_cols(eng, p, i, 2, x, rounds)

        def pe_norm(eng, p):
            nt = p.kw["nt"]
            eng.wait_ge(S("sq_used"), p.at("sq_used"))
            if p.at("rms_ready"):
                eng.wait_ge(S("rms_ready"), p.at("rms_ready"))
            up(mm(ps[:, 7, 0:nt], onesPP, sqsum[:, 0:nt], start=True, stop=True), "ms_sum")

        W_X = (("hi", "hi"), ("hi", "lo"), ("lo", "hi"))

        def pe_gemm(eng, p):
            k = p.kw
            a, b = k["tok"]
            ks, u0, per, step, evac = k["ks"], p.at("unit_done"), k["per"], k["step"], k["evac"]
            w_part = {"hi": w_hi, "lo": w_lo}
            x_part = {"hi": h_hi, "lo": h_lo} if k["src"] == "h" else {"hi": g_hi, "lo": g_lo}
            x_ready, x_chunks = ("h_ready", KC) if k["src"] == "h" else ("g_ready", FH)
            def weights(i, u):
                eng.wait_ge(S("w_ready"), i * (step * per) + (u + 1))

            def operand(x):
                eng.wait_ge(S(x_ready), p.at(x_ready) - x_chunks + x + 1)

            def chunk(j, u, c, x):
                for wp, xp in W_X:
                    last = mm(ps[:, j, 0:b - a], w_part[wp][:, u % RING, c, :], x_part[xp][:, x, a:b],
                              start=x == 0 and wp == xp, stop=x == sum(ks) - 1 and wp == "lo")
                return last

            def product(i, j, rounds):
                for s, kc in enumerate(ks):
                    u = u0 + j * per + s
                    weights(i, u)
                    if s == 0:
                        eng.wait_ge(S(f"bank_free{j}"), p.at(f"bank_free{j}") + i)
                    for c in range(kc):
                        x = sum(ks[:s]) + c
                        if j == 0:
                            operand(x)
                        last = chunk(j, u, c, x)
                    up(last, "unit_done", rounds)

            def product_pair(i, rounds):
                for j in range(2):
                    weights(i, u0 + j)
                    eng.wait_ge(S(f"bank_free{j}"), p.at(f"bank_free{j}") + i)
                for x in range(KC):
                    operand(x)
                    for j in range(2):
                        last = chunk(j, u0 + j, x, x)
                        if x == KC - 1:
                            up(last, "unit_done", rounds)

            def token_pair(i, j, rounds):
                u = u0 + 2 * j
                weights(i, u)
                weights(i, u + 1)
                operand(KC - 1)
                for tile in range(TT):
                    bank = 2 * j + tile // 2
                    if tile % 2 == 0:
                        eng.wait_ge(S(f"bank_free{bank}"), p.at(f"bank_free{bank}") + i)
                    for c in range(KC):
                        for wp, xp in W_X:
                            last = mm(ps[:, bank, (tile % 2) * SEQ:(tile % 2) * SEQ + SEQ], x_part[xp][:, c, tile * P:(tile + 1) * P],
                                      w_part[wp][:, u % RING:u % RING + 2, c, :], start=c == 0 and wp == xp, stop=c == KC - 1 and wp == "lo")
                up(last, "unit_done", rounds, by=2)

            for i, js, rounds in turns(eng, k["n"], step):
                paired = evac != "tok" and per == 1 and len(js) >= 2
                for j in js:
                    x = hosted(p, j, js)
                    if x is not None:
                        pe_rows(eng, p, i, k["hper"], x, rounds)
                    if evac == "tok":
                        token_pair(i, j, rounds)
                    elif paired and j < 2:
                        if j == 0:
                            product_pair(i, rounds)
                    else:
                        product(i, j, rounds)
                    if x is not None:
                        pe_cols(eng, p, i, k["hper"], x, rounds)

        def pe_store(eng, p):
            eng.wait_ge(S("normed"), p.at("normed"))
            for tile in range(2):
                for half in range(2):
                    for c in range(4):
                        last = tr(ps[:, 2 * tile + half, c * P:(c + 1) * P], hT[:, half * 4 + c, tile * P:(tile + 1) * P], ident)
                    up(last, "out_T")

        chain = {"dve": 0, "act": 0}
        act = nc.scalar.activation

        def alink(ins):
            chain["act"] += 1
            ins.then_inc(S("act_chain"), 1)
            nc.scalar.wait_ge(S("act_chain"), chain["act"])

        def act_setup(eng, p):
            eng.wait_ge(S("zeroed"), 6)
            eng.wait_ge(S("eps_set"), 1)
            eng.wait_ge(S("rows_sb"), 2)
            for blk in range(2):
                up(act(svec[:, blk, :, 0:2], cols1[:, 16 * blk:16 * blk + 16].rearrange("p (v k) -> p k v", v=2), ACT.Silu), "s_ready")

        def act_load(eng, p):
            a = 0 if p.kw["which"] == 0 else SEQ
            for c in range(1, KC, 2):
                eng.wait_ge(S("tokens_T"), p.at("tokens_T", c + 1))
                up(act(resid[:, c, a:NT], ps[:, c, a:NT], ACT.Copy), f"bank_free{c}")

        def act_squares(eng, p):
            nt = p.kw["nt"]
            if p.kw["after"] == "load":
                eng.wait_ge(S("tokens_T"), p.at("tokens_T"))
            if p.kw["after"] == "post" or p.at("normed"):
                eng.wait_ge(S("normed"), p.at("normed") - (KC * (nt // SEQ) if p.kw["after"] == "post" else 0))
            for c in range(KC):
                if p.kw["after"] == "load":
                    eng.wait_ge(S(f"bank_free{c}"), p.at(f"bank_free{c}"))
                else:
                    eng.wait_ge(S("normed"), p.at("normed") + (c + 1 - KC) * (nt // SEQ))
                act_square(eng, p, resid[:, c, 0:nt], 0, c, 1)

        def act_square(eng, p, src, i, j, rounds):
            if p.at("sq_used") + j >= 2:
                eng.wait_ge(S("sq_used"), i * 4 + (p.at("sq_used") + j - 1))
            up(act(sq[:, j % 2, 0:src.shape[-1]], src, ACT.Square), "sq_ready", rounds)

        def act_norm(eng, p):
            nt, mode = p.kw["nt"], p.kw["mode"]
            eng.wait_ge(S("ms_sum"), p.at("ms_sum", 1))
            if p.at("rstd_ready"):
                eng.wait_ge(S("rstd_ready"), p.at("rstd_ready"))
            up(act(rms[:, 0:nt], ps[:, 7, 0:nt], ACT.Sqrt, scale=1.0 / D, bias=epsc[:, :]), "rms_ready")
            if mode == "pre":
                m = 2 * p.kw["block"] + p.kw["l"]
                for c in range(KC):
                    eng.wait_ge(S("t_ready"), p.at("t_ready", c + 1))
                    for v in range(nt // SEQ):
                        sh = modT[m][:, p.kw["n"] * 24 + c, v:v + 1]
                        cols = slice(v * SEQ, (v + 1) * SEQ)
                        last = act(h_hi[:, c, cols], tnorm[:, c % 3, cols], ACT.Identity, bias=sh, scale=1.0)
                    up(last, "hi_ready")

        def act_split(eng, u, i=0, turn=0, rounds=1):
            eng.wait_ge(w_full[u % STAGE], i * (16 * turn // STAGE) + (16 * (u // STAGE) + 16))
            if u >= RING:
                eng.wait_ge(S("unit_done"), i * turn + (u - RING + 1))
            up(act(w_hi[:, u % RING], stage[:, u % STAGE], ACT.Copy), "w_hi", rounds)

        def act_feed(eng, p):
            if p.kw["after"]:
                eng.wait_ge(S(p.kw["after"]), p.at(p.kw["after"]))
            for s in range(LEAD):
                act_split(eng, p.at("unit_done") + s)

        def act_mixsplit(eng, p):
            for c in range(KC):
                up(act(h_hi[:, c, 0:p.kw["nt"]], mixT[:, c, 0:p.kw["nt"]], ACT.Copy), "hi_ready")

        def act_gemm(eng, p):
            k = p.kw
            a, b = k["tok"]
            n = b - a
            u0, per, step, evac = p.at("unit_done"), k["per"], k["step"], k["evac"]
            turn = per * step
            for i, js, rounds in turns(eng, k["n"], step, peel=not k["fed"]):
                for j in js:
                    for x in splits(p, i, j, rounds):
                        act_split(eng, u0 + x, i, turn, rounds)
                    if evac == "swiglu" and j % 2 == 0:
                        eng.wait_ge(S("unit_done"), i * turn + (u0 + j + 1))
                        eng.wait_ge(S(f"bank_free{j + 1}"), p.at(f"bank_free{j + 1}") + i)
                        up(act(sg[:, j // 2, 0:n], ps[:, j, 0:n], ACT.Silu), f"bank_free{j}", rounds)
                    elif evac == "tok":
                        eng.wait_ge(S("unit_done"), i * turn + (u0 + 2 * j + 2))
                        up(act(tok_dst(k, i, j, 0), tok_out(j, 0), ACT.Copy), f"bank_free{2 * j}", rounds)
                    elif evac == "copy" and j % 2 and not k["sumsq"]:
                        eng.wait_ge(S("unit_done"), i * turn + (u0 + j + 1))
                        up(act(gemm_dst(k, i, j, n), ps[:, j, 0:n], ACT.Copy), f"bank_free{j}", rounds)
                    if k["sumsq"]:
                        eng.wait_ge(S(f"bank_free{j}"), p.at(f"bank_free{j}") + i + 1)
                        src = big[:, :] if k["sumsq"] == "big" else resid[:, :, :].rearrange("p c n -> p (c n)")
                        act_square(eng, p, src[:, bass.ds(i * (4 * NT) + j * NT, n)], i, j, rounds)

        def tok_out(j, half):
            return ps[:, 2 * j + half, :].rearrange("p (a n) -> p a n", n=SEQ)

        def tok_dst(k, i, j, half):
            return vtok[:, 2 * half:2 * half + 2, bass.ds(i * (2 * SEQ) + (k["dst"] + j * SEQ), SEQ)]

        def gemm_dst(k, i, j, n):
            return big[:, bass.ds(i * (4 * NT) + (k["dst"] + j) * NT, n)]

        def act_store(eng, p):
            for g in (1, 3):
                eng.wait_ge(S("out_T"), g + 1)
                eng.wait_ge(S("out_sb"), g)
                up(act(vtok[:, g // 2, (g % 2) * 512:(g % 2) * 512 + 512], ps[:, g, :], ACT.Copy), "out_sb")

        V = nc.vector

        def link(ins):
            chain["dve"] += 1
            ins.then_inc(S("dve_chain"), 1)
            nc.vector.wait_ge(S("dve_chain"), chain["dve"])

        def dve_setup(eng, p):
            for z in (svec[:, :, :, :], wfbd[:, :, :], modb[:, :, :], wgate[:, :, :], gateb[:, :], wlr[:, :, :]):
                V.memset(z, 0.0).then_inc(S("zeroed"), 1)
            V.memset(epsc[:, :], EPS).then_inc(S("eps_set"), 1)
            link(V.memset(ones[:, :], 1.0))
            for i, (dst, n) in enumerate(((cols1, 120), (cols2, 47))):
                eng.wait_ge(S("rows_T"), i + 1)
                up(V.tensor_copy(dst[:, :], ps[:, i, 0:n]), "rows_sb")
            eng.wait_ge(S("consts_in"), 16 * CONST_LOADS)
            eng.wait_ge(S("rows_sb"), 2)
            link(V.tensor_scalar(nsink[:, :], sinkb[:, :], -1.0, None, ALU.mult))

        def dve_load(eng, p):
            a = 0 if p.kw["which"] == 0 else SEQ
            for c in range(0, KC, 2):
                eng.wait_ge(S("tokens_T"), p.at("tokens_T", c + 1))
                up(V.tensor_copy(resid[:, c, a:NT], ps[:, c, a:NT]), f"bank_free{c}")

        def dve_rows(eng, p, i, per_turn, x, rounds):
            par = x % 2
            eng.wait_ge(S("mod_rows"), i * per_turn + (p.at("mod_rows") + x + 1))
            up(V.tensor_tensor(modr[:, par, :], ps[:, 4 + par, 0:SEG], modb[:, par, :], ALU.add), f"mod_sum{par}", rounds)

        def dve_cols(eng, p, i, per_turn, x, rounds):
            m = p.kw["host"] or p.kw
            flat = modT[2 * m["block"] + m["l"]][:, :, :].rearrange("p c v -> p (c v)")
            eng.wait_ge(S("mod_cols"), i * per_turn + (p.at("mod_cols") + x + 1))
            up(V.tensor_copy(flat[:, bass.ds(i * (4 * per_turn) + 4 * (m["seg0"] + x), 4)], ps[:, 6, 0:4]), "mod_kept", rounds)

        def dve_mod(eng, p):
            segs = p.kw["segs"]
            for i, rounds in pairs(eng, segs):
                for x in range(2):
                    dve_rows(eng, p, i, 2, x, rounds)
                for x in range(2):
                    dve_cols(eng, p, i, 2, x, rounds)

        def dve_modvec(eng, p):
            blk, l = p.kw["block"], p.kw["l"]
            m = 2 * blk + l
            evacuated(eng, p)

            def gcol(at):
                return cols1[:, at:at + KC].unsqueeze(2).broadcast_to([P, KC, 2])

            T, A = modT[m], modA[m]
            if blk == 0:
                V.scalar_tensor_tensor(A[:, 0], T[:, 8:16, :], 1.0, gcol(G_PRE + 8 * l), ALU.add, ALU.mult)
                last = V.tensor_tensor(A[:, 1], T[:, 16:24, :], gcol(G_POST + 8 * l), ALU.mult)
            else:
                for i in p.kw["parts"]:
                    V.scalar_tensor_tensor(A[:, 2 * i], T[:, 24 * i + 8:24 * i + 16, :], 1.0, gcol(NORM_G + 24 * l + 8 * i), ALU.add, ALU.mult)
                    last = V.tensor_scalar(A[:, 2 * i + 1], T[:, 24 * i + 16:24 * i + 24, :], 1.0 if i == 1 else 0.5, None, ALU.mult)
            up(last, "mod_ready")
            eng.wait_ge(S("mod_ready"), p.at("mod_ready", 1))

        def dve_norm(eng, p):
            nt, mode = p.kw["nt"], p.kw["mode"]
            eng.wait_ge(S("rms_ready"), p.at("rms_ready", 1))
            up(V.reciprocal(rstd[:, 0:nt], rms[:, 0:nt]), "rstd_ready")
            eng.wait_ge(S("rstd_ready"), p.at("rstd_ready", 1))
            halves = [slice(v * SEQ, (v + 1) * SEQ) for v in range(nt // SEQ)]
            if mode != "final":
                m = 2 * p.kw["block"] + p.kw["l"]

            def scaled(c):
                if c >= 3:
                    eng.wait_ge(S("h_ready"), p.at("h_ready", c - 2))
                for v, cols in enumerate(halves):
                    last = V.scalar_tensor_tensor(tnorm[:, c % 3, cols], resid[:, c, cols], modA[m][:, 2 * p.kw["n"] if p.kw["block"] else 0, c, v:v + 1],
                                                  rstd[:, cols], ALU.mult, ALU.mult)
                up(last, "t_ready")

            def low_part(c):
                eng.wait_ge(S("hi_ready"), p.at("hi_ready", c + 1))
                for v, cols in enumerate(halves):
                    sh = modT[m][:, p.kw["n"] * 24 + c, v:v + 1]
                    last = V.scalar_tensor_tensor(h_lo[:, c, cols], tnorm[:, c % 3, cols], sh, h_hi[:, c, cols].bitcast(F32), ALU.add, ALU.subtract)
                up(last, "h_ready")

            if mode == "pre":
                scaled(0)
                for c in range(KC):
                    if c + 1 < KC:
                        scaled(c + 1)
                    low_part(c)
                return
            for c in range(KC):
                for v, cols in enumerate(halves):
                    if mode == "post":
                        y = big3[:, c, cols]
                        link(V.scalar_tensor_tensor(y, y, modA[m][:, 1, c, v:v + 1], rstd[:, cols], ALU.mult, ALU.mult))
                        up(V.tensor_tensor(resid[:, c, cols], resid[:, c, cols], y, ALU.add), "normed")
                    else:
                        up(V.scalar_tensor_tensor(hT[:, c, cols], resid[:, c, cols], cols1[:, FINAL_G + c:FINAL_G + c + 1],
                                                  rstd[:, cols], ALU.mult, ALU.mult), "normed")
            eng.wait_ge(S("normed"), p.at("normed", KC * (nt // SEQ)))

        def dve_split(eng, u, i=0, turn=0, rounds=1):
            eng.wait_ge(S("w_hi"), i * turn + (u + 1))
            up(V.tensor_tensor(w_lo[:, u % RING], stage[:, u % STAGE], w_hi[:, u % RING].bitcast(F32), ALU.subtract), "w_ready", rounds)

        def dve_feed(eng, p):
            for s in range(LEAD):
                dve_split(eng, p.at("unit_done") + s)

        def dve_mixsplit(eng, p):
            for c in range(KC):
                eng.wait_ge(S("hi_ready"), p.at("hi_ready", c + 1))
                x = mixT[:, c, 0:p.kw["nt"]]
                up(V.tensor_tensor(h_lo[:, c, 0:p.kw["nt"]], x, h_hi[:, c, 0:p.kw["nt"]].bitcast(F32), ALU.subtract), "h_ready")

        def dve_gemm(eng, p):
            k = p.kw
            a, b = k["tok"]
            n = b - a
            u0, per, step, evac = p.at("unit_done"), k["per"], k["step"], k["evac"]
            turn = per * step
            def evacuate(i, j, rounds):
                if evac in ("copy", "swiglu") and not k["sumsq"] and (j % 2) != (evac == "swiglu"):
                    return
                eng.wait_ge(S("unit_done"), i * turn + (u0 + j * per + per))
                if evac == "swiglu":
                    eng.wait_ge(S(f"bank_free{j - 1}"), p.at(f"bank_free{j - 1}") + i + 1)
                    eng.wait_ge(S("g_ready"), i * 2 + (p.at("g_ready") + j // 2))
                    up(V.tensor_tensor(gt[:, 0:n], sg[:, j // 2, 0:n], ps[:, j, 0:n], ALU.mult), f"bank_free{j}", rounds)
                    cols = bass.ds(i * (2 * NT) + (j // 2) * NT, n)
                    hi, lo = (g[:, :, :].rearrange("p c n -> p (c n)")[:, cols] for g in (g_hi, g_lo))
                    eng.wait_ge(S(f"bank_free{j}"), p.at(f"bank_free{j}") + i + 1)
                    up(V.tensor_copy(hi, gt[:, 0:n]), "g_hi_ready", rounds)
                    eng.wait_ge(S("g_hi_ready"), i * 2 + (p.at("g_hi_ready") + j // 2 + 1))
                    up(V.tensor_tensor(lo, gt[:, 0:n], hi.bitcast(F32), ALU.subtract), "g_ready", rounds)
                elif evac == "resid":
                    gate = modA[2 + k["l"]][:, :, :, :].rearrange("p s c v -> p (s c v)")
                    for v in range(n // SEQ):
                        cols = bass.ds(i * (4 * NT) + j * NT + v * SEQ, SEQ)
                        rs = resid[:, :, :].rearrange("p c n -> p (c n)")[:, cols]
                        at = (2 * k["g"] + 1) * KC * 2 + j * 2 + v
                        last = V.scalar_tensor_tensor(rs, ps[:, j, v * SEQ:(v + 1) * SEQ], gate[:, bass.ds(i * 8 + at, 1)], rs,
                                                      ALU.mult, ALU.add)
                    up(last, f"bank_free{j}", rounds)
                elif evac == "tok":
                    up(V.tensor_copy(tok_dst(k, i, j, 1), tok_out(j, 1)), f"bank_free{2 * j + 1}", rounds)
                else:
                    up(V.tensor_copy(gemm_dst(k, i, j, n), ps[:, j, 0:n]), f"bank_free{j}", rounds)

            for i, js, rounds in turns(eng, k["n"], step, peel=not k["fed"]):
                for j in js:
                    seg = hosted(p, j, js)
                    if seg is not None:
                        dve_rows(eng, p, i, k["hper"], seg, rounds)
                    for x in splits(p, i, j, rounds):
                        dve_split(eng, u0 + x, i, turn, rounds)
                    evacuate(i, j, rounds)
                    if seg is not None:
                        dve_cols(eng, p, i, k["hper"], seg, rounds)

        def pool_sums(eng, p, n, items, step):
            if p.at("ms_sum"):
                eng.wait_ge(S("ms_sum"), p.at("ms_sum"))
            up(nc.gpsimd.memset(sqsum[:, :], 0.0), "sums_clear")
            eng.wait_ge(S("sums_clear"), p.at("sums_clear", 1))
            for i, js, rounds in turns(eng, items, step):
                for j in js:
                    eng.wait_ge(S("sq_ready"), i * step + (p.at("sq_ready") + j + 1))
                    if p.at("sq_used") + j:
                        eng.wait_ge(S("sq_used"), i * step + (p.at("sq_used") + j))
                    up(nc.gpsimd.tensor_tensor(sqsum[:, 0:n], sqsum[:, 0:n], sq[:, j % 2, 0:n], ALU.add), "sq_used", rounds)

        def pool_squares(eng, p):
            if p.kw["after"] == "load":
                eng.wait_ge(S("tokens_T"), p.at("tokens_T"))
            pool_sums(eng, p, p.kw["nt"], KC, KC)

        def pool_gemm(eng, p):
            if p.kw["sumsq"]:
                eng.wait_ge(S("unit_done"), p.at("unit_done", 1))
                pool_sums(eng, p, p.kw["tok"][1] - p.kw["tok"][0], p.kw["n"], 4)

        def dve_store(eng, p):
            for g in (0, 2):
                eng.wait_ge(S("out_T"), g + 1)
                if g:
                    eng.wait_ge(S("out_sb"), g)
                up(V.tensor_copy(vtok[:, g // 2, (g % 2) * 512:(g % 2) * 512 + 512], ps[:, g, :]), "out_sb")

        probs = scr[:, 0:2048].rearrange("p (s k) -> p s k", k=512)
        probsT = scr[:, 2048:4096].rearrange("p (s b q) -> p s b q", s=2, b=4)
        dftU = scr[:, 4096:6144].rearrange("p (g k) -> p g k", k=512)
        dftF = scr[:, 6144:7168].rearrange("p (c n) -> p c n", n=NT)
        kswap = scr[:, 7168:7680]
        nmx, nm, rsum, esink = (small[:, 32 * i:32 * i + 32] for i in range(4))

        def items1(p):
            x = [(h, 0, 0, 4) for h in range(HEADS)]
            return x + ([(h, SEQ, SEQ, 2) for h in range(HEADS)] if p.kw["both"] else [])

        def pe_mix1(eng, p):
            l, sets = p.kw["l"], 2 if p.kw["both"] else 1
            items = items1(p)
            evacuated(eng, p)
            for a in range(TT):
                last = tr(ps[:, 4, a * P:(a + 1) * P], big3[:, 5, a * P:(a + 1) * P], ident)
            up(last, "v_T")
            for c in range(2):
                for s in range(sets):
                    for a in range(2):
                        last = mm(ps[:, 2 * c + s, a * 256:a * 256 + 256], big3[:, 10 + c, s * SEQ + a * P:s * SEQ + a * P + P],
                                  C("dftc"), start=True, stop=True)
                    up(last, "dft1")
            eng.wait_ge(S("dft1_sb"), p.at("dft1_sb", 2 * sets))
            eng.wait_ge(S("v_sb"), p.at("v_sb", 1))
            for c in range(2):
                for s in range(sets):
                    for a in range(2):
                        for part in range(2):
                            last = mm(ps[:, 4 + c, s * SEQ:s * SEQ + SEQ], dftU[:, 2 * c + s, a * 256 + part * P:a * 256 + part * P + P],
                                      dftn[:, a, part, :], start=a + part == 0, stop=a + part == 2)
                up(last, "dft2")
            for c in range(2):
                eng.wait_ge(S("dft2_sb"), p.at("dft2_sb", c + 1))
                up(mm(ps[:, 6 + c, 0:sets * SEQ], wfbd[:, 2 * l + c, :], dftF[:, c, 0:sets * SEQ], start=True, stop=True), "dft3")

            eng.wait_ge(S("k_swapped"), p.at("k_swapped", 1))

            def scores(i):
                h, q0, k0, kt = items[i]
                if i >= 2:
                    eng.wait_ge(S("probs_raw"), p.at("probs_raw", 2 * i - 2))
                r = slice(64 * (h % 2), 64 * (h % 2) + 64)
                keys = big3[r, 4, k0:k0 + kt * P] if h // Q_PER_KV == h % 2 else kswap[r, k0:k0 + kt * P]
                for qt in range(2):
                    b = 2 * (i % 2) + qt
                    last = mm(ps[:, b, 0:kt * P], big3[r, h // 2, q0 + qt * P:q0 + qt * P + P], keys, start=True, stop=q0 > 0)
                    if q0 == 0:
                        cut = (1 - qt) * P
                        last = mm(ps[:, b, cut:cut + P], ident, wmask[:, qt, :], start=False, stop=True)
                    up(last, "scores_ready")

            def transposes(i):
                h, q0, k0, kt = items[i]
                for qt in range(2):
                    eng.wait_ge(S("probs_ready"), p.at("probs_ready", 2 * i + qt + 1))
                    if i >= 1:
                        eng.wait_ge(S("probsT_sb"), p.at("probsT_sb", 2 * i - 1 + qt))
                    for kb in range(kt):
                        last = tr(ps[:, 4 + qt, kb * P:kb * P + P], probs[:, 2 * (i % 2) + qt, kb * P:kb * P + P], ident)
                    up(last, "probsT_done")

            def values(i):
                h, q0, k0, kt = items[i]
                pair = i // 2
                eng.wait_ge(S("probsT_sb"), p.at("probsT_sb", 2 * i + 2))
                if pair < 2:
                    eng.wait_ge(S("dft3_gated"), p.at("dft3_gated", 2))
                else:
                    eng.wait_ge(S("att_gated"), p.at("att_gated", pair - 1))
                g, r = h // Q_PER_KV, slice(64 * (h % 2), 64 * (h % 2) + 64)
                for kb in range(kt):
                    last = mm(ps[r, 6 + pair % 2, 0:SEQ], vtok[:, k0 // P + kb, g * HD:(g + 1) * HD], probsT[:, i % 2, kb, :],
                              start=kb == 0, stop=kb == kt - 1)
                up(last, "pv_done")

            scores(0)
            for i in range(len(items)):
                if i + 1 < len(items):
                    scores(i + 1)
                transposes(i)
                if i:
                    values(i - 1)
            values(len(items) - 1)
            eng.wait_ge(S("att_gated"), p.at("att_gated", len(items) // 2))
            eng.wait_ge(S("conv_done"), p.at("conv_done", 1))

        def act_mix1(eng, p):
            l, sets = p.kw["l"], 2 if p.kw["both"] else 1
            items, nt = items1(p), sets * SEQ
            evacuated(eng, p)
            eng.wait_ge(S("v_T"), p.at("v_T", 1))
            up(act(vtok[:, :, 0:P], ps[:, 4, :].rearrange("p (a n) -> p a n", n=P), ACT.Copy), "v_sb")
            for c in range(2):
                for s in range(sets):
                    eng.wait_ge(S("dft1"), p.at("dft1", sets * c + s + 1))
                    up(act(dftU[:, 2 * c + s, :], ps[:, 2 * c + s, :], ACT.Copy), "dft1_sb")
            for c in range(2):
                eng.wait_ge(S("dft2"), p.at("dft2", c + 1))
                up(act(dftF[:, c, 0:nt], ps[:, 4 + c, 0:nt], ACT.Copy), "dft2_sb")
            for a, b in ((12, 14), (6, 10), (20, 22)):
                last = act(big3[:, a:b, 0:nt], big3[:, a:b, 0:nt], ACT.Silu)
            up(last, "gates_done")

            def exps(i):
                h, q0, k0, kt = items[i]
                for qt in range(2):
                    n = 2 * i + qt
                    eng.wait_ge(S("negmax_ready"), p.at("negmax_ready", n + 1))
                    act(esink[:, n:n + 1], sinkb[:, l * HEADS + h:l * HEADS + h + 1], ACT.Exp, bias=nm[:, n:n + 1])
                    b = 2 * (i % 2) + qt
                    up(act(probs[:, b, 0:kt * P], ps[:, b, 0:kt * P], ACT.Exp, bias=nm[:, n:n + 1], scale=HD ** -0.5,
                           accum_out=rsum[:, n:n + 1]), "probs_raw")

            def keep_T(i):
                h, q0, k0, kt = items[i]
                if i >= 2:
                    eng.wait_ge(S("pv_done"), p.at("pv_done", i - 1))
                for qt in range(2):
                    eng.wait_ge(S("probsT_done"), p.at("probsT_done", 2 * i + qt + 1))
                    up(act(probsT[:, i % 2, 0:kt, qt * P:qt * P + P], ps[:, 4 + qt, 0:kt * P].rearrange("p (b q) -> p b q", q=P), ACT.Copy),
                       "probsT_sb")

            for i in range(len(items)):
                exps(i)
                if i:
                    keep_T(i - 1)
            keep_T(len(items) - 1)

        def conv3(y, x, w, bias, nt, done=None):
            link(V.tensor_scalar(y[:, 0:nt], x[:, 0:nt], w(1), bias, ALU.mult, ALU.add))
            for s in range(nt // SEQ):
                a, b = s * SEQ, (s + 1) * SEQ
                link(V.scalar_tensor_tensor(y[:, a + 1:b], x[:, a:b - 1], w(0), y[:, a + 1:b], ALU.mult, ALU.add))
                ins = V.scalar_tensor_tensor(y[:, a:b - 1], x[:, a + 1:b], w(2), y[:, a:b - 1], ALU.mult, ALU.add)
                up(ins, done) if done and b == nt else link(ins)

        def rotary(chunks, n, tmp, name):
            shape = [P, n, SEQ]
            x, tmp = chunks[:, :, 0:SEQ], tmp.rearrange("p (c n) -> p c n", n=SEQ)
            link(V.stream_shuffle(tmp, x, SWAP16))
            link(V.tensor_tensor(tmp, tmp, ropeS.unsqueeze(1).broadcast_to(shape), ALU.mult))
            link(V.tensor_tensor(x, x, ropeC.unsqueeze(1).broadcast_to(shape), ALU.mult))
            up(V.tensor_tensor(x, x, tmp, ALU.add), name)

        def dve_mix1(eng, p):
            l, sets = p.kw["l"], 2 if p.kw["both"] else 1
            items, nt = items1(p), sets * SEQ
            hflat = hT[:, :, :].rearrange("p c n -> p (c n)")
            evacuated(eng, p)
            rotary(big3[:, 0:5], 5, hflat[:, 0:5 * SEQ], "roped")
            eng.wait_ge(S("roped"), p.at("roped", 1))
            V.tensor_copy(kswap[0:64, :], big3[64:128, 4, :])
            up(V.tensor_copy(kswap[64:128, :], big3[0:64, 4, :]), "k_swapped")
            for c in range(2):
                t_, y = hT[:, 4 + c, 0:nt], hT[:, 6 + c, 0:nt]
                link(V.tensor_tensor(t_, big3[:, 14 + c, 0:nt], big3[:, 18 + c, 0:nt], ALU.mult))
                conv3(y, t_, lambda tap: cols2[:, CONV_W + (l * 3 + tap) * 2 + c:CONV_W + (l * 3 + tap) * 2 + c + 1],
                      cols2[:, CONV_B + 2 * l + c:CONV_B + 2 * l + c + 1], nt)
                link(V.tensor_tensor(y, y, big3[:, 16 + c, 0:nt], ALU.mult))
            eng.wait_ge(S("gates_done"), p.at("gates_done", 1))
            up(V.tensor_tensor(mixT[:, 6:8, 0:nt], hT[:, 6:8, 0:nt], big3[:, 20:22, 0:nt], ALU.mult), "conv_done")
            for c in range(2):
                eng.wait_ge(S("dft3"), p.at("dft3", c + 1))
                up(V.tensor_tensor(mixT[:, 4 + c, 0:nt], ps[:, 6 + c, 0:nt], big3[:, 12 + c, 0:nt], ALU.mult), "dft3_gated")

            def maxima(i):
                h, q0, k0, kt = items[i]
                for qt in range(2):
                    n = 2 * i + qt
                    eng.wait_ge(S("scores_ready"), p.at("scores_ready", n + 1))
                    link(V.reduce_max(nmx[:, n:n + 1], ps[:, 2 * (i % 2) + qt, 0:kt * P], AX.X, negate=True))
                    up(V.tensor_scalar(nm[:, n:n + 1], nmx[:, n:n + 1], HD ** -0.5, nsink[:, l * HEADS + h:l * HEADS + h + 1],
                                       ALU.mult, ALU.min), "negmax_ready")

            def normalise(i):
                h, q0, k0, kt = items[i]
                for qt in range(2):
                    n = 2 * i + qt
                    eng.wait_ge(S("probs_raw"), p.at("probs_raw", n + 1))
                    link(V.tensor_tensor(rsum[:, n:n + 1], rsum[:, n:n + 1], esink[:, n:n + 1], ALU.add))
                    link(V.reciprocal(nmx[:, n:n + 1], rsum[:, n:n + 1]))
                    pr = probs[:, 2 * (i % 2) + qt, 0:kt * P]
                    up(V.tensor_scalar(pr, pr, nmx[:, n:n + 1], None, ALU.mult), "probs_ready")

            def gate(pair):
                h, q0, k0, kt = items[2 * pair]
                eng.wait_ge(S("pv_done"), p.at("pv_done", 2 * pair + 2))
                up(V.tensor_tensor(mixT[:, h // 2, q0:q0 + SEQ], ps[:, 6 + pair % 2, 0:SEQ], big3[:, 6 + h // 2, q0:q0 + SEQ], ALU.mult),
                   "att_gated")

            maxima(0)
            for i in range(len(items)):
                if i + 1 < len(items):
                    maxima(i + 1)
                normalise(i)
                if i >= 3 and i % 2:
                    gate((i - 3) // 2)
            gate(len(items) // 2 - 1)

        wT = scr[:, 2048:3072].rearrange("p (s k) -> p s k", k=512)
        decay = scr[:, 3072:6144].rearrange("p (s t r q) -> p s t r q", s=2, t=2, r=3)
        dargs = scr[:, 6144:7168].rearrange("p (t r q) -> p t r q", t=2, r=2)
        dnm, ebm = scr[:, 7168:7680], scr[:, 7680:8192]
        hsq = scr[:, 0:2048].rearrange("p (h n) -> p h n", n=NT)
        grow = [hT[0:64, i, :] for i in range(4)]
        acol = hT[:, 5, 0:4 * 64]
        items2 = [(h, qt) for h in range(DA_HEADS) for qt in range(TT)]

        def keys2(qt):
            return (0, 4) if qt < 2 else (SEQ, 2)

        def pe_even(eng, p):
            evacuated(eng, p)
            for k in range(KC):
                for part in (h_hi, h_lo):
                    last = mm(ps[:, 6, :], wgate[:, k, :], part[:, k, :].bitcast(F32), start=k == 0 and part is h_hi, stop=k == KC - 1 and part is h_lo)
            up(last, "gate_rows")
            eng.wait_ge(S("roped2"), p.at("roped2", 1))

            def scores(i):
                h, qt = items2[i]
                k0, kt = keys2(qt)
                if i >= 2:
                    eng.wait_ge(S("probs_raw"), p.at("probs_raw", 2 * i - 2))
                for c in range(2):
                    r = slice(64 * c, 64 * c + 64)
                    up(mm(ps[:, 2 * (i % 2) + c, 0:kt * P], big3[r, h, qt * P:qt * P + P], big3[r, 4 + h, k0:k0 + kt * P],
                          start=True, stop=True), "scores_ready")

            def transposes(i):
                kt = keys2(items2[i][1])[1]
                eng.wait_ge(S("probs_ready"), p.at("probs_ready", i + 1))
                if i >= 2:
                    eng.wait_ge(S("probsT_sb"), p.at("probsT_sb", i - 1))
                for kb in range(kt):
                    last = tr(ps[:, 4 + i % 2, kb * P:kb * P + P], probs[:, 2 * (i % 2), kb * P:kb * P + P], ident)
                up(last, "probsT_done")

            def values(i):
                h, qt = items2[i]
                k0, kt = keys2(qt)
                g = i // 2
                eng.wait_ge(S("probsT_sb"), p.at("probsT_sb", i + 1))
                if g < 2:
                    eng.wait_ge(S("gate_bias"), p.at("gate_bias", 1))
                else:
                    eng.wait_ge(S("att_evac"), p.at("att_evac", g - 1))
                for kb in range(kt):
                    last = mm(ps[:, 6 + g % 2, (qt % 2) * P:(qt % 2) * P + P], vtok[:, k0 // P + kb, h * P:h * P + P],
                              wT[:, i % 2, kb * P:kb * P + P], start=kb == 0, stop=kb == kt - 1)
                up(last, "pv_done")

            scores(0)
            for i in range(len(items2)):
                if i + 1 < len(items2):
                    scores(i + 1)
                transposes(i)
                if i:
                    values(i - 1)
            values(len(items2) - 1)

            def head_sums(n):
                eng.wait_ge(S("hsq"), p.at("hsq", n + 1))
                for h in range(4):
                    last = mm(ps[:, h, :], onesPP, hsq[:, h, :], start=True, stop=True)
                up(last, "hsum")

            head_sums(0)
            eng.wait_ge(S("rows_ready"), p.at("rows_ready", 1))
            eng.wait_ge(S("att_evac"), p.at("att_evac", 8))
            for a in range(TT):
                last = tr(ps[:, 7, a * 64:a * 64 + 64], grow[0][:, a * P:a * P + P], ident[0:64, 0:64])
            up(last, "acol_T")
            eng.wait_ge(S("conv_silu"), p.at("conv_silu", 1))
            eng.wait_ge(S("hms"), p.at("hms", 1))
            for h in range(ML_HEADS):
                r = slice(64 * (h % 2), 64 * (h % 2) + 64)
                if h:
                    eng.wait_ge(S("weighted"), p.at("weighted", 2 * h))
                q = big3[r, 16 + h // 2, :]
                k = big3[r, 18 + h // 2, :]
                for a in range(2):
                    mm(ps[:, a, :], k[:, SEQ + a * P:SEQ + a * P + P], q, start=True, stop=True)
                    last = mm(ps[:, 2, a * SEQ:a * SEQ + SEQ], k[:, a * P:a * P + P], q[:, 0:SEQ], start=True, stop=True)
                up(last, "qk_done")
                for d in range(2):
                    j = 2 * h + d
                    pick = ident[0:64, 32 * d + h:32 * d + h + 1].broadcast_to([64, P])
                    if j:
                        eng.wait_ge(S("decay"), p.at("decay", j))
                        eng.wait_ge(S("ebm"), p.at("ebm", j))
                    up(mm(ps[:, 3, :], pick, grow[2], start=True, stop=True), "bcast")
                    up(mm(ps[:, 4, :], pick, grow[3], start=True, stop=True), "bcast")
                    eng.wait_ge(S("weighted"), p.at("weighted", j + 1))
                    if j:
                        eng.wait_ge(S("mem_done"), p.at("mem_done", j))
                    for a in range(2):
                        both = decay[:, j % 2, a, 1:3, :]
                        mm(ps[:, 5, :], vtok[:, 2 + a, 512 + h * P:512 + h * P + P], both, start=a == 0, stop=False)
                    for a in range(2):
                        mm(ps[:, 5, 0:SEQ], vtok[:, a, 512 + h * P:512 + h * P + P], decay[:, j % 2, a, 0, :], start=False, stop=a == 1)
                    for a in range(2):
                        mm(ps[:, 6, :], onesPP, decay[:, j % 2, a, 1:3, :], start=a == 0, stop=False)
                    for a in range(2):
                        last = mm(ps[:, 6, 0:SEQ], onesPP, decay[:, j % 2, a, 0, :], start=False, stop=a == 1)
                    up(last, "numden")
            head_sums(1)
            eng.wait_ge(S("mix_done"), p.at("mix_done", 2))

        def act_even(eng, p):
            evacuated(eng, p)
            eng.wait_ge(S("lam_e"), p.at("lam_e", 1))
            up(act(small[:, 162:164], small[:, 160:162], ACT.Exp), "lam_ready")
            eng.wait_ge(S("gate_bias"), p.at("gate_bias", 1))
            alink(act(grow[2], grow[1], ACT.Abs))
            alink(act(grow[2], grow[2], ACT.Exp, scale=-1.0))
            up(act(grow[2], grow[2], ACT.Ln, bias=1.0), "gate_ln")

            def exps(i):
                kt = keys2(items2[i][1])[1]
                eng.wait_ge(S("negmax_ready"), p.at("negmax_ready", i + 1))
                for c in range(2):
                    n = 2 * i + c
                    b = 2 * (i % 2) + c
                    up(act(probs[:, b, 0:kt * P], ps[:, b, 0:kt * P], ACT.Exp, bias=nm[:, n:n + 1], scale=HD ** -0.5,
                           accum_out=rsum[:, n:n + 1]), "probs_raw")

            def keep_T(i):
                n = keys2(items2[i][1])[1] * P
                if i >= 2:
                    eng.wait_ge(S("pv_done"), p.at("pv_done", i - 1))
                eng.wait_ge(S("probsT_done"), p.at("probsT_done", i + 1))
                up(act(wT[:, i % 2, 0:n], ps[:, 4 + i % 2, 0:n], ACT.Copy), "probsT_sb")

            for i in range(len(items2)):
                exps(i)
                if i:
                    keep_T(i - 1)
            keep_T(len(items2) - 1)

            def head_roots(n, src, dst):
                up(act(hsq[:, :, :], src, ACT.Square), "hsq")
                eng.wait_ge(S("hms"), p.at("hms", n + 1))
                up(act(dst, dst, ACT.Sqrt), "hrms")

            eng.wait_ge(S("att_evac"), p.at("att_evac", 8))
            head_roots(0, big3[:, 20:24, :], mixT[:, 0:4, :])
            eng.wait_ge(S("conv_lin"), p.at("conv_lin", 1))
            up(act(big3[:, 16:20, :], big3[:, 16:20, :], ACT.Silu), "conv_silu")
            up(act(big3[:, 12:16, :], big3[:, 12:16, :], ACT.Sigmoid), "osig")
            eng.wait_ge(S("acol_T"), p.at("acol_T", 1))
            alink(act(acol, ps[:, 7, 0:4 * 64], ACT.Copy))
            for h in range(ML_HEADS):
                for d in range(2):
                    j = 2 * h + d

                    def a_of(tile):
                        at = tile * 64 + 32 * d + h
                        return acol[:, at:at + 1]

                    eng.wait_ge(S("bcast"), p.at("bcast", 2 * j + 2))
                    if j:
                        eng.wait_ge(S("mem_done"), p.at("mem_done", j))
                    up(act(ebm, ps[:, 4, :], ACT.Exp, scale=-1.0), "ebm")
                    eng.wait_ge(S("args"), p.at("args", j + 1))
                    if j >= 2:
                        eng.wait_ge(S("numden"), p.at("numden", j - 1))
                    for a in range(2):
                        act(decay[:, j % 2, a, 0, :], dargs[:, a, 0, :], ACT.Exp, bias=a_of(a))
                        act(decay[:, j % 2, a, 1, :], ps[:, 3, 0:SEQ], ACT.Exp, bias=a_of(2 + a), scale=-1.0)
                        last = act(decay[:, j % 2, a, 2, :], dargs[:, a, 1, :], ACT.Exp, bias=a_of(2 + a))
                    up(last, "decay")
                    eng.wait_ge(S("numden"), p.at("numden", j + 1))
                    up(act(dnm, ps[:, 6, :], ACT.Abs), "den_abs")
            eng.wait_ge(S("mem_done"), p.at("mem_done", 8))
            head_roots(1, big3[:, 0:4, :], mixT[:, 4:8, :])

        def dve_even(eng, p):
            evacuated(eng, p)
            eng.wait_ge(S("gate_rows"), p.at("gate_rows", 1))
            V.tensor_scalar(grow[0], ps[0:64, 6, :], gateb[:, 0:1], None, ALU.add)
            link(V.tensor_copy(grow[1], ps[64:128, 6, :]))
            up(V.tensor_scalar(grow[1], grow[1], gateb[:, 1:2], None, ALU.add), "gate_bias")
            rotary(big3[:, 0:8], 8, mixT[:, 0:4, :].rearrange("p c n -> p (c n)"), "roped2")
            for i in range(2):
                link(V.tensor_tensor(dlam[:, 128 * i:128 * i + 64], dlam[:, 128 * i:128 * i + 64], dlam[:, 128 * i + 64:128 * i + 128], ALU.mult))
                ins = V.reduce_sum(small[:, 160 + i:161 + i], dlam[:, 128 * i:128 * i + 64], AX.X)
                link(ins) if i == 0 else up(ins, "lam_e")
            eng.wait_ge(S("lam_ready"), p.at("lam_ready", 1))
            link(V.scalar_tensor_tensor(small[:, 164:165], small[:, 163:164], -LAM_INIT, small[:, 162:163], ALU.add, ALU.subtract))
            link(V.tensor_scalar(small[:, 165:166], cols2[:, DIFF_G:DIFF_G + 1], 1.0 - LAM_INIT, None, ALU.mult))

            def maxima(i):
                kt = keys2(items2[i][1])[1]
                for c in range(2):
                    n = 2 * i + c
                    eng.wait_ge(S("scores_ready"), p.at("scores_ready", n + 1))
                    link(V.reduce_max(nmx[:, n:n + 1], ps[:, 2 * (i % 2) + c, 0:kt * P], AX.X, negate=True))
                up(V.tensor_scalar(nm[:, 2 * i:2 * i + 2], nmx[:, 2 * i:2 * i + 2], HD ** -0.5, None, ALU.mult), "negmax_ready")

            def combine(i):
                kt = keys2(items2[i][1])[1]
                n, b = 2 * i, 2 * (i % 2)
                eng.wait_ge(S("probs_raw"), p.at("probs_raw", n + 2))
                link(V.reciprocal(esink[:, n:n + 2], rsum[:, n:n + 2]))
                link(V.tensor_tensor(esink[:, n + 1:n + 2], esink[:, n + 1:n + 2], small[:, 164:165], ALU.mult))
                p0, p1 = probs[:, b, 0:kt * P], probs[:, b + 1, 0:kt * P]
                link(V.tensor_scalar(p0, p0, esink[:, n:n + 1], None, ALU.mult))
                up(V.scalar_tensor_tensor(p0, p1, esink[:, n + 1:n + 2], p0, ALU.mult, ALU.add), "probs_ready")

            def keep(g):
                eng.wait_ge(S("pv_done"), p.at("pv_done", 2 * g + 2))
                up(V.tensor_copy(big3[:, 20 + g // 2, (g % 2) * SEQ:(g % 2) * SEQ + SEQ], ps[:, 6 + g % 2, 0:SEQ]), "att_evac")

            maxima(0)
            for i in range(len(items2)):
                if i + 1 < len(items2):
                    maxima(i + 1)
                combine(i)
                if i >= 3 and i % 2:
                    keep((i - 3) // 2)
            keep(len(items2) // 2 - 1)

            for c in range(4):
                conv3(big3[:, 16 + c, :], big3[:, 8 + c, :], lambda tap: cols2[:, MCONV_W + tap * 4 + c:MCONV_W + tap * 4 + c + 1],
                      cols2[:, MCONV_B + c:MCONV_B + c + 1], NT, "conv_lin" if c == 3 else None)

            def head_norm(n, src, g, dst):
                eng.wait_ge(S("hsum"), p.at("hsum", n + 1))
                up(V.tensor_scalar(dst, ps[:, 0:4, :], 1.0 / P, EPS, ALU.mult, ALU.add), "hms")
                eng.wait_ge(S("hrms"), p.at("hrms", n + 1))
                link(V.reciprocal(dst, dst))
                for h in range(4):
                    ins = V.scalar_tensor_tensor(dst[:, h, :], src[:, h, :], g(h), dst[:, h, :], ALU.mult, ALU.mult)
                return ins

            up(head_norm(0, big3[:, 20:24, :], lambda h: small[:, 165:166], mixT[:, 0:4, :]), "mix_done")

            f, b, a, m = grow[1], grow[3], grow[0], grow[2]
            eng.wait_ge(S("gate_ln"), p.at("gate_ln", 1))
            link(V.scalar_tensor_tensor(f, f, 0.0, grow[2], ALU.min, ALU.subtract))

            def scan(dst, data, op0, op1, first):
                fw, bw = slice(0, 32), slice(32, 64)
                link(V.tensor_tensor_scan(dst[fw, SEQ:NT], first(fw, SEQ, NT), data[fw, SEQ:NT], 0.0, op0, op1))
                link(V.tensor_tensor_scan(dst[fw, 0:SEQ], first(fw, 0, SEQ), data[fw, 0:SEQ], dst[fw, NT - 1:NT], op0, op1))
                link(V.tensor_tensor_scan(dst[bw, SEQ:NT][:, ::-1], first(bw, SEQ, NT)[:, ::-1], data[bw, SEQ:NT][:, ::-1], 0.0, op0, op1))
                link(V.tensor_tensor_scan(dst[bw, 0:SEQ][:, ::-1], first(bw, 0, SEQ)[:, ::-1], data[bw, 0:SEQ][:, ::-1], dst[bw, SEQ:SEQ + 1], op0, op1))

            scan(b, f, ALU.mult, ALU.add, lambda r, s, e: ones[r, 0:SEQ])
            link(V.tensor_tensor(a, a, b, ALU.subtract))
            scan(m, a, ALU.max, ALU.max, lambda r, s, e: a[r, s:e])
            up(V.tensor_tensor(b, b, m, ALU.add), "rows_ready")

            for h in range(ML_HEADS):
                for d in range(2):
                    j = 2 * h + d
                    eng.wait_ge(S("bcast"), p.at("bcast", 2 * j + 1))
                    if j:
                        eng.wait_ge(S("decay"), p.at("decay", j))
                    mrow = ps[:, 3, :].rearrange("p (r q) -> p r q", r=2)
                    for t_ in range(2):
                        last = V.scalar_tensor_tensor(dargs[:, t_], mrow, -1.0, mmask[:, d, t_].unsqueeze(1).broadcast_to([P, 2, SEQ]),
                                                      ALU.mult, ALU.add)
                    up(last, "args")
                    eng.wait_ge(S("decay"), p.at("decay", j + 1))
                    eng.wait_ge(S("qk_done"), p.at("qk_done", h + 1))
                    for t_ in range(2):
                        w = decay[:, j % 2, t_]
                        V.scalar_tensor_tensor(w[:, 1:3, :], ps[:, t_, :].rearrange("p (r q) -> p r q", r=2), HD ** -0.5, w[:, 1:3, :],
                                               ALU.mult, ALU.mult)
                        last = V.scalar_tensor_tensor(w[:, 0, :], ps[:, 2, t_ * SEQ:t_ * SEQ + SEQ], HD ** -0.5, w[:, 0, :], ALU.mult, ALU.mult)
                    up(last, "weighted")
                    eng.wait_ge(S("den_abs"), p.at("den_abs", j + 1))
                    link(V.tensor_tensor(dnm, dnm, ebm, ALU.max))
                    link(V.reciprocal(dnm, dnm))
                    if d == 0:
                        up(V.tensor_tensor(big3[:, h, :], ps[:, 5, :], dnm, ALU.mult), "mem_done")
                    else:
                        link(V.tensor_tensor(dnm, ps[:, 5, :], dnm, ALU.mult))
                        up(V.tensor_tensor(big3[:, h, :], big3[:, h, :], dnm, ALU.add), "mem_done")
            link(head_norm(1, big3[:, 0:4, :], lambda h: cols2[:, ML_G + h:ML_G + h + 1], mixT[:, 4:8, :]))
            eng.wait_ge(S("osig"), p.at("osig", 1))
            up(V.tensor_tensor(mixT[:, 4:8, :], mixT[:, 4:8, :], big3[:, 12:16, :], ALU.mult), "mix_done")

        lrT = scr[0:64, 0:512]
        ckd = scr[:, 512:2560].rearrange("p (i n) -> p i n", n=SEQ)
        ckdT = scr[:, 2560:4608].rearrange("p (i n) -> p i n", n=SEQ)
        state = scr[:, 4608:6656].rearrange("p (i n) -> p i n", n=SEQ)
        amask = scr[:, 0:2048].rearrange("p (i n) -> p i n", n=SEQ)
        bend, blast, eblast = small[:, 0:8], small[:, 32:64], small[:, 64:96]
        STREAMS = [(d, h) for d in range(2) for h in range(GLA_HEADS)]

        def pe_odd(eng, p):
            evacuated(eng, p)
            for k in range(KC):
                for part in (h_hi, h_lo):
                    last = mm(ps[0:64, 0, :], wlr[:, k, :], part[:, k, :].bitcast(F32), start=k == 0 and part is h_hi, stop=k == KC - 1 and part is h_lo)
            up(last, "lr_done")
            eng.wait_ge(S("lr_sb"), p.at("lr_sb", 1))
            for i, (d, h) in enumerate(STREAMS):
                if i >= 4:
                    eng.wait_ge(S("z_sb"), p.at("z_sb", i - 3))
                r = slice(32 * d, 32 * d + 16)
                up(mm(ps[:, 1 + i % 4, :], wgla[r, h * P:h * P + P], lrT[r, :], start=True, stop=True), "z_done")
            eng.wait_ge(S("z_sb"), p.at("z_sb", 8))
            for i, (d, h) in enumerate(STREAMS):
                eng.wait_ge(S("ckd"), p.at("ckd", i + 1))
                if i >= 4:
                    eng.wait_ge(S("ckd_sb"), p.at("ckd_sb", i - 3))
                for a in range(2):
                    last = tr(ps[:, i % 4, a * P:a * P + P], ckd[:, i, a * P:a * P + P], ident)
                up(last, "ckd_T")
            for i, (d, h) in enumerate(STREAMS):
                eng.wait_ge(S("ckd_sb"), p.at("ckd_sb", i + 1))
                if i >= 4:
                    eng.wait_ge(S("st_sb"), p.at("st_sb", i - 3))
                for a in range(2):
                    last = mm(ps[:, 4 + i % 4, 0:SEQ], ckdT[:, i, a * P:a * P + P], vtok[:, 2 + a, h * SEQ:h * SEQ + SEQ], start=a == 0, stop=a == 1)
                up(last, "st_done")
            for i, (d, h) in enumerate(STREAMS):
                eng.wait_ge(S("x_in"), p.at("x_in", i + 1))
                eng.wait_ge(S("xkd_sb"), p.at("xkd_sb", i - 3)) if i >= 4 else eng.wait_ge(S("ckd_sb"), p.at("ckd_sb", 8))
                for a in range(2):
                    last = tr(ps[:, i % 4, a * P:a * P + P], hT[:, i, a * P:a * P + P], ident)
                up(last, "xkd_T")
                eng.wait_ge(S("a_sb"), p.at("a_sb", i - 3)) if i >= 4 else eng.wait_ge(S("st_sb"), p.at("st_sb", 8))
                for a in range(2):
                    last = mm(ps[:, 4 + i % 4, a * P:a * P + P], mixT[:, i, SEQ + a * P:SEQ + a * P + P], mixT[:, i, a * P:a * P + P],
                              start=True, stop=True)
                up(last, "a_done")
            eng.wait_ge(S("xkd_sb"), p.at("xkd_sb", 8))
            eng.wait_ge(S("a_sb"), p.at("a_sb", 8))
            for i, (d, h) in enumerate(STREAMS):
                for half in range(2):
                    for a in range(2):
                        mm(ps[:, h, half * SEQ + a * P:half * SEQ + a * P + P], vtok[:, a, h * SEQ + half * P:h * SEQ + half * P + P],
                           amask[:, i, a * P:a * P + P], start=d + half + a == 0, stop=False, skip_group_check=True)
            for st in range(4):
                for i, (d, h) in enumerate(STREAMS):
                    c = 3 - st if d else st
                    r, a, n = slice(64 * (c % 2), 64 * (c % 2) + 64), c // 2, 8 * st + i
                    if st:
                        eng.wait_ge(S("u_sb"), p.at("u_sb", n - 7))
                    for half in range(2):
                        last = mm(ps[:, h, half * SEQ + c * CHUNK:half * SEQ + c * CHUNK + CHUNK], state[:, i, half * P:half * P + P],
                                  mixT[:, i, c * CHUNK:c * CHUNK + CHUNK], start=False, stop=True, skip_group_check=True)
                    if st < 3:
                        if n >= 4:
                            eng.wait_ge(S("u_sb"), p.at("u_sb", n - 3))
                        up(mm(ps[:, 4 + n % 4, 0:SEQ], hT[r, i, SEQ + a * P:SEQ + a * P + P], vtok[r, a, h * SEQ:h * SEQ + SEQ],
                              start=True, stop=True), "u_done")
            up(last, "o_done")
            for h in range(GLA_HEADS):
                eng.wait_ge(S("hsq"), p.at("hsq", h + 1))
                for half in range(2):
                    last = mm(ps[:, 4 + h, 0:SEQ], onesPP, hT[:, h, half * SEQ:half * SEQ + SEQ], start=half == 0, stop=half == 1)
                up(last, "hsum")
            eng.wait_ge(S("mix_done"), p.at("mix_done", 4))

        def act_odd(eng, p):
            evacuated(eng, p)
            eng.wait_ge(S("lr_done"), p.at("lr_done", 1))
            up(act(lrT, ps[0:64, 0, :], ACT.Copy), "lr_sb")
            up(act(big3[:, 8:16, 0:SEQ], big3[:, 8:16, 0:SEQ], ACT.Silu), "r_silu")
            for d in range(2):
                eng.wait_ge(S("z_sb"), p.at("z_sb", 4 * d + 4))
                z, e = big3[:, 16 + 4 * d:20 + 4 * d, :], hT[:, 4 * d:4 * d + 4, :]
                alink(act(e, z, ACT.Abs))
                alink(act(e, e, ACT.Exp, scale=-1.0))
                up(act(e, e, ACT.Ln, bias=1.0), "la_ln")
            for i in range(8):
                eng.wait_ge(S("cums"), p.at("cums", i + 1))
                up(act(ckd[:, i, :], big3[:, 16 + i, SEQ:NT], ACT.Exp, bias=bend[:, i:i + 1], scale=-1.0 / GLA_TAU), "c_exp")
            for i in range(8):
                eng.wait_ge(S("ckd_T"), p.at("ckd_T", i + 1))
                up(act(ckdT[:, i, :], ps[:, i % 4, 0:SEQ], ACT.Copy), "ckd_sb")
            for i in range(8):
                b = big3[:, 16 + i, 0:SEQ]
                act(mixT[:, i, 0:SEQ], b, ACT.Exp, scale=1.0 / GLA_TAU)
                act(mixT[:, i, SEQ:NT], b, ACT.Exp, scale=-1.0 / GLA_TAU)
                for c in range(4):
                    cols = slice(c * CHUNK, (c + 1) * CHUNK)
                    act(hT[:, i, cols], b[:, cols], ACT.Exp, bias=blast[:, 4 * i + c:4 * i + c + 1], scale=-1.0 / GLA_TAU)
                up(act(eblast[:, 4 * i:4 * i + 4], blast[:, 4 * i:4 * i + 4], ACT.Exp), "x_exp")
            for i in range(8):
                eng.wait_ge(S("xkd_T"), p.at("xkd_T", i + 1))
                up(act(hT[:, i, SEQ:NT], ps[:, i % 4, 0:SEQ], ACT.Copy), "xkd_sb")
            for h in range(GLA_HEADS):
                eng.wait_ge(S("o_sb"), p.at("o_sb", h + 1))
                up(act(hT[:, h, :], big3[:, 4 + h, :], ACT.Square), "hsq")
            for h in range(GLA_HEADS):
                eng.wait_ge(S("hms"), p.at("hms", h + 1))
                up(act(hT[:, 4 + h, 0:SEQ], hT[:, 4 + h, 0:SEQ], ACT.Sqrt), "hrms")

        def dve_odd(eng, p):
            evacuated(eng, p)
            for i in range(8):
                eng.wait_ge(S("z_done"), p.at("z_done", i + 1))
                up(V.tensor_scalar(big3[:, 16 + i, :], ps[:, 1 + i % 4, :], cols2[:, GLA_B + i:GLA_B + i + 1], None, ALU.add), "z_sb")
            for d in range(2):
                eng.wait_ge(S("la_ln"), p.at("la_ln", d + 1))
                z, e = big3[:, 16 + 4 * d:20 + 4 * d, :], hT[:, 4 * d:4 * d + 4, :]
                link(V.scalar_tensor_tensor(z, z, 0.0, e, ALU.min, ALU.subtract))
                for h in range(GLA_HEADS):
                    i = 4 * d + h
                    back = slice(None, None, -1) if d else slice(None)
                    bc, bx = big3[:, 16 + i, SEQ:NT], big3[:, 16 + i, 0:SEQ]
                    V.tensor_tensor_scan(bc[:, back], ones[:, 0:SEQ], bc[:, back], 0.0, ALU.mult, ALU.add)
                    link(V.tensor_tensor_scan(bx[:, back], restart[:, d, :][:, back], bx[:, back], 0.0, ALU.mult, ALU.add))
                    end = bc[:, 0:1] if d else bc[:, SEQ - 1:SEQ]
                    ends = bx.rearrange("p (c k) -> p c k", k=CHUNK)[:, :, 0 if d else CHUNK - 1]
                    V.tensor_scalar(blast[:, 4 * i:4 * i + 4], ends, 1.0 / GLA_TAU, None, ALU.mult)
                    up(V.tensor_scalar(bend[:, i:i + 1], end, 1.0 / GLA_TAU, None, ALU.mult), "cums")
            for i, (d, h) in enumerate(STREAMS):
                eng.wait_ge(S("c_exp"), p.at("c_exp", i + 1))
                up(V.tensor_tensor(ckd[:, i, :], ckd[:, i, :], big3[:, 4 + h, SEQ:NT], ALU.mult), "ckd")
            for i in range(8):
                eng.wait_ge(S("st_done"), p.at("st_done", i + 1))
                up(V.tensor_copy(state[:, i, :], ps[:, 4 + i % 4, 0:SEQ]), "st_sb")
            link(V.memset(amask[:, :, :], 0.0))
            for i, (d, h) in enumerate(STREAMS):
                eng.wait_ge(S("x_exp"), p.at("x_exp", i + 1))
                V.scalar_tensor_tensor(mixT[:, i, 0:SEQ], big3[:, h, 0:SEQ], P ** -0.5, mixT[:, i, 0:SEQ], ALU.mult, ALU.mult)
                V.tensor_tensor(mixT[:, i, SEQ:NT], big3[:, 4 + h, 0:SEQ], mixT[:, i, SEQ:NT], ALU.mult)
                up(V.tensor_tensor(hT[:, i, 0:SEQ], big3[:, 4 + h, 0:SEQ], hT[:, i, 0:SEQ], ALU.mult), "x_in")
            for i, (d, h) in enumerate(STREAMS):
                eng.wait_ge(S("a_done"), p.at("a_done", i + 1))
                up(V.copy_predicated(amask[:, i, :].rearrange("p (a q) -> p a q", a=2),
                                     gmask[:, d, :].bitcast(U32).unsqueeze(1).broadcast_to([P, 2, P]),
                                     ps[:, 4 + i % 4, 0:SEQ].rearrange("p (a q) -> p a q", a=2)), "a_sb")
            for st in range(3):
                for i, (d, h) in enumerate(STREAMS):
                    c, n = 3 - st if d else st, 8 * st + i
                    eng.wait_ge(S("u_done"), p.at("u_done", n + 1))
                    up(V.scalar_tensor_tensor(state[:, i, :], state[:, i, :], eblast[:, 4 * i + c:4 * i + c + 1], ps[:, 4 + n % 4, 0:SEQ],
                                              ALU.mult, ALU.add), "u_sb")
            eng.wait_ge(S("o_done"), p.at("o_done", 1))
            for h in range(GLA_HEADS):
                up(V.tensor_copy(big3[:, 4 + h, :], ps[:, h, :]), "o_sb")
            for h in range(GLA_HEADS):
                eng.wait_ge(S("hsum"), p.at("hsum", h + 1))
                up(V.tensor_scalar(hT[:, 4 + h, 0:SEQ], ps[:, 4 + h, 0:SEQ], 1.0 / (2 * P), EPS, ALU.mult, ALU.add), "hms")
            eng.wait_ge(S("r_silu"), p.at("r_silu", 1))
            for h in range(GLA_HEADS):
                eng.wait_ge(S("hrms"), p.at("hrms", h + 1))
                rs = hT[:, 4 + h, 0:SEQ]
                link(V.reciprocal(rs, rs))
                for half in range(2):
                    o = mixT[:, 2 * h + half, 0:SEQ]
                    link(V.scalar_tensor_tensor(o, big3[:, 4 + h, half * SEQ:half * SEQ + SEQ], cols2[:, GLA_G + half:GLA_G + half + 1], rs,
                                                ALU.mult, ALU.mult))
                    last = V.tensor_tensor(o, o, big3[:, 8 + 2 * h + half, 0:SEQ], ALU.mult)
                up(last, "mix_done")

        def run(eng, stages):
            for p in phases:
                if p.kind in stages:
                    stages[p.kind](eng, p)

        @block.gpsimd
        def _(eng):
            run(eng, {"squares": pool_squares, "gemm": pool_gemm})

        @block.sync
        def _(eng):
            run(eng, {"setup": sp_setup, "load": sp_load, "fetch": sp_fetch, "mod": sp_mod, "gemm": sp_gemm, "store": sp_store})

        @block.tensor
        def _(eng):
            run(eng, {"setup": pe_setup, "load": pe_load, "mod": pe_mod, "norm": pe_norm, "gemm": pe_gemm,
                      "mix1": pe_mix1, "even": pe_even, "odd": pe_odd, "store": pe_store})

        @block.scalar
        def _(eng):
            run(eng, {"setup": act_setup, "load": act_load, "squares": act_squares, "feed": act_feed, "mixsplit": act_mixsplit, "norm": act_norm, "gemm": act_gemm,
                      "mix1": act_mix1, "even": act_even, "odd": act_odd, "store": act_store})

        @block.vector
        def _(eng):
            run(eng, {"setup": dve_setup, "load": dve_load, "feed": dve_feed, "mixsplit": dve_mixsplit, "mod": dve_mod, "modvec": dve_modvec, "norm": dve_norm,
                      "gemm": dve_gemm, "mix1": dve_mix1, "even": dve_even, "odd": dve_odd, "store": dve_store})

    for name, n in total.items():
        assert seen.get(name, 0) == n, (name, seen.get(name, 0), n)


INPUTS = ["x", "c", "ctx", "c_ctx", "w_mod", "b_mod", "g_pre", "g_post", "w_in", "w_out", "sink", "w_fourier", "conv_w",
          "conv_b", "c_2", "ctx_2", "c_ctx_2", "ada_w_2", "ada_b_2", "norm_g_2", "ffn_w_in_2", "ffn_w_out_2",
          "even_w_in_2", "even_w_out_2", "diff_lambda_2", "diff_norm_g_2", "mlstm_conv_w_2", "mlstm_conv_b_2",
          "mlstm_gate_b_2", "mlstm_norm_g_2", "odd_w_in_2", "odd_w_out_2", "gla_w_gate_2", "gla_b_gate_2",
          "gla_norm_g_2", "final_g_2"]


def dram_views(ap):
    v = dict(ap)
    for n in ("x", "ctx", "ctx_2"):
        v[n] = ap[n][0]
    for n in ("c", "c_2"):
        v[n] = ap[n][0].rearrange("(r p) -> r p", p=P)
    for n in ("c_ctx", "c_ctx_2", "final_g_2"):
        v[n] = ap[n].rearrange("(r p) -> r p", p=P)
    for n in ("g_pre", "g_post", "conv_b", "mlstm_conv_b_2", "diff_norm_g_2", "gla_norm_g_2"):
        v[n] = ap[n].rearrange("l (r p) -> (l r) p", p=P)
    for n in ("norm_g_2", "conv_w", "mlstm_conv_w_2"):
        v[n] = ap[n].rearrange("l s (r p) -> (l s r) p", p=P)
    v["mlstm_norm_g_2"] = ap["mlstm_norm_g_2"][0]
    v["gla_b_gate_2"] = ap["gla_b_gate_2"][0].rearrange("d (r p) -> (d r) p", p=P)
    v["gla_w_gate_2"] = ap["gla_w_gate_2"][0]
    v["sink"] = ap["sink"].rearrange("l h -> (l h)")
    v["diff_lambda_2"] = ap["diff_lambda_2"][0].rearrange("a b -> (a b)")
    v["mlstm_gate_b_2"] = ap["mlstm_gate_b_2"][0].rearrange("a (b o) -> (a b) o", o=1)
    wf = ap["w_fourier"].rearrange("l (c g) p n -> g p (l c) n", g=2)
    v["w_fourier"] = [wf[0], wf[1]]
    return v


def kernel(**inputs):
    import concourse.bacc as bacc
    from concourse.bass_utils import run_bass_kernel_spmd

    nc = bacc.Bacc("TRN2", target_bir_lowering=False, num_devices=1)
    arrays, aps = {}, {}
    for name in INPUTS:
        a = np.ascontiguousarray(inputs[name])
        arrays[f"in_{name}"] = a
        aps[name] = nc.dram_tensor(f"in_{name}", a.shape, mybir.dt.from_np(a.dtype), kind="ExternalInput").ap()
    arrays["in_const"] = np.ascontiguousarray(np.concatenate(list(CONST.values()), axis=1))
    const = nc.dram_tensor("in_const", (P, CONST_W), F32, kind="ExternalInput").ap()
    out = nc.dram_tensor("out_0", (1, SEQ, D), F32, kind="ExternalOutput").ap()
    build_program(nc, dram_views(aps), const, out[0])
    result = run_bass_kernel_spmd(nc, [arrays], core_ids=[0])
    return result.results[0]["out_0"]
```

```python
import math
from contextlib import ExitStack

import numpy as np

import concourse.bass as bass
from concourse import mybir

F32 = mybir.dt.float32
U32 = mybir.dt.uint32
F32R = mybir.dt.float32r
ALU = mybir.AluOpType
ACT = mybir.ActivationFunctionType
AX = mybir.AxisListType

P = 128
D = 1024
KC = D // P
SEQ = 256
CTX = 256
NT = SEQ + CTX
TT = NT // P
DEPTH = 2
EPS = 1e-6
BANK = 512

HD = 64
HEADS = 8
Q_PER_KV = 4
PROJ1 = 2816
D_FF = 2816
FC = D_FF // P
EVEN_IN = 3088
ODD_IN = 3104
DA_HEADS = 4
ML_HEADS = 4
GLA_HEADS = 4
CHUNK = 64
LAM_INIT = 0.8 - 0.6 * math.exp(-0.3 * 0)
GLA_TAU = 16.0

STAGE = 2
RING = 4
DEEP = 4
LEAD = 2
FH = FC // 2
SEG = 256
NEG = -1.0e30


def shape_constants():
    c = {}
    c["ident"] = np.eye(P, dtype=np.float32)
    freqs = HD // 4
    inv = np.power(np.float32(10000.0), -np.arange(freqs, dtype=np.float32) / np.float32(freqs)).astype(np.float32)
    t = np.arange(SEQ)
    pos = np.stack([t // 64, t % 64]).astype(np.float32)
    rope = np.zeros((P, 2, SEQ), np.float32)
    for p in range(P):
        axis, half, f = (p % 64) // 32, (p % 32) // 16, p % 16
        ang = (pos[axis] * inv[f]).astype(np.float32)
        rope[p, 0] = np.cos(ang)
        rope[p, 1] = np.sin(ang) * (-1.0 if half == 0 else 1.0)
    c["rope"] = rope.reshape(P, 2 * SEQ)
    a64 = 2 * np.pi * (np.outer(np.arange(64), np.arange(64)) % 64) / 64
    dftc = np.zeros((P, 2, P))
    for g in range(2):
        s = slice(64 * g, 64 * g + 64)
        dftc[s, 0, s] = np.cos(a64) / 8
        dftc[s, 1, s] = np.sin(a64) / 8
    c["dftc"] = dftc.reshape(P, 2 * P).astype(np.float32)
    an = 2 * np.pi * (np.outer(np.arange(SEQ), np.arange(SEQ)) % SEQ) / SEQ
    dftn = np.stack([np.cos(an), -np.sin(an)]) / 16
    c["dftn"] = dftn.reshape(2, 2, P, SEQ).transpose(2, 1, 0, 3).reshape(P, 4 * SEQ).astype(np.float32)
    q, k = np.arange(P)[:, None], np.arange(P)[None, :]
    c["wmask"] = np.stack([np.where(k <= q, 0, NEG), np.where(k >= q, 0, NEG)], 1).reshape(P, 2 * P).astype(np.float32)
    m = np.zeros((P, 2, 2, SEQ), np.float32)
    for tile in range(2):
        s = tile * P + np.arange(P)[:, None]
        tq = np.arange(SEQ)[None, :]
        m[:, 0, tile] = np.where(tq >= s, 0, NEG)
        m[:, 1, tile] = np.where(tq <= s, 0, NEG)
    c["mmask"] = m.reshape(P, 4 * SEQ)
    s, tq = np.arange(P)[:, None], np.arange(P)[None, :]
    same = s // CHUNK == tq // CHUNK
    c["gmask"] = np.stack([(tq >= s) & same, (tq <= s) & same], 1).astype(np.float32).reshape(P, 2 * P)
    r = np.ones((P, 2, SEQ), np.float32)
    r[:, 0, 0::CHUNK] = 0
    r[:, 1, CHUNK - 1::CHUNK] = 0
    c["restart"] = r.reshape(P, 2 * SEQ)
    return c


CONST = shape_constants()
CONST_COLS = {}
_at = 0
for _n, _a in CONST.items():
    CONST_COLS[_n] = (_at, _a.shape[1])
    _at += _a.shape[1]
CONST_W = _at


class Phase:

    def __init__(self, kind, rises, **kw):
        self.kind, self.rises, self.kw, self.start = kind, rises, kw, {}

    def at(self, name, k=0):
        return self.start.get(name, 0) + k


def gemm_rises(n, per, evac, fed, sumsq):
    r = {"unit_done": n * per, "w_hi": n * per - (0 if fed else LEAD)}
    r["w_ready"] = r["w_hi"]
    for j in range(4):
        r[f"bank_free{j}"] = len(range(j // 2, n, 2)) if evac == "tok" else len(range(j, n, 4))
    if evac == "swiglu":
        r["g_hi_ready"] = r["g_ready"] = n // 2
    if sumsq:
        r.update({"sq_ready": n, "sq_used": n - 1, "sums_clear": 1})
    return r


def plan():
    ph = []

    def add(kind, rises, **kw):
        ph.append(Phase(kind, rises, **kw))

    def gemm(w, col0, n, evac, tok=(0, NT), src="h", ks=(KC,), row0=0, fed=True, peel=False, sumsq=None, hper=0, order=tuple(range(KC)), **kw):
        per = 2 if evac == "tok" else len(ks)
        r = gemm_rises(n, per, evac, fed, sumsq)
        host = None
        if hper:
            host = dict(queue[0])
            segs = hper * (n // 4)
            queue[0]["seg0"] += segs
            if queue[0]["seg0"] == queue[0]["segs"]:
                queue.pop(0)
            assert not queue or queue[0]["seg0"] < queue[0]["segs"]
            r.update({"mod_rows": segs, "mod_cols": segs, "mod_sum0": segs // 2, "mod_sum1": segs // 2, "mod_kept": segs})
        add("gemm", r, hper=hper, host=host, order=order, w=w, col0=col0, n=n, evac=evac, tok=tok, src=src, ks=ks,
            per=per, step=2 if evac == "tok" else 4, row0=row0, fed=fed, peel=peel or not fed, sumsq=sumsq, **kw)

    def squares(nt, after):
        add("squares", {"sq_ready": KC, "sq_used": KC - 1, "sums_clear": 1}, nt=nt, after=after)

    def norm(mode, nt, n=0, **kw):
        r = {"ms_sum": 1, "rms_ready": 1, "diag_ready": nt // SEQ, "rstd_ready": nt // SEQ}
        if mode == "pre":
            r.update({"t_ready": KC, "hi_ready": KC, "h_ready": KC})
        else:
            r["normed"] = KC * (nt // SEQ)
        add("norm", r, mode=mode, nt=nt, n=n, **kw)

    def feed():
        add("feed", {"w_hi": LEAD, "w_ready": LEAD})

    out_rises = {"hi_ready": KC, "h_ready": KC, "w_hi": LEAD, "w_ready": LEAD}

    queue = [dict(block=b, l=l, seg0=0, segs=(3, 9)[b] * D // SEG) for b in range(2) for l in range(DEPTH)]

    def mod(segs):
        m = dict(queue[0])
        queue[0]["seg0"] += segs
        add("mod", {"mod_rows": segs, "mod_cols": segs, "mod_sum0": segs // 2, "mod_sum1": segs // 2,
                    "mod_kept": segs}, host=None, n=segs, **m)

    def modvec(block, l, parts=(0,)):
        add("modvec", {"mod_ready": 1}, block=block, l=l, parts=parts)

    add("setup", {"rows_T": 1, "rows_sb": 1, "s_ready": 2})
    add("load", {"tokens_T": 8, **{f"bank_free{b}": 1 for b in range(8)}}, which=0)
    squares(NT, "load")
    for l in range(DEPTH):
        both = l < DEPTH - 1
        nt = NT if both else SEQ
        if l == 0:
            mod(2 * D // SEG)
            feed()
            modvec(0, l, (0,))
            add("constants", {"rows_T": 1, "rows_sb": 1})
        else:
            modvec(0, l, (0, 1))
        norm("pre", NT, block=0, l=l, n=0)
        if both:
            gemm(("w_in", l), 0, 4, "copy", dst=0)
            gemm(("w_in", l), 512, 4, "copy", dst=4, hper=4)
            gemm(("w_in", l), 1024, 6, "copy", dst=8, hper=4)
            add("gates", {"gates_done": 1}, nt=nt)
            gemm(("w_in", l), 1792, 8, "copy", dst=14, fed=False, hper=2)
        else:
            gemm(("w_in", l), 0, 4, "copy", tok=(0, nt), dst=0)
            add("fetch", {})
            gemm(("w_in", l), 512, 2, "copy", dst=4)
            gemm(("w_in", l), 768, 8, "copy", tok=(0, nt), dst=6, hper=2)
            add("gates", {"gates_done": 1}, nt=nt)
            gemm(("w_in", l), 1792, 8, "copy", tok=(0, nt), dst=14, fed=False, hper=2)
        tiles = TT if both else 2
        na, sets = 8 * tiles, tiles // 2
        add("mix1", {"v_T": 1, "v_sb": 1, "k_swapped": 1, "roped": 1, "gates_done": 1, "scores_ready": na, "negmax_ready": na,
                     "probs_raw": na, "probsT_done": na, "probsT_sb": na, "pv_done": na, "sink_args": tiles, "sink_exp": tiles,
                     "att_kept": tiles, "att_T": 4, "att_gated": 4, "dft1": 2 * sets, "dft1_sb": 2 * sets, "dft2": 2, "dft2_sb": 2,
                     "dft3": 2, "dft3_gated": 2, "conv_done": 1, **out_rises}, l=l, both=both)
        gemm(("w_out", l), 0, 8, "copy", tok=(0, nt), dst=0, sumsq="big", hper=2, order=(4, 5, 6, 7, 0, 1, 2, 3))
        if both:
            modvec(0, l, (1,))
        norm("post", nt, block=0, l=l)
        if both:
            squares(nt, "post")
    add("load", {"tokens_T": 8, **{f"bank_free{b}": 1 for b in range(8)}}, which=1)
    squares(NT, "load")
    for l in range(DEPTH):
        last = l == DEPTH - 1
        modvec(1, l, (0,) if l == 0 else (0, 1, 2))

        def ffn(i, nt, hpers):
            norm("pre", nt, block=1, l=l, n=2 * i)
            for half in range(2):
                gemm(("ffn_w_in_2", l, i), half * FH * P, 2 * FH, "swiglu", tok=(0, nt), hper=hpers[2 * half])
                gemm(("ffn_w_out_2", l, i), 0, KC, "resid", tok=(0, nt), src="g", ks=(6, 5), row0=half * FH, l=l, g=2 * i,
                     sumsq="resid" if half else None, fed=not (last and i and half), peel=i and half, hper=hpers[2 * half + 1])

        if l == 0:
            ffn(0, NT, (2, 2, 2, 0))
            modvec(1, 0, (1, 2))
        else:
            ffn(0, NT, (0, 0, 0, 0))
        norm("pre", NT, block=1, l=l, n=1)
        w = ("even_w_in_2", 0) if l == 0 else ("odd_w_in_2", 0)
        if l == 0:
            gemm(w, 0, 8, "copy", dst=0)
            add("rotary", {"roped2": 1, "lam_e": 1}, half=0)
            gemm(w, 1024, 2, "tok", dst="vda")
            add("rotary", {"roped2": 1}, half=1)
            gemm(w, 1536, 4, "copy", dst=8)
            add("presplit", {"small_hi": 1, "small_lo": 1, "lam_ready": 1}, l=l)
            gemm(w, 2048, 2, "tok", dst="vm")
            add("rows", {"gate_rows": 1, "gate_bias": 1, "gate_ln": 1, "rows_ready": 1})
            gemm(w, 2560, 4, "copy", dst=12, fed=False)
            add("even", {"scores_ready": 32, "negmax_ready": 16, "probs_raw": 32, "probs_ready": 16, "probsT_done": 16, "probsT_sb": 16,
                         "pv_done": 16, "att_evac": 16, "att_sq": 16, "conv_lin": 1, "conv_silu": 1, "ones_set": 1,
                         "acol_T": 1, "acol_sb": 1, "ecol_sb": 1, "bcast": 8, "args": 8, "decay": 8, "qk_done": 4, "weighted": 8,
                         "numden": 8, "mem_done": 8, "roots": 2, "rstds": 2, "att_normed": 1, "mem_normed": 4,
                         "att_T": 4, "mem_T": 4, "osig": 1, "mem_gated": 4, **out_rises}, l=l)
            gemm(("even_w_out_2", 0), 0, 8, "resid", l=l, g=1, sumsq="resid")
        else:
            add("presplit", {"small_hi": 1, "small_lo": 1}, l=l)
            gemm(w, 0, 4, "copy", tok=(0, SEQ), dst=0)
            add("decay_gates", {"lr_done": 1, "lr_sb": 1, "z_done": 8, "z_sb": 8})
            gemm(w, 512, 4, "copy", dst=4)
            gemm(w, 1024, 2, "tok", dst="vtok", dst0=0, decays=0)
            ph[-1].rises.update({"la_ln": 1, "decayed": 1})
            gemm(w, 1536, 2, "tok", dst="vtok", dst0=2, decays=1)
            ph[-1].rises.update({"la_ln": 1, "decayed": 1})
            gemm(w, 2048, 8, "copy", tok=(0, SEQ), dst=8, fed=False)
            add("odd", {"cums": 8, "c_exp": 8, "ckd": 8, "ckd_T": 8, "ckd_sb": 8, "st_done": 8, "st_sb": 8, "masked": 1,
                        "x_exp": 8, "e_exp": 1, "x_in": 8, "xkd_T": 8, "xkd_sb": 8, "a_done": 8, "a_sb": 8,
                        "u_done": 24, "u_sb": 24, "o_done": 4, "r_silu": 1, "o_sq": 8, "o_roots": 1, "o_normed": 4, "o_T": 4,
                        "o_gated": 8, **out_rises}, l=l)
            gemm(("odd_w_out_2", 0), 0, 8, "resid", tok=(0, SEQ), l=l, g=1, sumsq="resid")
        ffn(1, SEQ if last else NT, (0, 0, 0, 0) if last else (2, 4, 2, 4))
    norm("final", SEQ)
    add("store", {"out_T": 4, "out_sb": 4})
    total = {}
    for p in ph:
        p.start = dict(total)
        for k, v in p.rises.items():
            total[k] = total.get(k, 0) + v
    return ph, total


def build_program(nc, t, const, out):
    phases, total = plan()
    seen = {}
    with ExitStack() as stack:
        def sb(name, shape, dt=F32):
            return stack.enter_context(nc.sbuf_tensor(name, shape, dt))

        sizes = {"resid": KC * NT, "big": 24 * NT, "hT": KC * NT, "mixT": KC * NT, "vtok": TT * D + TT * ML_HEADS, "stage": STAGE * KC * P,
                 "scr": 2 * RING * KC * P, "modw": 2 * KC * SEG,
                 "wfbd": 4 * P, "svec": 2 * KC * 32}
        base_of = {}
        end = -(-nc.sbuf_base // 32) * 32
        for name, n in sizes.items():
            base_of[name] = end
            end += 4 * n
        sb("stretch", [P, sum(sizes.values())])

        def over(name, base, at, shape, dt=F32):
            return nc.alloc_sbuf_tensor_at(name, shape, dt, offset=base_of[base] + 4 * at)

        resid = over("resid", "resid", 0, [P, KC, NT])
        big = over("big", "big", 0, [P, 24 * NT])
        big3 = big[:, :].rearrange("p (c n) -> p c n", n=NT)
        vtok = over("vtok", "vtok", 0, [P, TT, D])
        vda = over("vda", "vtok", 0, [P, TT, 4, P])
        vm = over("vm", "vtok", TT * 4 * P, [P, TT, 4, P + 1])
        hT = over("hT", "hT", 0, [P, KC, NT])
        mixT = over("mixT", "mixT", 0, [P, KC, NT])
        stage = over("stage", "stage", 0, [P, STAGE, KC, P])
        scr = over("scr", "scr", 0, [P, 2 * RING * KC * P])
        modw = over("modw", "modw", 0, [P, 2, KC, SEG])
        deep = over("deep", "modw", 0, [P, DEEP, KC, P])

        wgate_p = [over(f"wgate_{n}", "big", (20 + 2 * i) * NT, [P, KC, P], F32R) for i, n in enumerate(("hi", "lo"))]
        wlr_p = [over(f"wlr_{n}", at, 0, [P, KC, 64], F32R) for n, at in (("hi", "wfbd"), ("lo", "svec"))]

        h_hi = over("h_hi", "hT", 0, [P, KC, NT], F32R)
        h_lo = over("h_lo", "mixT", 0, [P, KC, NT], F32R)
        g_hi = over("g_hi", "big", 0, [P, 12, NT], F32R)
        g_lo = over("g_lo", "big", 12 * NT, [P, 12, NT], F32R)
        w_hi = over("w_hi", "scr", 0, [P, RING, KC, P], F32R)
        w_lo = over("w_lo", "scr", 4096, [P, RING, KC, P], F32R)
        modb = sb("modb", [P, 2, SEG])
        modr = sb("modr", [P, 2, SEG])
        cst = sb("cst", [P, CONST_W])
        rows1 = sb("rows1", [120, P])
        rows2 = sb("rows2", [47, P])
        cols1 = sb("cols1", [P, 120])
        cols2 = sb("cols2", [P, 47])
        svec = over("svec", "svec", 0, [P, 2, KC, 32])
        modT = [sb(f"modT{i}", [P, 24 if i < 2 else 72, 2]) for i in range(4)]
        modA = [sb(f"modA{i}", [P, 2 if i < 2 else 6, KC, 2]) for i in range(4)]
        ps = stack.enter_context(nc.psum_tensor("ps", [P, 8, BANK], F32))
        epsc = sb("epsc", [P, 1])
        work = vtok[:, :, :].rearrange("p a d -> p (a d)")
        sq = work[:, 0:1024].rearrange("p (s n) -> p s n", n=NT)
        sqsum, diag = work[:, 1024:1536], work[:, 1536:2048]
        sg = work[:, 2560:3584].rearrange("p (s n) -> p s n", n=NT)
        gt = work[:, 3584:4096]
        tnorm = work[:, 2560:4096].rearrange("p (s n) -> p s n", n=NT)

        def rstd_of(v):
            return ps[:, 6 + v, 0:SEQ]

        ones = sb("ones", [P, SEQ])
        wfbd = over("wfbd", "wfbd", 0, [P, 4, P])
        sinkb = sb("sinkb", [P, DEPTH * HEADS])
        nsink = sb("nsink", [P, DEPTH * HEADS])
        dlam = sb("dlam", [P, 4 * HD])
        small = sb("small", [P, 256])
        wgate = sb("wgate", [P, KC, P])
        gateb = sb("gateb", [64, 2])
        wlr = sb("wlr", [P, KC, 64])
        wgla = sb("wgla", [64, GLA_HEADS * P])

        sems = {}

        def S(name):
            if name not in sems:
                sems[name] = stack.enter_context(nc.semaphore(name))
            return sems[name]

        def up(ins, name, times=1, by=1):
            seen[name] = seen.get(name, 0) + times * by
            return ins.then_inc(S(name), by)

        def C(name):
            a, n = CONST_COLS[name]
            return cst[:, a:a + n]

        for n in list(total) + ["consts_in", "rows_in", "tokens_in", "zeroed", "eps_set", "dve_chain", "act_chain", "pool_chain", "out_written"]:
            S(n)
        w_full = [S(f"w_full{s}") for s in range(STAGE)]
        deep_full = [S(f"deep_full{s}") for s in range(DEEP)]
        first_deep = next(p.at("unit_done") for p in phases if p.kind == "gemm" and p.at("mod_rows") == total["mod_rows"])
        mod_full = [S(f"mod_full{s}") for s in range(2)]
        ident = C("ident")
        ropeC, ropeS = C("rope")[:, 0:SEQ], C("rope")[:, SEQ:2 * SEQ]
        dftn = C("dftn").rearrange("p (t c n) -> p t c n", t=2, c=2)
        wmask = C("wmask").rearrange("p (t k) -> p t k", t=2)
        mmask = C("mmask").rearrange("p (d t k) -> p d t k", d=2, t=2)
        gmask = C("gmask").rearrange("p (d k) -> p d k", d=2)
        restart = C("restart").rearrange("p (d k) -> p d k", d=2)
        onesPP = ones[:, 0:P]
        xstage = vtok[:, :, :]

        G_PRE, G_POST, NORM_G, FINAL_G = 32, 48, 64, 112
        CONV_W, CONV_B, MCONV_W, MCONV_B, DIFF_G, ML_G, GLA_G, GLA_B = 0, 12, 16, 28, 32, 33, 37, 39
        SWAP16 = [i ^ 16 for i in range(32)]

        block = stack.enter_context(nc.Block())

        def weight(key):
            w = t[key[0]]
            for i in key[1:]:
                w = w[i]
            return w

        def evacuated(eng, p):
            for b in range(8):
                if p.at(f"bank_free{b}"):
                    eng.wait_ge(S(f"bank_free{b}"), p.at(f"bank_free{b}"))
            for name in ("mod_sum0", "mod_sum1", "mod_kept"):
                if p.at(name):
                    eng.wait_ge(S(name), p.at(name))

        def turns(eng, n, step, peel=False):
            full = n // step
            if peel and n % step == 0:
                full -= 1
            if full > 1:
                with eng.Fori(0, full) as i:
                    yield i, range(step), full
            elif full == 1:
                yield 0, range(step), 1
            if n - full * step:
                yield full, range(n - full * step), 1

        def pairs(eng, segs):
            yield 0, 1
            with eng.Fori(1, segs // 2) as i:
                yield i, segs // 2 - 1

        def hosted(p, j, js):
            k = p.kw
            every = k["step"] // k["hper"] if k["hper"] else 0
            return j // every if every and len(js) == k["step"] and j % every == 0 else None

        def arrival(u, i=0, turn=0):
            if u < first_deep:
                return stage[:, u % STAGE], w_full[u % STAGE], i * (16 * turn // STAGE) + (16 * (u // STAGE) + 16), STAGE
            v = u - first_deep
            return deep[:, v % DEEP], deep_full[v % DEEP], i * (16 * turn // DEEP) + (16 * (v // DEEP) + 16), DEEP

        def splits(p, i, j, rounds):
            k = p.kw
            for s in range(k["per"]):
                x = j * k["per"] + s + LEAD
                if rounds > 1 or k["fed"] or i * k["step"] * k["per"] + x < k["n"] * k["per"]:
                    yield x

        def vectors(eng, rows, parts):
            k = 0
            for name, n in parts:
                eng.dma_start(rows[k:k + n, :], t[name]).then_inc(S("rows_in" if rows is rows1 else "consts_in"), 16)
                k += n

        def sp_setup(eng, p):
            vectors(eng, rows1, ROWS1)
            eng.dma_start(ident, const[:, 0:P]).then_inc(S("rows_in"), 16)
            for i, n in enumerate(("x", "ctx")):
                eng.dma_start(xstage[:, 2 * i:2 * i + 2, :], t[n].rearrange("(a p) d -> p a d", p=P)).then_inc(S("tokens_in"), 16)
            eng.wait_ge(S("zeroed"), ZEROED)
            first = next(q for q in phases if q.kind == "mod")
            for x in range(2):
                sp_segment(eng, first, 0, 2, x)

        def act_loads(eng):
            eng.dma_start(cst[:, P:], const[:, P:]).then_inc(S("consts_in"), 16)
            vectors(eng, rows2, ROWS2)
            eng.dma_start(sinkb[:, :], t["sink"].partition_broadcast(P)).then_inc(S("consts_in"), 16)
            eng.dma_start(dlam[:, :], t["diff_lambda_2"].partition_broadcast(P)).then_inc(S("consts_in"), 16)
            eng.wait_ge(S("zeroed"), ZEROED)
            for g in range(2):
                eng.dma_start(wfbd[64 * g:64 * g + 64, :, 64 * g:64 * g + 64], t["w_fourier"][g]).then_inc(S("consts_in"), 16)
            evw = t["even_w_in_2"][0].rearrange("(k p) n -> p k n", p=P)
            for g in range(2):
                for d in range(2):
                    at = 3072 + 8 * g + 4 * d
                    eng.dma_start(wgate[:, :, 64 * g + 32 * d:64 * g + 32 * d + 4], evw[:, :, at:at + 4],
                                  allow_slow_non_contiguous=True).then_inc(S("consts_in"), 16)
                    eng.dma_start(gateb[32 * d:32 * d + 4, g:g + 1], t["mlstm_gate_b_2"][8 * g + 4 * d:8 * g + 4 * d + 4, :],
                                  allow_slow_non_contiguous=True).then_inc(S("consts_in"), 16)
            odw = t["odd_w_in_2"][0].rearrange("(k p) n -> p k n", p=P)
            for d in range(2):
                eng.dma_start(wlr[:, :, 32 * d:32 * d + 16], odw[:, :, 3072 + 16 * d:3088 + 16 * d]).then_inc(S("consts_in"), 16)
                eng.dma_start(wgla[32 * d:32 * d + 16, :], t["gla_w_gate_2"][d]).then_inc(S("consts_in"), 16)

        ROWS1 = (("c", 8), ("c_ctx", 8), ("c_2", 8), ("c_ctx_2", 8), ("g_pre", 16), ("g_post", 16), ("norm_g_2", 48), ("final_g_2", 8))
        ROWS2 = (("conv_w", 12), ("conv_b", 4), ("mlstm_conv_w_2", 12), ("mlstm_conv_b_2", 4),
                 ("diff_norm_g_2", 1), ("mlstm_norm_g_2", 4), ("gla_norm_g_2", 2), ("gla_b_gate_2", 8))
        CONST_LOADS = 1 + len(ROWS2) + 2 + 2 + 8 + 4
        ZEROED = 6

        def sp_segment(eng, p, i, per_turn, x):
            m = p.kw["host"] or p.kw
            blk, l = m["block"], m["l"]
            w = (t["w_mod"], t["ada_w_2"])[blk][l].rearrange("(k p) n -> p k n", p=P)
            b = (t["b_mod"], t["ada_b_2"])[blk]
            par = x % 2
            cols = bass.ds((i * per_turn + (m["seg0"] + x)) * SEG, SEG)
            before = p.at(f"mod_sum{par}") + x // 2
            if before or not isinstance(i, int):
                eng.wait_ge(S(f"mod_sum{par}"), i * (per_turn // 2) + before)
            eng.dma_start(modw[:, par], w[:, :, cols]).then_inc(mod_full[par], 16)
            eng.dma_start(modb[0:2, par, :], b[l:l + 1, cols].broadcast_to([2, SEG])).then_inc(mod_full[par], 16)

        def sp_mod(eng, p):
            for i, _ in pairs(eng, p.kw["n"]):
                if isinstance(i, int):
                    continue
                for x in range(2):
                    sp_segment(eng, p, i, 2, x)

        def sp_fetch(eng, p):
            eng.wait_ge(S("normed"), p.at("normed"))
            for a in range(2):
                eng.dma_start(big3[:, 6 + 4 * a:10 + 4 * a, SEQ:NT], t["ctx_2"][a * P:(a + 1) * P, :]
                              .rearrange("p (c n) -> p c n", n=SEQ)).then_inc(S("tokens_in"), 16)

        def sp_gemm(eng, p):
            k = p.kw
            w, ks, u0, per, step = weight(k["w"]), k["ks"], p.at("unit_done"), k["per"], k["step"]
            w3 = w.rearrange("(k p) n -> p k n", p=P)
            if u0 == first_deep:
                eng.wait_ge(S("mod_rows"), total["mod_rows"])
            for i, js, _ in turns(eng, k["n"], step):
                for j in js:
                    x = hosted(p, j, js)
                    if x is not None:
                        sp_segment(eng, p, i, k["hper"], x)
                    for s in range(per):
                        u = u0 + j * per + s
                        slot, full, _, again = arrival(u)
                        if u >= STAGE:
                            eng.wait_ge(S("w_ready"), i * (step * per) + (u - again + 1))
                        rows = slice(k["row0"], k["row0"] + KC)
                        if k["evac"] == "swiglu":
                            col = i * (2 * P) + (k["col0"] + (j // 2) * P + (j % 2) * D_FF)
                        elif k["evac"] == "tok":
                            col = i * (4 * P) + (k["col0"] + (2 * j + s) * P)
                        else:
                            col = i * (4 * P) + (k["col0"] + j * P)
                            first = k["row0"] + sum(ks[:s])
                            rows = slice(first, first + ks[s])
                        eng.dma_start(slot[:, 0:rows.stop - rows.start, :], w3[:, rows, bass.ds(col, P)]).then_inc(full, 16)

        def sp_store(eng, p):
            for tile in range(2):
                for half in range(2):
                    eng.wait_ge(S("out_sb"), 2 * tile + half + 1)
                    eng.dma_start(out[tile * P:(tile + 1) * P, half * 512:half * 512 + 512],
                                  vtok[:, tile, half * 512:half * 512 + 512]).then_inc(S("out_written"), 16)
            eng.wait_ge(S("out_written"), 64)

        mm, tr = nc.tensor.matmul, nc.tensor.transpose

        def pe_setup(eng, p):
            eng.wait_ge(S("rows_in"), 16 * (len(ROWS1) + 1))
            up(tr(ps[:, 0, 0:120], rows1[:, :], ident[0:120, 0:120]), "rows_T")

        def pe_constants(eng, p):
            eng.wait_ge(S("consts_in"), 16 * CONST_LOADS)
            eng.wait_ge(S("tokens_T"), p.at("tokens_T"))
            evacuated(eng, p)
            up(tr(ps[:, 1, 0:47], rows2[:, :], ident[0:47, 0:47]), "rows_T")

        def pe_load(eng, p):
            which = p.kw["which"]
            eng.wait_ge(S("tokens_in"), 32 + 32 * which)
            if which == 0:
                eng.wait_ge(S("rows_sb"), 1)
            else:
                eng.wait_ge(S("normed"), p.at("normed"))
            evacuated(eng, p)
            for c in range(KC):
                tiles = range(4) if which == 0 else (2, 3)
                for a in tiles:
                    if which == 0:
                        tokens = xstage[:, a, c * P:(c + 1) * P]
                    else:
                        tokens = big3[:, 6 + 4 * (a - 2) + c // 2, SEQ + (c % 2) * P:SEQ + (c % 2) * P + P]
                    last = tr(ps[:, c, a * P:(a + 1) * P], tokens, ident)
                up(last, "tokens_T")

        def pe_rows(eng, p, i, per_turn, x, rounds):
            m = p.kw["host"] or p.kw
            par = x % 2
            eng.wait_ge(mod_full[par], i * (16 * per_turn) + (16 * p.at("mod_rows") + 32 * (x // 2) + 32))
            if p.at(f"mod_sum{par}") + x // 2 or not isinstance(i, int):
                eng.wait_ge(S(f"mod_sum{par}"), i * (per_turn // 2) + (p.at(f"mod_sum{par}") + x // 2))
            for k in range(KC):
                j = k % 4
                last = mm(ps[32 * j:32 * j + 32, 4 + par, 0:SEG], svec[:, m["block"], k, :], modw[:, par, k, :], start=k < 4, stop=k >= 4)
            up(last, "mod_rows", rounds)

        def pe_cols(eng, p, i, per_turn, x, rounds):
            par = x % 2
            eng.wait_ge(S(f"mod_sum{par}"), i * (per_turn // 2) + (p.at(f"mod_sum{par}") + x // 2 + 1))
            if p.at("mod_kept") + x or not isinstance(i, int):
                eng.wait_ge(S("mod_kept"), i * per_turn + (p.at("mod_kept") + x))
            for c in range(2):
                last = tr(ps[:, 6, c * P:(c + 1) * P], modr[:, par, c * P:(c + 1) * P], ident)
            up(last, "mod_cols", rounds)

        def pe_mod(eng, p):
            segs = p.kw["n"]
            eng.wait_ge(S("s_ready"), 2)
            evacuated(eng, p)
            for i, rounds in pairs(eng, segs):
                for x in range(2):
                    pe_rows(eng, p, i, 2, x, rounds)
                for x in range(2):
                    pe_cols(eng, p, i, 2, x, rounds)

        def pe_norm(eng, p):
            nt = p.kw["nt"]
            for name in ("mod_sum1", "mod_kept"):
                if p.at(name):
                    eng.wait_ge(S(name), p.at(name))
            eng.wait_ge(S("sq_used"), p.at("sq_used"))
            for a in range(nt // P):
                mm(ps[:, 5, a * 64:(a + 1) * 64], sqsum[:, a * P:(a + 1) * P], ones[:, 0:64], start=a == 0, stop=False, skip_group_check=True)
            eng.wait_ge(S("sq_ready"), p.at("sq_ready"))
            for a in range(nt // P):
                last = mm(ps[:, 5, a * 64:(a + 1) * 64], sq[:, (KC - 1) % 2, a * P:(a + 1) * P], ones[:, 0:64],
                          start=False, stop=True, skip_group_check=True)
            up(last, "ms_sum")
            for v in range(nt // SEQ):
                eng.wait_ge(S("diag_ready"), p.at("diag_ready", v + 1))
                up(mm(rstd_of(v), onesPP, diag[:, v * SEQ:(v + 1) * SEQ], start=True, stop=True), "rstd_ready")

        W_X = (("hi", "hi"), ("hi", "lo"), ("lo", "hi"))

        def pe_gemm(eng, p):
            k = p.kw
            a, b = k["tok"]
            ks, u0, per, step, evac = k["ks"], p.at("unit_done"), k["per"], k["step"], k["evac"]
            w_part = {"hi": w_hi, "lo": w_lo}
            x_part = {"hi": h_hi, "lo": h_lo} if k["src"] == "h" else {"hi": g_hi, "lo": g_lo}
            x_ready, x_chunks = ("h_ready", KC) if k["src"] == "h" else ("g_ready", FH)
            def weights(i, u):
                eng.wait_ge(S("w_ready"), i * (step * per) + (u + 1))

            order = k["order"]

            def operand(n):
                eng.wait_ge(S(x_ready), p.at(x_ready) - x_chunks + n + 1)

            def chunk(j, u, c, x, first, final):
                for wp, xp in W_X:
                    last = mm(ps[:, j, 0:b - a], w_part[wp][:, u % RING, c, :], x_part[xp][:, x, a:b],
                              start=first and wp == xp, stop=final and wp == "lo")
                return last

            def product(i, j, rounds):
                for s, kc in enumerate(ks):
                    u = u0 + j * per + s
                    weights(i, u)
                    if s == 0:
                        eng.wait_ge(S(f"bank_free{j}"), p.at(f"bank_free{j}") + i)
                    for n in range(kc):
                        c = order[n] if per == 1 else n
                        x = sum(ks[:s]) + c
                        if j == 0:
                            operand(sum(ks[:s]) + n)
                        last = chunk(j, u, c, x, s + n == 0, s == per - 1 and n == kc - 1)
                    up(last, "unit_done", rounds)

            def product_pair(i, rounds):
                for j in range(2):
                    weights(i, u0 + j)
                    eng.wait_ge(S(f"bank_free{j}"), p.at(f"bank_free{j}") + i)
                for n, x in enumerate(order):
                    operand(n)
                    for j in range(2):
                        last = chunk(j, u0 + j, x, x, n == 0, n == KC - 1)
                        if n == KC - 1:
                            up(last, "unit_done", rounds)

            def token_pair(i, j, rounds):
                u = u0 + 2 * j
                weights(i, u)
                weights(i, u + 1)
                operand(KC - 1)
                for tile in range(TT):
                    bank = 2 * j + tile // 2
                    if tile % 2 == 0:
                        eng.wait_ge(S(f"bank_free{bank}"), p.at(f"bank_free{bank}") + i)
                    for c in range(KC):
                        for wp, xp in W_X:
                            last = mm(ps[:, bank, (tile % 2) * SEQ:(tile % 2) * SEQ + SEQ], x_part[xp][:, c, tile * P:(tile + 1) * P],
                                      w_part[wp][:, u % RING:u % RING + 2, c, :], start=c == 0 and wp == xp, stop=c == KC - 1 and wp == "lo")
                up(last, "unit_done", rounds, by=2)

            for i, js, rounds in turns(eng, k["n"], step):
                paired = evac != "tok" and per == 1 and len(js) >= 2
                for j in js:
                    x = hosted(p, j, js)
                    if x is not None:
                        pe_rows(eng, p, i, k["hper"], x, rounds)
                    if evac == "tok":
                        token_pair(i, j, rounds)
                    elif paired and j < 2:
                        if j == 0:
                            product_pair(i, rounds)
                    else:
                        product(i, j, rounds)
                    if x is not None:
                        pe_cols(eng, p, i, k["hper"], x, rounds)

        def pe_store(eng, p):
            eng.wait_ge(S("normed"), p.at("normed"))
            for tile in range(2):
                for half in range(2):
                    for c in range(4):
                        last = tr(ps[:, 2 * tile + half, c * P:(c + 1) * P], hT[:, half * 4 + c, tile * P:(tile + 1) * P], ident)
                    up(last, "out_T")

        chain = {"dve": 0, "act": 0, "pool": 0}
        act = nc.scalar.activation

        def alink(ins):
            chain["act"] += 1
            ins.then_inc(S("act_chain"), 1)
            nc.scalar.wait_ge(S("act_chain"), chain["act"])

        def act_setup(eng, p):
            eng.wait_ge(S("zeroed"), ZEROED)
            eng.wait_ge(S("eps_set"), 1)
            eng.wait_ge(S("rows_sb"), 1)
            for blk in range(2):
                up(act(svec[:, blk, :, 0:2], cols1[:, 16 * blk:16 * blk + 16].rearrange("p (v k) -> p k v", v=2), ACT.Silu), "s_ready")
            act_loads(eng)

        def act_load(eng, p):
            a = 0 if p.kw["which"] == 0 else SEQ
            for c in range(1, KC, 2):
                eng.wait_ge(S("tokens_T"), p.at("tokens_T", c + 1))
                up(act(resid[:, c, a:NT], ps[:, c, a:NT], ACT.Copy), f"bank_free{c}")

        def act_squares(eng, p):
            nt = p.kw["nt"]
            if p.kw["after"] == "load":
                eng.wait_ge(S("tokens_T"), p.at("tokens_T"))
            if p.kw["after"] == "post" or p.at("normed"):
                eng.wait_ge(S("normed"), p.at("normed") - (KC * (nt // SEQ) if p.kw["after"] == "post" else 0))
            for c in range(KC):
                if p.kw["after"] == "load":
                    eng.wait_ge(S(f"bank_free{c}"), p.at(f"bank_free{c}"))
                else:
                    eng.wait_ge(S("normed"), p.at("normed") + (c + 1 - KC) * (nt // SEQ))
                act_square(eng, p, resid[:, c, 0:nt], 0, c, 1)

        def act_square(eng, p, src, i, j, rounds):
            if p.at("sq_used") + j >= 2:
                eng.wait_ge(S("sq_used"), i * 4 + (p.at("sq_used") + j - 1))
            up(act(sq[:, j % 2, 0:src.shape[-1]], src, ACT.Square), "sq_ready", rounds)

        def act_norm(eng, p):
            nt, mode = p.kw["nt"], p.kw["mode"]
            rms = small[:, 204:204 + nt // P]
            act(small[:, 212:213], epsc[:, :], ACT.Sqrt)
            eng.wait_ge(S("ms_sum"), p.at("ms_sum", 1))
            up(act(rms, ps[:, 5, 0:nt // 2:64], ACT.Sqrt, scale=1.0 / D, bias=epsc[:, :]), "rms_ready")
            if mode == "pre":
                m = 2 * p.kw["block"] + p.kw["l"]
                for c in range(KC):
                    eng.wait_ge(S("t_ready"), p.at("t_ready", c + 1))
                    for v in range(nt // SEQ):
                        sh = modT[m][:, p.kw["n"] * 24 + c, v:v + 1]
                        cols = slice(v * SEQ, (v + 1) * SEQ)
                        last = act(h_hi[:, c, cols], tnorm[:, c % 3, cols], ACT.Identity, bias=sh, scale=1.0)
                    up(last, "hi_ready")

        def act_split(eng, u, i=0, turn=0, rounds=1):
            slot, full, arrived, _ = arrival(u, i, turn)
            eng.wait_ge(full, arrived)
            if u >= RING:
                eng.wait_ge(S("unit_done"), i * turn + (u - RING + 1))
            up(act(w_hi[:, u % RING], slot, ACT.Copy), "w_hi", rounds)

        def act_feed(eng, p):
            for s in range(LEAD):
                act_split(eng, p.at("unit_done") + s)

        def act_high(p, c, x, nt, **kw):
            up(act(h_hi[:, c, 0:nt], x, ACT.Copy, **kw), "hi_ready")

        def act_presplit(eng, p):
            if p.kw["l"]:
                eng.wait_ge(S("mod_rows"), p.at("mod_rows"))
            w, parts = (wlr, wlr_p) if p.kw["l"] else (wgate, wgate_p)
            eng.wait_ge(S("unit_done"), p.at("unit_done"))
            if p.kw["l"] == 0:
                eng.wait_ge(S("roped2"), p.at("roped2"))
                eng.wait_ge(S("lam_e"), p.at("lam_e"))
                up(act(small[:, 162:164], small[:, 160:162], ACT.Exp), "lam_ready")
            up(act(parts[0][:, :, :], w[:, :, :], ACT.Copy), "small_hi")

        def act_gemm(eng, p):
            k = p.kw
            a, b = k["tok"]
            n = b - a
            u0, per, step, evac = p.at("unit_done"), k["per"], k["step"], k["evac"]
            turn = per * step
            for i, js, rounds in turns(eng, k["n"], step, peel=k["peel"]):
                for j in js:
                    for x in splits(p, i, j, rounds):
                        if rounds > 1:
                            act_split(eng, u0 + x, i, turn, rounds)
                        else:
                            act_split(eng, u0 + i * turn + x)
                    if "decays" in k and j == 0:
                        act_decays(eng, p)
                    if evac == "swiglu" and j % 2 == 0:
                        eng.wait_ge(S("unit_done"), i * turn + (u0 + j + 1))
                        eng.wait_ge(S(f"bank_free{j + 1}"), p.at(f"bank_free{j + 1}") + i)
                        up(act(sg[:, j // 2, 0:n], ps[:, j, 0:n], ACT.Silu), f"bank_free{j}", rounds)
                    elif evac == "tok":
                        eng.wait_ge(S("unit_done"), i * turn + (u0 + 2 * j + 2))
                        up(act(tok_dst(k, i, j, 0), tok_out(j, 0), ACT.Copy), f"bank_free{2 * j}", rounds)
                    elif evac == "copy" and j % 2 and not k["sumsq"]:
                        eng.wait_ge(S("unit_done"), i * turn + (u0 + j + 1))
                        up(act(gemm_dst(k, i, j, n), ps[:, j, 0:n], ACT.Copy), f"bank_free{j}", rounds)
                    if k["sumsq"]:
                        eng.wait_ge(S(f"bank_free{j}"), p.at(f"bank_free{j}") + i + 1)
                        src = big[:, :] if k["sumsq"] == "big" else resid[:, :, :].rearrange("p c n -> p (c n)")
                        act_square(eng, p, src[:, bass.ds(i * (4 * NT) + j * NT, n)], i, j, rounds)

        def tok_out(j, half):
            return ps[:, 2 * j + half, :].rearrange("p (a g n) -> p a g n", a=2, n=P)

        def tok_dst(k, i, j, half):
            tiles = slice(2 * half, 2 * half + 2)
            if k["dst"] == "vtok":
                return vtok[:, tiles, bass.ds(i * (2 * SEQ) + (k["dst0"] + j) * SEQ, SEQ)].rearrange("p a (g n) -> p a g n", n=P)
            return {"vda": vda, "vm": vm}[k["dst"]][:, tiles, 2 * j:2 * j + 2, 0:P]

        def gemm_dst(k, i, j, n):
            return big[:, bass.ds(i * (4 * NT) + (k["dst"] + j) * NT, n)]

        def act_store(eng, p):
            for g in (1, 3):
                eng.wait_ge(S("out_T"), g + 1)
                eng.wait_ge(S("out_sb"), g)
                up(act(vtok[:, g // 2, (g % 2) * 512:(g % 2) * 512 + 512], ps[:, g, :], ACT.Copy), "out_sb")

        V = nc.vector

        def link(ins):
            chain["dve"] += 1
            ins.then_inc(S("dve_chain"), 1)
            nc.vector.wait_ge(S("dve_chain"), chain["dve"])

        def dve_setup(eng, p):
            for z in (svec[:, :, :, :], wfbd[:, :, :], modb[:, :, :], wgate[:, :, :], gateb[:, :], wlr[:, :, :]):
                V.memset(z, 0.0).then_inc(S("zeroed"), 1)
            V.memset(epsc[:, :], EPS).then_inc(S("eps_set"), 1)
            link(V.memset(ones[:, :], 1.0))
            eng.wait_ge(S("rows_T"), 1)
            up(V.tensor_copy(cols1[:, :], ps[:, 0, 0:120]), "rows_sb")
            eng.wait_ge(S("rows_sb"), 1)

        def dve_constants(eng, p):
            eng.wait_ge(S("rows_T"), 2)
            up(V.tensor_copy(cols2[:, :], ps[:, 1, 0:47]), "rows_sb")
            eng.wait_ge(S("consts_in"), 16 * CONST_LOADS)
            eng.wait_ge(S("rows_sb"), 2)
            link(V.tensor_scalar(nsink[:, :], sinkb[:, :], -1.0, None, ALU.mult))

        def dve_load(eng, p):
            a = 0 if p.kw["which"] == 0 else SEQ
            for c in range(0, KC, 2):
                eng.wait_ge(S("tokens_T"), p.at("tokens_T", c + 1))
                up(V.tensor_copy(resid[:, c, a:NT], ps[:, c, a:NT]), f"bank_free{c}")

        def dve_rows(eng, p, i, per_turn, x, rounds):
            par = x % 2
            eng.wait_ge(S("mod_rows"), i * per_turn + (p.at("mod_rows") + x + 1))
            up(V.tensor_tensor(modr[:, par, :], ps[:, 4 + par, 0:SEG], modb[:, par, :], ALU.add), f"mod_sum{par}", rounds)

        def dve_cols(eng, p, i, per_turn, x, rounds):
            m = p.kw["host"] or p.kw
            flat = modT[2 * m["block"] + m["l"]][:, :, :].rearrange("p c v -> p (c v)")
            eng.wait_ge(S("mod_cols"), i * per_turn + (p.at("mod_cols") + x + 1))
            groups = ps[:, 6, 0:2 * P].rearrange("p (c j v) -> p c v j", c=2, j=4)[:, :, 0:2, :]
            up(V.reduce_sum(flat[:, bass.ds(i * (4 * per_turn) + 4 * (m["seg0"] + x), 4)].rearrange("p (c v) -> p c v", v=2), groups, AX.X),
               "mod_kept", rounds)

        def dve_mod(eng, p):
            segs = p.kw["n"]
            for i, rounds in pairs(eng, segs):
                for x in range(2):
                    dve_rows(eng, p, i, 2, x, rounds)
                for x in range(2):
                    dve_cols(eng, p, i, 2, x, rounds)

        def dve_modvec(eng, p):
            blk, l = p.kw["block"], p.kw["l"]
            m = 2 * blk + l
            evacuated(eng, p)

            def gcol(at):
                return cols1[:, at:at + KC].unsqueeze(2).broadcast_to([P, KC, 2])

            T, A = modT[m], modA[m]
            if blk == 0:
                if 0 in p.kw["parts"]:
                    last = V.scalar_tensor_tensor(A[:, 0], T[:, 8:16, :], 1.0, gcol(G_PRE + 8 * l), ALU.add, ALU.mult)
                if 1 in p.kw["parts"]:
                    last = V.tensor_tensor(A[:, 1], T[:, 16:24, :], gcol(G_POST + 8 * l), ALU.mult)
            else:
                for i in p.kw["parts"]:
                    V.scalar_tensor_tensor(A[:, 2 * i], T[:, 24 * i + 8:24 * i + 16, :], 1.0, gcol(NORM_G + 24 * l + 8 * i), ALU.add, ALU.mult)
                    last = V.tensor_scalar(A[:, 2 * i + 1], T[:, 24 * i + 16:24 * i + 24, :], 1.0 if i == 1 else 0.5, None, ALU.mult)
            up(last, "mod_ready")
            eng.wait_ge(S("mod_ready"), p.at("mod_ready", 1))

        def dve_norm(eng, p):
            nt, mode = p.kw["nt"], p.kw["mode"]
            eng.wait_ge(S("rms_ready"), p.at("rms_ready", 1))
            tiles = nt // P
            rms, inv = small[:, 204:204 + tiles], small[:, 208:208 + tiles]
            link(V.reciprocal(inv, rms))
            for v in range(nt // SEQ):
                up(V.tensor_tensor(diag[:, v * SEQ:(v + 1) * SEQ].rearrange("p (a n) -> p a n", n=P), ident.unsqueeze(1).broadcast_to([P, 2, P]),
                                   inv[:, 2 * v:2 * v + 2].unsqueeze(2).broadcast_to([P, 2, P]), ALU.mult), "diag_ready")
            halves = [slice(v * SEQ, (v + 1) * SEQ) for v in range(nt // SEQ)]
            if mode != "final":
                m = 2 * p.kw["block"] + p.kw["l"]

            def scaled(c):
                if c >= 3:
                    eng.wait_ge(S("h_ready"), p.at("h_ready", c - 2))
                for v, cols in enumerate(halves):
                    if c == 0:
                        eng.wait_ge(S("rstd_ready"), p.at("rstd_ready", v + 1))
                    last = V.scalar_tensor_tensor(tnorm[:, c % 3, cols], resid[:, c, cols], modA[m][:, 2 * p.kw["n"] if p.kw["block"] else 0, c, v:v + 1],
                                                  rstd_of(v), ALU.mult, ALU.mult)
                up(last, "t_ready")

            def low_part(c):
                eng.wait_ge(S("hi_ready"), p.at("hi_ready", c + 1))
                for v, cols in enumerate(halves):
                    sh = modT[m][:, p.kw["n"] * 24 + c, v:v + 1]
                    last = V.scalar_tensor_tensor(h_lo[:, c, cols], tnorm[:, c % 3, cols], sh, h_hi[:, c, cols].bitcast(F32), ALU.add, ALU.subtract)
                up(last, "h_ready")

            if mode == "pre":
                scaled(0)
                for c in range(KC):
                    if c + 1 < KC:
                        scaled(c + 1)
                    low_part(c)
                return
            for c in range(KC):
                for v, cols in enumerate(halves):
                    if c == 0:
                        eng.wait_ge(S("rstd_ready"), p.at("rstd_ready", v + 1))
                    if mode == "post":
                        y = big3[:, c, cols]
                        link(V.scalar_tensor_tensor(y, y, modA[m][:, 1, c, v:v + 1], rstd_of(v), ALU.mult, ALU.mult))
                        up(V.tensor_tensor(resid[:, c, cols], resid[:, c, cols], y, ALU.add), "normed")
                    else:
                        up(V.scalar_tensor_tensor(hT[:, c, cols], resid[:, c, cols], cols1[:, FINAL_G + c:FINAL_G + c + 1],
                                                  rstd_of(v), ALU.mult, ALU.mult), "normed")
            eng.wait_ge(S("normed"), p.at("normed", KC * (nt // SEQ)))

        def dve_split(eng, u, i=0, turn=0, rounds=1):
            eng.wait_ge(S("w_hi"), i * turn + (u + 1))
            up(V.tensor_tensor(w_lo[:, u % RING], arrival(u)[0], w_hi[:, u % RING].bitcast(F32), ALU.subtract), "w_ready", rounds)

        def dve_feed(eng, p):
            for s in range(LEAD):
                dve_split(eng, p.at("unit_done") + s)

        def dve_low(eng, p, n, c, nt):
            eng.wait_ge(S("hi_ready"), p.at("hi_ready", n + 1))
            up(V.tensor_tensor(h_lo[:, c, 0:nt], mixT[:, c, 0:nt], h_hi[:, c, 0:nt].bitcast(F32), ALU.subtract), "h_ready")

        def dve_presplit(eng, p):
            w, parts = (wlr, wlr_p) if p.kw["l"] else (wgate, wgate_p)
            eng.wait_ge(S("small_hi"), p.at("small_hi", 1))
            up(V.tensor_tensor(parts[1][:, :, :], w[:, :, :], parts[0][:, :, :].bitcast(F32), ALU.subtract), "small_lo")

        def dve_gemm(eng, p):
            k = p.kw
            a, b = k["tok"]
            n = b - a
            u0, per, step, evac = p.at("unit_done"), k["per"], k["step"], k["evac"]
            turn = per * step
            def evacuate(i, j, rounds):
                if evac in ("copy", "swiglu") and not k["sumsq"] and (j % 2) != (evac == "swiglu"):
                    return
                eng.wait_ge(S("unit_done"), i * turn + (u0 + j * per + per))
                if evac == "swiglu":
                    eng.wait_ge(S(f"bank_free{j - 1}"), p.at(f"bank_free{j - 1}") + i + 1)
                    eng.wait_ge(S("g_ready"), i * 2 + (p.at("g_ready") + j // 2))
                    up(V.tensor_tensor(gt[:, 0:n], sg[:, j // 2, 0:n], ps[:, j, 0:n], ALU.mult), f"bank_free{j}", rounds)
                    cols = bass.ds(i * (2 * NT) + (j // 2) * NT, n)
                    hi, lo = (g[:, :, :].rearrange("p c n -> p (c n)")[:, cols] for g in (g_hi, g_lo))
                    eng.wait_ge(S(f"bank_free{j}"), p.at(f"bank_free{j}") + i + 1)
                    up(V.tensor_copy(hi, gt[:, 0:n]), "g_hi_ready", rounds)
                    eng.wait_ge(S("g_hi_ready"), i * 2 + (p.at("g_hi_ready") + j // 2 + 1))
                    up(V.tensor_tensor(lo, gt[:, 0:n], hi.bitcast(F32), ALU.subtract), "g_ready", rounds)
                elif evac == "resid":
                    gate = modA[2 + k["l"]][:, :, :, :].rearrange("p s c v -> p (s c v)")
                    for v in range(n // SEQ):
                        cols = bass.ds(i * (4 * NT) + j * NT + v * SEQ, SEQ)
                        rs = resid[:, :, :].rearrange("p c n -> p (c n)")[:, cols]
                        at = (2 * k["g"] + 1) * KC * 2 + j * 2 + v
                        last = V.scalar_tensor_tensor(rs, ps[:, j, v * SEQ:(v + 1) * SEQ], gate[:, bass.ds(i * 8 + at, 1)], rs,
                                                      ALU.mult, ALU.add)
                    up(last, f"bank_free{j}", rounds)
                elif evac == "tok":
                    up(V.tensor_copy(tok_dst(k, i, j, 1), tok_out(j, 1)), f"bank_free{2 * j + 1}", rounds)
                else:
                    up(V.tensor_copy(gemm_dst(k, i, j, n), ps[:, j, 0:n]), f"bank_free{j}", rounds)

            for i, js, rounds in turns(eng, k["n"], step, peel=k["peel"]):
                for j in js:
                    seg = hosted(p, j, js)
                    if seg is not None:
                        dve_rows(eng, p, i, k["hper"], seg, rounds)
                    for x in splits(p, i, j, rounds):
                        if rounds > 1:
                            dve_split(eng, u0 + x, i, turn, rounds)
                        else:
                            dve_split(eng, u0 + i * turn + x)
                    if "decays" in k and j == 0:
                        dve_decays(eng, p)
                    evacuate(i, j, rounds)
                    if seg is not None:
                        dve_cols(eng, p, i, k["hper"], seg, rounds)

        def pool_sums(eng, p, n, items, step):
            if p.at("ms_sum"):
                eng.wait_ge(S("ms_sum"), p.at("ms_sum"))
            up(nc.gpsimd.memset(sqsum[:, :], 0.0), "sums_clear")
            eng.wait_ge(S("sums_clear"), p.at("sums_clear", 1))
            for i, js, rounds in turns(eng, items - 1, step):
                for j in js:
                    eng.wait_ge(S("sq_ready"), i * step + (p.at("sq_ready") + j + 1))
                    if p.at("sq_used") + j:
                        eng.wait_ge(S("sq_used"), i * step + (p.at("sq_used") + j))
                    up(nc.gpsimd.tensor_tensor(sqsum[:, 0:n], sqsum[:, 0:n], sq[:, j % 2, 0:n], ALU.add), "sq_used", rounds)

        def pool_squares(eng, p):
            if p.kw["after"] == "load":
                eng.wait_ge(S("tokens_T"), p.at("tokens_T"))
            pool_sums(eng, p, p.kw["nt"], KC, KC)

        def pool_gemm(eng, p):
            if p.kw["sumsq"]:
                eng.wait_ge(S("unit_done"), p.at("unit_done", 1))
                pool_sums(eng, p, p.kw["tok"][1] - p.kw["tok"][0], p.kw["n"], 4)

        def dve_store(eng, p):
            for g in (0, 2):
                eng.wait_ge(S("out_T"), g + 1)
                if g:
                    eng.wait_ge(S("out_sb"), g)
                up(V.tensor_copy(vtok[:, g // 2, (g % 2) * 512:(g % 2) * 512 + 512], ps[:, g, :]), "out_sb")

        G = nc.gpsimd

        def plink(ins):
            chain["pool"] += 1
            ins.then_inc(S("pool_chain"), 1)
            G.wait_ge(S("pool_chain"), chain["pool"])

        def conv3(x, y, taps, w, bias, sets, done=None):
            x, y, tap0, tap2 = (z.rearrange("p (s n) -> p s n", s=sets) for z in (x, y) + taps)
            G.tensor_scalar(y, x, w[1], bias, ALU.mult, ALU.add)
            G.tensor_scalar(tap0, x, w[0], None, ALU.mult)
            plink(G.tensor_scalar(tap2, x, w[2], None, ALU.mult))
            plink(G.tensor_tensor(y[:, :, 1:SEQ], y[:, :, 1:SEQ], tap0[:, :, 0:SEQ - 1], ALU.add))
            ins = G.tensor_tensor(y[:, :, 0:SEQ - 1], y[:, :, 0:SEQ - 1], tap2[:, :, 1:SEQ], ALU.add)
            up(ins, done) if done else plink(ins)

        probs = vtok[:, :, P:P + 512]
        probsT = vtok[:, :, P + 512:P + 512 + 2 * P].rearrange("p b (s q) -> p s b q", s=2)
        dftU = scr[:, 4096:6144].rearrange("p (g k) -> p g k", k=512)
        dftF = scr[:, 6144:7168].rearrange("p (c n) -> p c n", n=NT)
        kswap, tapped = big3[:, 22, :], big3[:, 23, :]
        atok1 = hT[:, 0:4, :]
        nmx, nm, rsum, esink = (small[:, 32 * i:32 * i + 32] for i in range(4))

        def items1(p):
            return [(t_, h, 0 if t_ < 2 else SEQ, 4 if t_ < 2 else 2) for t_ in range(TT if p.kw["both"] else 2) for h in range(HEADS)]

        ATT_BANK = (2, 3, 6, 7)

        def pe_mix1(eng, p):
            l, sets = p.kw["l"], 2 if p.kw["both"] else 1
            items = items1(p)
            evacuated(eng, p)
            for a in range(TT):
                last = tr(ps[:, 4, a * P:(a + 1) * P], big3[:, 5, a * P:(a + 1) * P], ident)
            up(last, "v_T")
            for c in range(2):
                for s in range(sets):
                    for a in range(2):
                        last = mm(ps[:, 2 * c + s, a * 256:a * 256 + 256], big3[:, 10 + c, s * SEQ + a * P:s * SEQ + a * P + P],
                                  C("dftc"), start=True, stop=True)
                    up(last, "dft1")
            eng.wait_ge(S("dft1_sb"), p.at("dft1_sb", 2 * sets))
            eng.wait_ge(S("v_sb"), p.at("v_sb", 1))
            for c in range(2):
                for s in range(sets):
                    for a in range(2):
                        for part in range(2):
                            last = mm(ps[:, 4 + c, s * SEQ:s * SEQ + SEQ], dftU[:, 2 * c + s, a * 256 + part * P:a * 256 + part * P + P],
                                      dftn[:, a, part, :], start=a + part == 0, stop=a + part == 2)
                up(last, "dft2")
            eng.wait_ge(S("k_swapped"), p.at("k_swapped", 1))

            def scores(n):
                t_, h, k0, kt = items[n]
                if n >= 4:
                    eng.wait_ge(S("probs_raw"), p.at("probs_raw", n - 3))
                r = slice(64 * (h % 2), 64 * (h % 2) + 64)
                keys = big3[r, 4, k0:k0 + kt * P] if h // Q_PER_KV == h % 2 else kswap[r, k0:k0 + kt * P]
                last = mm(ps[:, n % 4, 0:kt * P], big3[r, h // 2, t_ * P:t_ * P + P], keys, start=True, stop=t_ > 1)
                if t_ < 2:
                    cut = (1 - t_) * P
                    last = mm(ps[:, n % 4, cut:cut + P], ident, wmask[:, t_, :], start=False, stop=True)
                up(last, "scores_ready")

            def transposes(n):
                kt = items[n][3]
                eng.wait_ge(S("probs_raw"), p.at("probs_raw", n + 1))
                if n >= 2:
                    eng.wait_ge(S("probsT_sb"), p.at("probsT_sb", n - 1))
                for kb in range(kt):
                    last = tr(ps[:, 4 + n % 2, kb * P:kb * P + P], probs[:, n % 4, kb * P:kb * P + P], ident)
                up(last, "probsT_done")

            def values(n):
                t_, h, k0, kt = items[n]
                g = h // Q_PER_KV
                eng.wait_ge(S("probsT_sb"), p.at("probsT_sb", n + 1))
                if h == 0:
                    if t_ < 2:
                        eng.wait_ge(S("dft3_gated"), p.at("dft3_gated", 2))
                    else:
                        eng.wait_ge(S("att_kept"), p.at("att_kept", t_ - 1))
                for kb in range(kt):
                    last = mm(ps[:, 6 + t_ % 2, h * HD:(h + 1) * HD], probsT[:, n % 2, kb, :], vtok[:, k0 // P + kb, g * HD:(g + 1) * HD],
                              start=kb == 0, stop=kb == kt - 1)
                up(last, "pv_done")

            N = len(items)
            scores(0)
            scores(1)
            for c in range(2):
                eng.wait_ge(S("dft2_sb"), p.at("dft2_sb", c + 1))
                up(mm(ps[:, 6 + c, 0:sets * SEQ], wfbd[:, 2 * l + c, :], dftF[:, c, 0:sets * SEQ], start=True, stop=True), "dft3")
            scores(2)
            for n in range(N):
                if n + 3 < N:
                    scores(n + 3)
                transposes(n)
                if n:
                    values(n - 1)
            values(N - 1)
            eng.wait_ge(S("att_kept"), p.at("att_kept", N // HEADS))
            for c in range(4):
                for t_ in range(N // HEADS):
                    last = tr(ps[:, ATT_BANK[c], t_ * P:t_ * P + P], atok1[:, t_, c * P:c * P + P], ident)
                up(last, "att_T")

        def act_gates(eng, p):
            for b in range(4):
                eng.wait_ge(S(f"bank_free{b}"), p.at(f"bank_free{b}"))
            act(big3[:, 6:10, 0:p.kw["nt"]], big3[:, 6:10, 0:p.kw["nt"]], ACT.Silu)
            up(act(big3[:, 12:14, 0:p.kw["nt"]], big3[:, 12:14, 0:p.kw["nt"]], ACT.Silu), "gates_done")

        def act_mix1(eng, p):
            l, sets = p.kw["l"], 2 if p.kw["both"] else 1
            items, nt = items1(p), sets * SEQ
            evacuated(eng, p)
            eng.wait_ge(S("v_T"), p.at("v_T", 1))
            up(act(vtok[:, :, 0:P], ps[:, 4, :].rearrange("p (a n) -> p a n", n=P), ACT.Copy), "v_sb")
            for c in range(2):
                for s in range(sets):
                    eng.wait_ge(S("dft1"), p.at("dft1", sets * c + s + 1))
                    up(act(dftU[:, 2 * c + s, :], ps[:, 2 * c + s, :], ACT.Copy), "dft1_sb")
            up(act(big3[:, 20:22, 0:nt], big3[:, 20:22, 0:nt], ACT.Silu), "gates_done")
            for c in range(2):
                eng.wait_ge(S("dft2"), p.at("dft2", c + 1))
                up(act(dftF[:, c, 0:nt], ps[:, 4 + c, 0:nt], ACT.Copy), "dft2_sb")

            def exps(n):
                kt = items[n][3]
                eng.wait_ge(S("negmax_ready"), p.at("negmax_ready", n + 1))
                if n >= 4:
                    eng.wait_ge(S("probsT_done"), p.at("probsT_done", n - 3))
                up(act(probs[:, n % 4, 0:kt * P], ps[:, n % 4, 0:kt * P], ACT.Exp, bias=nm[:, n:n + 1], scale=HD ** -0.5,
                       accum_out=rsum[:, n:n + 1]), "probs_raw")
                t_, h = items[n][0:2]
                if h == HEADS - 1:
                    eng.wait_ge(S("sink_args"), p.at("sink_args", t_ + 1))
                    e = esink[:, HEADS * t_:HEADS * t_ + HEADS]
                    up(act(e, e, ACT.Exp), "sink_exp")

            def keep_T(n):
                kt = items[n][3]
                if n >= 2:
                    eng.wait_ge(S("pv_done"), p.at("pv_done", n - 1))
                eng.wait_ge(S("probsT_done"), p.at("probsT_done", n + 1))
                up(act(probsT[:, n % 2, 0:kt, :], ps[:, 4 + n % 2, 0:kt * P].rearrange("p (b q) -> p b q", q=P), ACT.Copy), "probsT_sb")

            for n in range(len(items)):
                exps(n)
                if n:
                    keep_T(n - 1)
                if n == HEADS - 1:
                    eng.wait_ge(S("dft3_gated"), p.at("dft3_gated", 2))
                    act_feed(eng, p)
                if n == HEADS + 3:
                    eng.wait_ge(S("conv_done"), p.at("conv_done", 1))
                    for c in range(4, KC):
                        act_high(p, c, mixT[:, c, 0:nt], nt)
            keep_T(len(items) - 1)
            eng.wait_ge(S("att_T"), p.at("att_T", 4))
            for c in range(4):
                eng.wait_ge(S("att_gated"), p.at("att_gated", c + 1))
                act_high(p, c, mixT[:, c, 0:nt], nt)

        def rotary(chunks, n, tmp, name):
            shape = [P, n, SEQ]
            x, tmp = chunks[:, :, 0:SEQ], tmp.rearrange("p (c n) -> p c n", n=SEQ)
            link(V.stream_shuffle(tmp, x, SWAP16))
            link(V.tensor_tensor(tmp, tmp, ropeS.unsqueeze(1).broadcast_to(shape), ALU.mult))
            link(V.tensor_tensor(x, x, ropeC.unsqueeze(1).broadcast_to(shape), ALU.mult))
            up(V.tensor_tensor(x, x, tmp, ALU.add), name)

        def dve_mix1(eng, p):
            l, sets = p.kw["l"], 2 if p.kw["both"] else 1
            items, nt = items1(p), sets * SEQ
            hflat = hT[:, :, :].rearrange("p c n -> p (c n)")
            evacuated(eng, p)
            rotary(big3[:, 0:5], 5, hflat[:, 0:5 * SEQ], "roped")
            eng.wait_ge(S("roped"), p.at("roped", 1))
            V.tensor_copy(kswap[0:64, :], big3[64:128, 4, :])
            up(V.tensor_copy(kswap[64:128, :], big3[0:64, 4, :]), "k_swapped")

            def gate_fourier():
                eng.wait_ge(S("gates_done"), p.at("gates_done"))
                for c in range(2):
                    eng.wait_ge(S("dft3"), p.at("dft3", c + 1))
                    up(V.tensor_tensor(mixT[:, 4 + c, 0:nt], ps[:, 6 + c, 0:nt], big3[:, 12 + c, 0:nt], ALU.mult), "dft3_gated")

            def maxima(n):
                t_, h, k0, kt = items[n]
                eng.wait_ge(S("scores_ready"), p.at("scores_ready", n + 1))
                link(V.reduce_max(nmx[:, n:n + 1], ps[:, n % 4, 0:kt * P], AX.X, negate=True))
                up(V.tensor_scalar(nm[:, n:n + 1], nmx[:, n:n + 1], HD ** -0.5, nsink[:, l * HEADS + h:l * HEADS + h + 1],
                                   ALU.mult, ALU.min), "negmax_ready")
                if h == HEADS - 1:
                    heads = slice(n + 1 - HEADS, n + 1)
                    eng.wait_ge(S("negmax_ready"), p.at("negmax_ready", n + 1))
                    up(V.tensor_tensor(esink[:, heads], nm[:, heads], sinkb[:, l * HEADS:(l + 1) * HEADS], ALU.add), "sink_args")

            def keep(t_):
                heads = slice(t_ * HEADS, (t_ + 1) * HEADS)
                eng.wait_ge(S("sink_exp"), p.at("sink_exp", t_ + 1))
                link(V.tensor_tensor(rsum[:, heads], rsum[:, heads], esink[:, heads], ALU.add))
                link(V.reciprocal(rsum[:, heads], rsum[:, heads]))
                eng.wait_ge(S("pv_done"), p.at("pv_done", HEADS * (t_ + 1)))
                up(V.tensor_tensor(atok1[:, t_, :].rearrange("p (h e) -> p h e", e=HD), ps[:, 6 + t_ % 2, :].rearrange("p (h e) -> p h e", e=HD),
                                   rsum[:, heads].unsqueeze(2).broadcast_to([P, HEADS, HD]), ALU.mult), "att_kept")

            for n in range(len(items)):
                if n == 2:
                    gate_fourier()
                maxima(n)
                if n == HEADS + 2:
                    dve_feed(eng, p)
                if n == HEADS + 5:
                    for c in range(4, KC):
                        dve_low(eng, p, c - 4, c, nt)
                if n >= HEADS and n % HEADS == 4:
                    keep(n // HEADS - 1)
            keep(len(items) // HEADS - 1)
            for c in range(4):
                eng.wait_ge(S("att_T"), p.at("att_T", c + 1))
                up(V.tensor_tensor(mixT[:, c, 0:nt], ps[:, ATT_BANK[c], 0:nt], big3[:, 6 + c, 0:nt], ALU.mult), "att_gated")
                if c:
                    dve_low(eng, p, 3 + c, c - 1, nt)
            dve_low(eng, p, 7, 3, nt)

        def pool_mix1(eng, p):
            l, sets = p.kw["l"], 2 if p.kw["both"] else 1
            nt = sets * SEQ
            evacuated(eng, p)
            for c in range(2):
                b = big3[:, 16 + c, 0:nt]
                w = [cols2[:, CONV_W + (l * 3 + tap) * 2 + c:CONV_W + (l * 3 + tap) * 2 + c + 1] for tap in range(3)]
                x, y = hT[:, 4 + c, 0:nt], hT[:, 6 + c, 0:nt]
                plink(G.tensor_tensor(x, big3[:, 14 + c, 0:nt], big3[:, 18 + c, 0:nt], ALU.mult))
                conv3(x, y, (tapped[:, 0:nt], mixT[:, 6 + c, 0:nt]), w, cols2[:, CONV_B + 2 * l + c:CONV_B + 2 * l + c + 1], sets)
                plink(G.tensor_tensor(y, y, b, ALU.mult))
            eng.wait_ge(S("gates_done"), p.at("gates_done", 1))
            up(G.tensor_tensor(mixT[:, 6:8, 0:nt], hT[:, 6:8, 0:nt], big3[:, 20:22, 0:nt], ALU.mult), "conv_done")

        probs2 = scr[:, 0:3072].rearrange("p (s k) -> p s k", k=512)
        wT = scr[:, 3072:4096].rearrange("p (s k) -> p s k", k=512)
        rot = big[:, 20 * NT:22 * NT]
        junk = hT[:, 7, 0:P]
        decay = big[:, 4 * NT:10 * NT].rearrange("p (s t r q) -> p s t r q", s=2, t=2, r=3)
        dargs = mixT[:, 0:4, :].rearrange("p (s t) (r q) -> p s t r q", s=2, r=2)
        convt = mixT[:, 6:8, :]
        atok = hT[:, 0:4, :].rearrange("p t (h e) -> p t h e", h=4)
        mtok = big3[:, 0:4, :].rearrange("p t (h e) -> p t h e", h=4)
        grow = [big3[0:64, 20 + i, :] for i in range(4)]
        acol, ecol = hT[:, 5, 0:256], hT[:, 6, 0:256]
        ssq = small[:, 168:200]
        dcol = small[:, 200:204]
        items2 = [(h, qt) for h in range(DA_HEADS) for qt in range(TT)]
        N2 = len(items2)

        def keys2(qt):
            return (0, 4) if qt < 2 else (SEQ, 2)

        def narrow(eng, p, out, parts):
            eng.wait_ge(S("small_lo"), p.at("small_lo"))
            x = {"hi": h_hi, "lo": h_lo}
            w = {"hi": parts[0], "lo": parts[1]}
            for k in range(KC):
                for wp, xp in W_X:
                    last = mm(out, w[wp][:, k, :], x[xp][:, k, :], start=k == 0 and wp == xp, stop=k == KC - 1 and wp == "lo")
            return last

        def pe_rows_of_gates(eng, p):
            for name in ("bank_free6", "mod_kept"):
                eng.wait_ge(S(name), p.at(name))
            up(narrow(eng, p, ps[:, 6, :], wgate_p), "gate_rows")

        def pe_even(eng, p):
            evacuated(eng, p)
            eng.wait_ge(S("roped2"), p.at("roped2"))

            def scores(i):
                h, qt = items2[i]
                k0, kt = keys2(qt)
                if i >= 3:
                    eng.wait_ge(S("probs_raw"), p.at("probs_raw", 2 * i - 4))
                for c in range(2):
                    r = slice(64 * c, 64 * c + 64)
                    up(mm(ps[:, 2 * (i % 3) + c, 0:kt * P], big3[r, h, qt * P:qt * P + P], big3[r, 4 + h, k0:k0 + kt * P],
                          start=True, stop=True), "scores_ready")

            def transposes(i):
                kt = keys2(items2[i][1])[1]
                eng.wait_ge(S("probs_ready"), p.at("probs_ready", i + 1))
                if i:
                    eng.wait_ge(S("probsT_sb"), p.at("probsT_sb", i))
                for kb in range(kt):
                    last = tr(ps[:, 6, kb * P:kb * P + P], probs2[:, 2 * (i % 3), kb * P:kb * P + P], ident)
                up(last, "probsT_done")

            def values(i):
                h, qt = items2[i]
                k0, kt = keys2(qt)
                eng.wait_ge(S("probsT_sb"), p.at("probsT_sb", i + 1))
                if i:
                    eng.wait_ge(S("att_evac"), p.at("att_evac", i))
                else:
                    eng.wait_ge(S("ecol_sb"), p.at("ecol_sb", 1))
                for kb in range(kt):
                    last = mm(ps[:, 7, 0:P], wT[:, i % 2, kb * P:kb * P + P], vda[:, k0 // P + kb, h, :], start=kb == 0, stop=kb == kt - 1)
                up(last, "pv_done")

            scores(0)
            scores(1)
            eng.wait_ge(S("rows_ready"), p.at("rows_ready"))
            for half, row in enumerate((grow[0], grow[3])):
                for a in range(TT):
                    last = tr(ps[:, 7, half * 256 + a * 64:half * 256 + a * 64 + 64], row[:, a * P:a * P + P], ident[0:64, 0:64])
            up(last, "acol_T")
            for i in range(N2):
                if i + 2 < N2:
                    scores(i + 2)
                transposes(i)
                if i:
                    values(i - 1)
            values(N2 - 1)

            eng.wait_ge(S("probs_raw"), p.at("probs_raw", 2 * N2))

            def maxima_row(j):
                h, d = j // 2, j % 2
                if j >= 2:
                    eng.wait_ge(S("decay"), p.at("decay", j - 1))
                pick = ident[0:64, 32 * d + h:32 * d + h + 1].broadcast_to([64, P])
                up(mm(ps[:, 3 + j % 2, :], pick, grow[2], start=True, stop=True), "bcast")

            def products(h):
                r = slice(64 * (h % 2), 64 * (h % 2) + 64)
                if h:
                    eng.wait_ge(S("weighted"), p.at("weighted", 2 * h))
                else:
                    eng.wait_ge(S("conv_silu"), p.at("conv_silu", 1))
                q = big3[r, 16 + h // 2, :]
                k = big3[r, 18 + h // 2, :]
                for a in range(2):
                    mm(ps[:, a, :], k[:, SEQ + a * P:SEQ + a * P + P], q, start=True, stop=True)
                    last = mm(ps[:, 2, a * SEQ:a * SEQ + SEQ], k[:, a * P:a * P + P], q[:, 0:SEQ], start=True, stop=True)
                up(last, "qk_done")

            def memory(j):
                h, d = j // 2, j % 2
                eng.wait_ge(S("weighted"), p.at("weighted", j + 1))
                if j:
                    eng.wait_ge(S("mem_done"), p.at("mem_done", j))
                else:
                    eng.wait_ge(S("ones_set"), p.at("ones_set", 1))
                for tile in range(TT):
                    a = tile % 2
                    q = slice(a * P, a * P + P)
                    near = [s for s in range(2) if (s >= a if d else s <= a)]
                    terms = [(s, 0) for s in near] if tile < 2 else [(2 + s, 2) for s in near]
                    if tile < 2:
                        terms += [(2, 1), (3, 1)]
                    for n, (s, part) in enumerate(terms):
                        last = mm(ps[:, 5 + tile // 2, a * (P + 1):(a + 1) * (P + 1)], decay[:, j % 2, s % 2, part, q], vm[:, s, h, :],
                                  start=n == 0, stop=n == len(terms) - 1)
                up(last, "numden")

            maxima_row(0)
            products(0)
            maxima_row(1)
            for j in range(8):
                if j + 2 < 8:
                    maxima_row(j + 2)
                if j % 2 and j < 7:
                    products(j // 2 + 1)
                memory(j)

            eng.wait_ge(S("att_normed"), p.at("att_normed", 1))
            for h in range(DA_HEADS):
                for tile in range(TT):
                    last = tr(ps[:, h, tile * P:tile * P + P], atok[:, tile, h, :], ident)
                up(last, "att_T")
            for h in range(ML_HEADS):
                eng.wait_ge(S("mem_normed"), p.at("mem_normed", h + 1))
                for tile in range(TT):
                    last = tr(ps[:, 4 + h, tile * P:tile * P + P], mtok[:, tile, h, :], ident)
                up(last, "mem_T")
            eng.wait_ge(S("h_ready"), p.at("h_ready", 2))

        def act_rows_of_gates(eng, p):
            eng.wait_ge(S("gate_bias"), p.at("gate_bias", 1))
            alink(act(grow[2], grow[1], ACT.Abs))
            alink(act(grow[2], grow[2], ACT.Exp, scale=-1.0))
            up(act(grow[2], grow[2], ACT.Ln, bias=1.0), "gate_ln")

        def act_even(eng, p):
            evacuated(eng, p)

            def exps(i):
                kt = keys2(items2[i][1])[1]
                eng.wait_ge(S("negmax_ready"), p.at("negmax_ready", i + 1))
                if i >= 3:
                    eng.wait_ge(S("probsT_done"), p.at("probsT_done", i - 2))
                for c in range(2):
                    n = 2 * i + c
                    b = 2 * (i % 3) + c
                    up(act(probs2[:, b, 0:kt * P], ps[:, b, 0:kt * P], ACT.Exp, bias=nm[:, n:n + 1], scale=HD ** -0.5,
                           accum_out=rsum[:, n:n + 1]), "probs_raw")

            def keep_T(i):
                n = keys2(items2[i][1])[1] * P
                if i >= 2:
                    eng.wait_ge(S("pv_done"), p.at("pv_done", i - 1))
                eng.wait_ge(S("probsT_done"), p.at("probsT_done", i + 1))
                up(act(wT[:, i % 2, 0:n], ps[:, 6, 0:n], ACT.Copy), "probsT_sb")

            def square(x, at, name, start):
                if start:
                    eng.wait_ge(S(name), start)
                return act(junk, x, ACT.Square, accum_out=ssq[:, at:at + 1])

            def square_att(i):
                h, qt = items2[i]
                eng.wait_ge(S("att_evac"), p.at("att_evac", i + 1))
                up(square(atok[:, qt, h, :], 4 * qt + h, "att_sq", p.at("att_sq", i) if i else 0), "att_sq")

            for i in range(N2 + 3):
                if i < N2:
                    exps(i)
                if i == 0:
                    eng.wait_ge(S("acol_T"), p.at("acol_T", 1))
                    up(act(acol, ps[:, 7, 0:256], ACT.Copy), "acol_sb")
                    up(act(ecol, ps[:, 7, 256:512], ACT.Exp, scale=-1.0), "ecol_sb")
                if 0 <= i - 1 < N2:
                    keep_T(i - 1)
                if i >= 3:
                    square_att(i - 3)

            def roots(n):
                up(act(ssq[:, 16 * n:16 * n + 16], ssq[:, 16 * n:16 * n + 16], ACT.Sqrt, scale=1.0 / P, bias=epsc[:, :]), "roots")

            eng.wait_ge(S("conv_lin"), p.at("conv_lin", 1))
            up(act(big3[:, 16:20, :], big3[:, 16:20, :], ACT.Silu), "conv_silu")
            eng.wait_ge(S("acol_sb"), p.at("acol_sb", 1))

            def square_mem(h):
                eng.wait_ge(S("mem_done"), p.at("mem_done", 2 * h + 2))
                for tile in range(TT):
                    if h or tile:
                        eng.wait_ge(S("act_chain"), chain["act"])
                    chain["act"] += 1
                    act(junk, mtok[:, tile, h, :], ACT.Square, accum_out=ssq[:, 16 + 4 * tile + h:17 + 4 * tile + h]).then_inc(S("act_chain"), 1)

            for j in range(8):
                h, d = j // 2, j % 2

                def a_of(tile):
                    at = tile * 64 + 32 * d + h
                    return acol[:, at:at + 1]

                eng.wait_ge(S("args"), p.at("args", j + 1))
                if j >= 2:
                    eng.wait_ge(S("numden"), p.at("numden", j - 1))
                for a in range(2):
                    act(decay[:, j % 2, a, 0, :], dargs[:, j % 2, a, 0, :], ACT.Exp, bias=a_of(a))
                    act(decay[:, j % 2, a, 1, :], ps[:, 3 + j % 2, 0:SEQ], ACT.Exp, bias=a_of(2 + a), scale=-1.0)
                    last = act(decay[:, j % 2, a, 2, :], dargs[:, j % 2, a, 1, :], ACT.Exp, bias=a_of(2 + a))
                up(last, "decay")
                if j == 1:
                    act_feed(eng, p)
                if j in (3, 5, 7):
                    square_mem((j - 3) // 2)
            eng.wait_ge(S("att_sq"), p.at("att_sq", N2))
            roots(0)
            square_mem(3)
            eng.wait_ge(S("act_chain"), chain["act"])
            roots(1)
            eng.wait_ge(S("att_T"), p.at("att_T", 4))
            for h in range(DA_HEADS):
                act_high(p, h, ps[:, h, :], NT, scale=small[:, 165:166])
            up(act(big3[:, 12:16, :], big3[:, 12:16, :], ACT.Sigmoid), "osig")
            for h in range(ML_HEADS):
                eng.wait_ge(S("mem_gated"), p.at("mem_gated", h + 1))
                act_high(p, 4 + h, mixT[:, 4 + h, :], NT)

        def dve_rotary(eng, p):
            half = p.kw["half"]
            evacuated(eng, p)
            rotary(big3[:, 4 * half:4 * half + 4], 4, rot, "roped2")
            if half:
                return
            for i in range(2):
                link(V.tensor_tensor(dlam[:, 128 * i:128 * i + 64], dlam[:, 128 * i:128 * i + 64], dlam[:, 128 * i + 64:128 * i + 128], ALU.mult))
                ins = V.reduce_sum(small[:, 160 + i:161 + i], dlam[:, 128 * i:128 * i + 64], AX.X)
                link(ins) if i == 0 else up(ins, "lam_e")

        def dve_rows_of_gates(eng, p):
            eng.wait_ge(S("gate_rows"), p.at("gate_rows", 1))
            V.tensor_scalar(grow[0], ps[0:64, 6, :], gateb[:, 0:1], None, ALU.add)
            link(V.tensor_copy(grow[1], ps[64:128, 6, :]))
            up(V.tensor_scalar(grow[1], grow[1], gateb[:, 1:2], None, ALU.add), "gate_bias")
            f, b, a, m = grow[1], grow[3], grow[0], grow[2]
            eng.wait_ge(S("gate_ln"), p.at("gate_ln", 1))
            link(V.scalar_tensor_tensor(f, f, 0.0, grow[2], ALU.min, ALU.subtract))

            def scan(dst, data, op0, op1, first):
                fw, bw = slice(0, 32), slice(32, 64)
                V.tensor_tensor_scan(dst[fw, SEQ:NT], first(fw, SEQ, NT), data[fw, SEQ:NT], 0.0, op0, op1)
                link(V.tensor_tensor_scan(dst[bw, SEQ:NT][:, ::-1], first(bw, SEQ, NT)[:, ::-1], data[bw, SEQ:NT][:, ::-1], 0.0, op0, op1))
                V.tensor_tensor_scan(dst[fw, 0:SEQ], first(fw, 0, SEQ), data[fw, 0:SEQ], dst[fw, NT - 1:NT], op0, op1)
                link(V.tensor_tensor_scan(dst[bw, 0:SEQ][:, ::-1], first(bw, 0, SEQ)[:, ::-1], data[bw, 0:SEQ][:, ::-1], dst[bw, SEQ:SEQ + 1], op0, op1))

            scan(b, f, ALU.mult, ALU.add, lambda r, s, e: ones[r, 0:SEQ])
            link(V.tensor_tensor(a, a, b, ALU.subtract))
            scan(m, a, ALU.max, ALU.max, lambda r, s, e: a[r, s:e])
            up(V.tensor_tensor(b, b, m, ALU.add), "rows_ready")

        def dve_even(eng, p):
            evacuated(eng, p)
            def maxima(i):
                kt = keys2(items2[i][1])[1]
                for c in range(2):
                    n = 2 * i + c
                    eng.wait_ge(S("scores_ready"), p.at("scores_ready", n + 1))
                    ins = V.reduce_max(nmx[:, n:n + 1], ps[:, 2 * (i % 3) + c, 0:kt * P], AX.X, negate=True)
                link(ins)
                up(V.tensor_scalar(nm[:, 2 * i:2 * i + 2], nmx[:, 2 * i:2 * i + 2], HD ** -0.5, None, ALU.mult), "negmax_ready")

            def combine(i):
                kt = keys2(items2[i][1])[1]
                n, b = 2 * i, 2 * (i % 3)
                eng.wait_ge(S("probs_raw"), p.at("probs_raw", n + 2))
                link(V.reciprocal(esink[:, n:n + 2], rsum[:, n:n + 2]))
                link(V.scalar_tensor_tensor(esink[:, n + 1:n + 2], esink[:, n + 1:n + 2], small[:, 164:165], rsum[:, n:n + 1], ALU.mult, ALU.mult))
                p0, p1 = probs2[:, b, 0:kt * P], probs2[:, b + 1, 0:kt * P]
                up(V.scalar_tensor_tensor(p0, p1, esink[:, n + 1:n + 2], p0, ALU.mult, ALU.add), "probs_ready")

            def keep(i):
                h, qt = items2[i]
                eng.wait_ge(S("pv_done"), p.at("pv_done", i + 1))
                up(V.tensor_scalar(atok[:, qt, h, :], ps[:, 7, 0:P], esink[:, 2 * i:2 * i + 1], None, ALU.mult), "att_evac")

            maxima(0)
            eng.wait_ge(S("lam_ready"), p.at("lam_ready"))
            link(V.scalar_tensor_tensor(small[:, 164:165], small[:, 163:164], -LAM_INIT, small[:, 162:163], ALU.add, ALU.subtract))
            link(V.tensor_scalar(small[:, 165:166], cols2[:, DIFF_G:DIFF_G + 1], 1.0 - LAM_INIT, None, ALU.mult))
            for i in range(N2):
                if i + 1 < N2:
                    maxima(i + 1)
                combine(i)
                if i >= 2:
                    keep(i - 2)
            keep(N2 - 2)
            keep(N2 - 1)

            def args(j):
                eng.wait_ge(S("bcast"), p.at("bcast", j + 1))
                if j >= 2:
                    eng.wait_ge(S("decay"), p.at("decay", j - 1))
                mrow = ps[:, 3 + j % 2, :].rearrange("p (r q) -> p r q", r=2)
                for t_ in range(2):
                    last = V.scalar_tensor_tensor(dargs[:, j % 2, t_], mrow, -1.0, mmask[:, j % 2, t_].unsqueeze(1).broadcast_to([P, 2, SEQ]),
                                                  ALU.mult, ALU.add)
                up(last, "args")

            def weighted(j):
                eng.wait_ge(S("decay"), p.at("decay", j + 1))
                eng.wait_ge(S("qk_done"), p.at("qk_done", j // 2 + 1))
                for t_ in range(2):
                    w = decay[:, j % 2, t_]
                    V.scalar_tensor_tensor(w[:, 1:3, :], ps[:, t_, :].rearrange("p (r q) -> p r q", r=2), HD ** -0.5, w[:, 1:3, :],
                                           ALU.mult, ALU.mult)
                    last = V.scalar_tensor_tensor(w[:, 0, :], ps[:, 2, t_ * SEQ:t_ * SEQ + SEQ], HD ** -0.5, w[:, 0, :], ALU.mult, ALU.mult)
                up(last, "weighted")

            def memory(j):
                h, d = j // 2, j % 2
                eng.wait_ge(S("numden"), p.at("numden", j + 1))
                nd = ps[:, 5:7, 0:2 * (P + 1)].rearrange("p b (t n) -> p b t n", n=P + 1)
                den, dc = nd[:, :, :, P], dcol.rearrange("p (b t) -> p b t", b=2)
                if j == 0:
                    eng.wait_ge(S("ecol_sb"), p.at("ecol_sb", 1))
                floor = ecol.rearrange("p (b t r) -> p b t r", b=2, r=64)[:, :, :, 32 * d + h]
                link(V.scalar_tensor_tensor(dc, den, -1.0, floor, ALU.mult, ALU.max))
                link(V.tensor_tensor(dc, den, dc, ALU.max))
                link(V.reciprocal(dcol, dcol))
                if d == 0:
                    up(V.tensor_tensor(mtok[:, :, h, :].rearrange("p (b t) e -> p b t e", b=2), nd[:, :, :, 0:P],
                                       dc.unsqueeze(3).broadcast_to([P, 2, 2, P]), ALU.mult), "mem_done")
                else:
                    eng.wait_ge(S("mem_done"), p.at("mem_done", j))
                    for t_ in range(TT):
                        m = mtok[:, t_, h, :]
                        last = V.scalar_tensor_tensor(m, nd[:, t_ // 2, t_ % 2, 0:P], dcol[:, t_:t_ + 1], m, ALU.mult, ALU.add)
                    up(last, "mem_done")

            args(0)
            args(1)
            for j in range(8):
                weighted(j)
                if j == 2:
                    dve_feed(eng, p)
                if j + 2 < 8:
                    args(j + 2)
                if j:
                    memory(j - 1)
            eng.wait_ge(S("roots"), p.at("roots", 1))
            up(V.reciprocal(ssq[:, 0:16], ssq[:, 0:16]), "rstds")
            memory(7)
            eng.wait_ge(S("roots"), p.at("roots", 2))
            up(V.reciprocal(ssq[:, 16:32], ssq[:, 16:32]), "rstds")
            eng.wait_ge(S("rstds"), p.at("rstds", 2))
            rs = ssq[:, 16:32].rearrange("p (t h) -> p t h", h=4)
            for h in range(ML_HEADS):
                m = mtok[:, :, h, :]
                up(V.tensor_tensor(m, m, rs[:, :, h].unsqueeze(2).broadcast_to([P, TT, P]), ALU.mult), "mem_normed")
            for h in range(DA_HEADS):
                eng.wait_ge(S("hi_ready"), p.at("hi_ready", h + 1))
                up(V.scalar_tensor_tensor(h_lo[:, h, :], ps[:, h, :], small[:, 165:166], h_hi[:, h, :].bitcast(F32), ALU.mult, ALU.subtract), "h_ready")
            eng.wait_ge(S("osig"), p.at("osig", 1))
            for h in range(ML_HEADS):
                eng.wait_ge(S("mem_T"), p.at("mem_T", h + 1))
                up(V.scalar_tensor_tensor(mixT[:, 4 + h, :], ps[:, 4 + h, :], cols2[:, ML_G + h:ML_G + h + 1], big3[:, 12 + h, :], ALU.mult, ALU.mult),
                   "mem_gated")
                if h:
                    dve_low(eng, p, 3 + h, 3 + h, NT)
            dve_low(eng, p, 7, 7, NT)

        def pool_even(eng, p):
            evacuated(eng, p)
            up(G.memset(vm[:, :, :, P:P + 1], 1.0), "ones_set")
            for c in range(4):
                w = [cols2[:, MCONV_W + tap * 4 + c:MCONV_W + tap * 4 + c + 1] for tap in range(3)]
                conv3(big3[:, 8 + c, :], big3[:, 16 + c, :], (convt[:, 0, :], convt[:, 1, :]), w, cols2[:, MCONV_B + c:MCONV_B + c + 1], 2,
                      "conv_lin" if c == 3 else None)
            eng.wait_ge(S("rstds"), p.at("rstds", 1))
            rs = ssq[:, 0:16].rearrange("p (t h) -> p t h", h=4)
            up(G.tensor_tensor(atok, atok, rs.unsqueeze(3).broadcast_to([P, TT, 4, P]), ALU.mult), "att_normed")

        lrT = diag[0:64, :]
        ckd = scr[:, 512:2560].rearrange("p (i n) -> p i n", n=SEQ)
        ckdT = scr[:, 2560:4608].rearrange("p (i n) -> p i n", n=SEQ)
        state = scr[:, 4608:6656].rearrange("p (i n) -> p i n", n=SEQ)
        amask = big3[:, 8:16, SEQ:NT]
        otok = big[:, 16 * NT:20 * NT].rearrange("p (a h e) -> p a h e", a=2, h=GLA_HEADS)
        ojunk = big[:, 20 * NT:20 * NT + SEQ]
        softplus = big3[:, 8:16, SEQ:NT]

        def gates_of(d):
            return big3[:, 16 + 4 * d:20 + 4 * d, :].rearrange("p c (s n) -> p (c s) n", s=2)

        bend, blast, eblast = small[:, 0:8], small[:, 32:64], small[:, 64:96]
        STREAMS = [(d, h) for d in range(2) for h in range(GLA_HEADS)]

        def pe_decay_gates(eng, p):
            for name in ("bank_free4", "bank_free5", "bank_free6", "bank_free7", "mod_sum0", "mod_sum1", "mod_kept"):
                eng.wait_ge(S(name), p.at(name))
            up(narrow(eng, p, ps[0:64, 4, :], wlr_p), "lr_done")
            eng.wait_ge(S("lr_sb"), p.at("lr_sb", 1))
            for i, (d, h) in enumerate(STREAMS):
                if i >= 4:
                    eng.wait_ge(S("z_sb"), p.at("z_sb", i - 3))
                r = slice(32 * d, 32 * d + 16)
                up(mm(ps[:, 4 + i % 4, :], wgla[r, h * P:h * P + P], lrT[r, :], start=True, stop=True), "z_done")

        def pe_odd(eng, p):
            evacuated(eng, p)
            for i, (d, h) in enumerate(STREAMS):
                eng.wait_ge(S("ckd"), p.at("ckd", i + 1))
                if i >= 4:
                    eng.wait_ge(S("ckd_sb"), p.at("ckd_sb", i - 3))
                for a in range(2):
                    last = tr(ps[:, i % 4, a * P:a * P + P], ckd[:, i, a * P:a * P + P], ident)
                up(last, "ckd_T")
            for i, (d, h) in enumerate(STREAMS):
                eng.wait_ge(S("ckd_sb"), p.at("ckd_sb", i + 1))
                if i >= 4:
                    eng.wait_ge(S("st_sb"), p.at("st_sb", i - 3))
                for a in range(2):
                    last = mm(ps[:, 4 + i % 4, 0:SEQ], ckdT[:, i, a * P:a * P + P], vtok[:, 2 + a, h * SEQ:h * SEQ + SEQ], start=a == 0, stop=a == 1)
                up(last, "st_done")
            for i, (d, h) in enumerate(STREAMS):
                eng.wait_ge(S("x_in"), p.at("x_in", i + 1))
                eng.wait_ge(S("xkd_sb"), p.at("xkd_sb", i - 3)) if i >= 4 else eng.wait_ge(S("ckd_sb"), p.at("ckd_sb", 8))
                for a in range(2):
                    last = tr(ps[:, i % 4, a * P:a * P + P], hT[:, i, a * P:a * P + P], ident)
                up(last, "xkd_T")
                eng.wait_ge(S("a_sb"), p.at("a_sb", i - 3)) if i >= 4 else eng.wait_ge(S("st_sb"), p.at("st_sb", 8))
                for a in range(2):
                    last = mm(ps[:, 4 + i % 4, a * P:a * P + P], mixT[:, i, SEQ + a * P:SEQ + a * P + P], mixT[:, i, a * P:a * P + P],
                              start=True, stop=True)
                up(last, "a_done")
            eng.wait_ge(S("xkd_sb"), p.at("xkd_sb", 8))
            eng.wait_ge(S("a_sb"), p.at("a_sb", 8))
            for i, (d, h) in enumerate(STREAMS):
                for a in range(2):
                    mm(ps[:, h, a * SEQ:a * SEQ + SEQ], amask[:, i, a * P:a * P + P], vtok[:, a, h * SEQ:h * SEQ + SEQ],
                       start=d + a == 0, stop=False, skip_group_check=True)
            for st in range(4):
                for i, (d, h) in enumerate(STREAMS):
                    c = 3 - st if d else st
                    r, a, n = slice(64 * (c % 2), 64 * (c % 2) + 64), c // 2, 8 * st + i
                    if st:
                        eng.wait_ge(S("u_sb"), p.at("u_sb", n - 7))
                    last = mm(ps[r, h, a * SEQ:a * SEQ + SEQ], mixT[:, i, c * CHUNK:c * CHUNK + CHUNK], state[:, i, :],
                              start=False, stop=True, skip_group_check=True)
                    if st < 3:
                        if n >= 4:
                            eng.wait_ge(S("u_sb"), p.at("u_sb", n - 3))
                        up(mm(ps[:, 4 + n % 4, 0:SEQ], hT[r, i, SEQ + a * P:SEQ + a * P + P], vtok[r, a, h * SEQ:h * SEQ + SEQ],
                              start=True, stop=True), "u_done")
                    elif d:
                        up(last, "o_done")
            for h in range(GLA_HEADS):
                eng.wait_ge(S("o_normed"), p.at("o_normed", h + 1 if h < 2 else 4))
                for half in range(2):
                    for a in range(2):
                        last = tr(ps[:, 4 + h, half * SEQ + a * P:half * SEQ + a * P + P], otok[:, a, h, half * P:half * P + P], ident)
                up(last, "o_T")

        def act_decay_gates(eng, p):
            eng.wait_ge(S("lr_done"), p.at("lr_done", 1))
            up(act(lrT, ps[0:64, 4, :], ACT.Copy), "lr_sb")

        def act_decays(eng, p):
            d = p.kw["decays"]
            eng.wait_ge(S("z_sb"), p.at("z_sb"))
            if d:
                eng.wait_ge(S("decayed"), p.at("decayed"))
            z = gates_of(d)
            alink(act(softplus, z, ACT.Abs))
            alink(act(softplus, softplus, ACT.Exp, scale=-1.0))
            up(act(softplus, softplus, ACT.Ln, bias=1.0), "la_ln")

        def act_odd(eng, p):
            evacuated(eng, p)
            eng.wait_ge(S("decayed"), p.at("decayed"))
            for i in range(8):
                up(act(ckd[:, i, :], big3[:, 16 + i, SEQ:NT], ACT.Exp, bias=bend[:, i:i + 1], scale=-1.0 / GLA_TAU), "c_exp")
            for i in range(8):
                eng.wait_ge(S("ckd_T"), p.at("ckd_T", i + 1))
                up(act(ckdT[:, i, :], ps[:, i % 4, 0:SEQ], ACT.Copy), "ckd_sb")
            for i in range(8):
                b = big3[:, 16 + i, 0:SEQ]
                act(mixT[:, i, 0:SEQ], b, ACT.Exp, scale=1.0 / GLA_TAU)
                act(mixT[:, i, SEQ:NT], b, ACT.Exp, scale=-1.0 / GLA_TAU)
                eng.wait_ge(S("cums"), p.at("cums", i + 1))
                up(act(hT[:, i, 0:SEQ], hT[:, i, 0:SEQ], ACT.Exp), "x_exp")
            up(act(eblast, blast, ACT.Exp), "e_exp")
            for i in range(8):
                eng.wait_ge(S("xkd_T"), p.at("xkd_T", i + 1))
                up(act(hT[:, i, SEQ:NT], ps[:, i % 4, 0:SEQ], ACT.Copy), "xkd_sb")
            up(act(big3[:, 8:16, 0:SEQ], big3[:, 8:16, 0:SEQ], ACT.Silu), "r_silu")
            for h in range(GLA_HEADS):
                eng.wait_ge(S("o_done"), p.at("o_done", h + 1))
                for a in range(2):
                    n = 2 * h + a
                    if n:
                        eng.wait_ge(S("o_sq"), p.at("o_sq", n))
                    up(act(ojunk, ps[:, h, a * SEQ:a * SEQ + SEQ], ACT.Square, accum_out=ssq[:, n:n + 1]), "o_sq")
            eng.wait_ge(S("o_sq"), p.at("o_sq", 8))
            up(act(ssq[:, 0:8], ssq[:, 0:8], ACT.Sqrt, scale=1.0 / (2 * P), bias=epsc[:, :]), "o_roots")
            act_feed(eng, p)
            for c in range(KC):
                eng.wait_ge(S("o_gated"), p.at("o_gated", c + 1))
                act_high(p, c, mixT[:, c, 0:SEQ], SEQ)

        def dve_decay_gates(eng, p):
            for i in range(8):
                eng.wait_ge(S("z_done"), p.at("z_done", i + 1))
                up(V.tensor_scalar(big3[:, 16 + i, :], ps[:, 4 + i % 4, :], cols2[:, GLA_B + i:GLA_B + i + 1], None, ALU.add), "z_sb")

        def dve_decays(eng, p):
            d = p.kw["decays"]
            eng.wait_ge(S("la_ln"), p.at("la_ln", 1))
            z = gates_of(d)
            link(V.scalar_tensor_tensor(z, z, 0.0, softplus, ALU.min, ALU.subtract))
            for h in range(GLA_HEADS):
                i = 4 * d + h
                back = slice(None, None, -1) if d else slice(None)
                bc, bx = big3[:, 16 + i, SEQ:NT], big3[:, 16 + i, 0:SEQ]
                V.tensor_tensor_scan(bc[:, back], ones[:, 0:SEQ], bc[:, back], 0.0, ALU.mult, ALU.add)
                link(V.tensor_tensor_scan(bx[:, back], restart[:, d, :][:, back], bx[:, back], 0.0, ALU.mult, ALU.add))
                end = bc[:, 0:1] if d else bc[:, SEQ - 1:SEQ]
                ends = bx.rearrange("p (c k) -> p c k", k=CHUNK)[:, :, 0 if d else CHUNK - 1]
                V.tensor_scalar(blast[:, 4 * i:4 * i + 4], ends, 1.0 / GLA_TAU, None, ALU.mult)
                ins = V.tensor_scalar(bend[:, i:i + 1], end, 1.0 / GLA_TAU, None, ALU.mult)
            up(ins, "decayed")

        def dve_odd(eng, p):
            evacuated(eng, p)
            eng.wait_ge(S("decayed"), p.at("decayed"))
            for i in range(8):
                bx = big3[:, 16 + i, 0:SEQ]
                up(V.scalar_tensor_tensor(hT[:, i, 0:SEQ].rearrange("p (c k) -> p c k", k=CHUNK), bx.rearrange("p (c k) -> p c k", k=CHUNK),
                                          -1.0 / GLA_TAU, blast[:, 4 * i:4 * i + 4].unsqueeze(2).broadcast_to([P, 4, CHUNK]),
                                          ALU.mult, ALU.add), "cums")
            for i, (d, h) in enumerate(STREAMS):
                eng.wait_ge(S("c_exp"), p.at("c_exp", i + 1))
                up(V.tensor_tensor(ckd[:, i, :], ckd[:, i, :], big3[:, 4 + h, SEQ:NT], ALU.mult), "ckd")
            for i in range(8):
                eng.wait_ge(S("st_done"), p.at("st_done", i + 1))
                up(V.tensor_copy(state[:, i, :], ps[:, 4 + i % 4, 0:SEQ]), "st_sb")
            eng.wait_ge(S("masked"), p.at("masked", 1))
            for i, (d, h) in enumerate(STREAMS):
                eng.wait_ge(S("x_exp"), p.at("x_exp", i + 1))
                V.scalar_tensor_tensor(mixT[:, i, 0:SEQ], big3[:, h, 0:SEQ], P ** -0.5, mixT[:, i, 0:SEQ], ALU.mult, ALU.mult)
                V.tensor_tensor(mixT[:, i, SEQ:NT], big3[:, 4 + h, 0:SEQ], mixT[:, i, SEQ:NT], ALU.mult)
                up(V.tensor_tensor(hT[:, i, 0:SEQ], big3[:, 4 + h, 0:SEQ], hT[:, i, 0:SEQ], ALU.mult), "x_in")
            for i, (d, h) in enumerate(STREAMS):
                eng.wait_ge(S("a_done"), p.at("a_done", i + 1))
                up(V.copy_predicated(amask[:, i, :].rearrange("p (a q) -> p a q", a=2),
                                     gmask[:, d, :].bitcast(U32).unsqueeze(1).broadcast_to([P, 2, P]),
                                     ps[:, 4 + i % 4, 0:SEQ].rearrange("p (a q) -> p a q", a=2)), "a_sb")
            eng.wait_ge(S("e_exp"), p.at("e_exp", 1))
            for st in range(3):
                for i, (d, h) in enumerate(STREAMS):
                    c, n = 3 - st if d else st, 8 * st + i
                    eng.wait_ge(S("u_done"), p.at("u_done", n + 1))
                    up(V.scalar_tensor_tensor(state[:, i, :], state[:, i, :], eblast[:, 4 * i + c:4 * i + c + 1], ps[:, 4 + n % 4, 0:SEQ],
                                              ALU.mult, ALU.add), "u_sb")
            eng.wait_ge(S("o_roots"), p.at("o_roots", 1))
            link(V.reciprocal(ssq[:, 0:8], ssq[:, 0:8]))
            for h in range(GLA_HEADS):
                up(V.tensor_tensor(otok[:, :, h, :], ps[:, h, :].rearrange("p (a e) -> p a e", a=2),
                                   ssq[:, 2 * h:2 * h + 2].unsqueeze(2).broadcast_to([P, 2, SEQ]), ALU.mult), "o_normed")
            dve_feed(eng, p)
            eng.wait_ge(S("r_silu"), p.at("r_silu", 1))
            for c in range(KC):
                eng.wait_ge(S("o_T"), p.at("o_T", c // 2 + 1))
                up(V.scalar_tensor_tensor(mixT[:, c, 0:SEQ], ps[:, 4 + c // 2, c % 2 * SEQ:c % 2 * SEQ + SEQ], cols2[:, GLA_G + c % 2:GLA_G + c % 2 + 1],
                                          big3[:, 8 + c, 0:SEQ], ALU.mult, ALU.mult), "o_gated")
                if c:
                    dve_low(eng, p, c - 1, c - 1, SEQ)
            dve_low(eng, p, KC - 1, KC - 1, SEQ)

        def pool_odd(eng, p):
            evacuated(eng, p)
            up(G.memset(amask, 0.0), "masked")

        def run(eng, stages):
            for p in phases:
                if p.kind in stages:
                    stages[p.kind](eng, p)

        @block.gpsimd
        def _(eng):
            run(eng, {"squares": pool_squares, "gemm": pool_gemm, "mix1": pool_mix1, "even": pool_even, "odd": pool_odd})

        @block.sync
        def _(eng):
            run(eng, {"setup": sp_setup, "fetch": sp_fetch, "mod": sp_mod, "gemm": sp_gemm, "store": sp_store})

        @block.tensor
        def _(eng):
            run(eng, {"setup": pe_setup, "constants": pe_constants, "load": pe_load, "mod": pe_mod, "norm": pe_norm, "gemm": pe_gemm,
                      "mix1": pe_mix1, "rows": pe_rows_of_gates, "decay_gates": pe_decay_gates, "even": pe_even, "odd": pe_odd, "store": pe_store})

        @block.scalar
        def _(eng):
            run(eng, {"setup": act_setup, "load": act_load, "squares": act_squares, "feed": act_feed, "presplit": act_presplit, "gates": act_gates, "rows": act_rows_of_gates, "decay_gates": act_decay_gates, "norm": act_norm, "gemm": act_gemm,
                      "mix1": act_mix1, "even": act_even, "odd": act_odd, "store": act_store})

        @block.vector
        def _(eng):
            run(eng, {"setup": dve_setup, "constants": dve_constants, "load": dve_load, "feed": dve_feed, "presplit": dve_presplit, "rotary": dve_rotary, "rows": dve_rows_of_gates, "decay_gates": dve_decay_gates, "mod": dve_mod, "modvec": dve_modvec, "norm": dve_norm,
                      "gemm": dve_gemm, "mix1": dve_mix1, "even": dve_even, "odd": dve_odd, "store": dve_store})

    for name, n in total.items():
        assert seen.get(name, 0) == n, (name, seen.get(name, 0), n)


INPUTS = ["x", "c", "ctx", "c_ctx", "w_mod", "b_mod", "g_pre", "g_post", "w_in", "w_out", "sink", "w_fourier", "conv_w",
          "conv_b", "c_2", "ctx_2", "c_ctx_2", "ada_w_2", "ada_b_2", "norm_g_2", "ffn_w_in_2", "ffn_w_out_2",
          "even_w_in_2", "even_w_out_2", "diff_lambda_2", "diff_norm_g_2", "mlstm_conv_w_2", "mlstm_conv_b_2",
          "mlstm_gate_b_2", "mlstm_norm_g_2", "odd_w_in_2", "odd_w_out_2", "gla_w_gate_2", "gla_b_gate_2",
          "gla_norm_g_2", "final_g_2"]


def dram_views(ap):
    v = dict(ap)
    for n in ("x", "ctx", "ctx_2"):
        v[n] = ap[n][0]
    for n in ("c", "c_2"):
        v[n] = ap[n][0].rearrange("(r p) -> r p", p=P)
    for n in ("c_ctx", "c_ctx_2", "final_g_2"):
        v[n] = ap[n].rearrange("(r p) -> r p", p=P)
    for n in ("g_pre", "g_post", "conv_b", "mlstm_conv_b_2", "diff_norm_g_2", "gla_norm_g_2"):
        v[n] = ap[n].rearrange("l (r p) -> (l r) p", p=P)
    for n in ("norm_g_2", "conv_w", "mlstm_conv_w_2"):
        v[n] = ap[n].rearrange("l s (r p) -> (l s r) p", p=P)
    v["mlstm_norm_g_2"] = ap["mlstm_norm_g_2"][0]
    v["gla_b_gate_2"] = ap["gla_b_gate_2"][0].rearrange("d (r p) -> (d r) p", p=P)
    v["gla_w_gate_2"] = ap["gla_w_gate_2"][0]
    v["sink"] = ap["sink"].rearrange("l h -> (l h)")
    v["diff_lambda_2"] = ap["diff_lambda_2"][0].rearrange("a b -> (a b)")
    v["mlstm_gate_b_2"] = ap["mlstm_gate_b_2"][0].rearrange("a (b o) -> (a b) o", o=1)
    wf = ap["w_fourier"].rearrange("l (c g) p n -> g p (l c) n", g=2)
    v["w_fourier"] = [wf[0], wf[1]]
    return v


def kernel(**inputs):
    import concourse.bacc as bacc
    from concourse.bass_utils import run_bass_kernel_spmd

    nc = bacc.Bacc("TRN2", target_bir_lowering=False, num_devices=1)
    arrays, aps = {}, {}
    for name in INPUTS:
        a = np.ascontiguousarray(inputs[name])
        arrays[f"in_{name}"] = a
        aps[name] = nc.dram_tensor(f"in_{name}", a.shape, mybir.dt.from_np(a.dtype), kind="ExternalInput").ap()
    arrays["in_const"] = np.ascontiguousarray(np.concatenate(list(CONST.values()), axis=1))
    const = nc.dram_tensor("in_const", (P, CONST_W), F32, kind="ExternalInput").ap()
    out = nc.dram_tensor("out_0", (1, SEQ, D), F32, kind="ExternalOutput").ap()
    build_program(nc, dram_views(aps), const, out[0])
    result = run_bass_kernel_spmd(nc, [arrays], core_ids=[0])
    return result.results[0]["out_0"]
```
